# Optimizing a Trainium2 kernel written in Bass

```python
import math
import jax, jax.numpy as jnp
from jax import lax
import numpy as np

'''Two layers of a hybrid causal decoder trunk.

Layer 0 (even): one combined input projection feeds two parallel head groups,
  (A) multi-scale causal pooling mixer (4 channel groups, trailing windows 2/4/8/16)
  (B) Mamba-2 SSD mixer (16 heads, 2 B/C groups, state 128, causal conv, SiLU gate,
      chunked scan); their outputs are concatenated into one output projection.
Layer 1 (odd): one combined input projection feeds two parallel head groups,
  (C) Conformer convolution module (GLU -> causal depthwise conv w31 -> LayerNorm -> swish)
  (D) short gated convolution mixer y = B * conv3(C * h)
  concatenated into one output projection.
Every layer then cross-attends (4 heads) into 256 memory tokens and applies a
squared-ReLU MLP. Every sub-layer uses sandwich RMSNorm: x += post_norm(f(pre_norm(x))).

Inputs:  x (BATCH, SEQ, D_MODEL), mem (BATCH, 256, D_MODEL), plus weights.
Output:  (BATCH, SEQ, D_MODEL).
'''

D_MODEL = 1024
BATCH = 1
SEQ = 256
DEPTH = 2

N_MEM = 256
XA_HEADS = 4
XA_HEAD_DIM = D_MODEL // XA_HEADS

POOL_WINDOWS = (2, 4, 8, 16)
POOL_GROUP_DIM = D_MODEL // 8
POOL_WIDTH = len(POOL_WINDOWS) * POOL_GROUP_DIM

SSM_HEAD_DIM = 64
SSM_INNER = D_MODEL
SSM_HEADS = SSM_INNER // SSM_HEAD_DIM
SSM_GROUPS = 2
SSM_STATE = 128
SSM_CONV = 4
SSM_CHUNK = 128
SSM_GN = SSM_GROUPS * SSM_STATE
SSM_CONV_DIM = SSM_INNER + 2 * SSM_GN

AB_IN = POOL_WIDTH + SSM_INNER + SSM_CONV_DIM + SSM_HEADS
AB_OUT = POOL_WIDTH + SSM_INNER

CONF_DIM = D_MODEL
CONF_KERNEL = 31
SC_DIM = D_MODEL
SC_KERNEL = 3
CD_IN = 2 * CONF_DIM + 3 * SC_DIM
CD_OUT = CONF_DIM + SC_DIM

MLP_HIDDEN = 4 * D_MODEL
N_EVEN = (DEPTH + 1) // 2
N_ODD = DEPTH // 2
RMS_EPS = 1e-6
LN_EPS = 1e-5

kernel_name = 'hybrid_pool_ssd_conformer_shortconv'

def rmsnorm(x, g):
    xf = x.astype(jnp.float32)
    y = xf * lax.rsqrt(jnp.mean(xf * xf, axis=-1, keepdims=True) + RMS_EPS)
    return (y * g.astype(jnp.float32)).astype(x.dtype)

def causal_dwconv(u, w):
    width, ch = w.shape
    return lax.conv_general_dilated(
        u, w.astype(u.dtype)[:, None, :], window_strides=(1,),
        padding=[(width - 1, 0)], dimension_numbers=('NWC', 'WIO', 'NWC'),
        feature_group_count=ch)

def pool_mixer(u, pool_w, pool_scale):
    S = u.shape[1]
    count = jnp.arange(1, S + 1, dtype=jnp.float32)[None, :, None]
    outs = []
    for g, w in enumerate(POOL_WINDOWS):
        ug = u[..., g * POOL_GROUP_DIM:(g + 1) * POOL_GROUP_DIM]
        cs = jnp.cumsum(ug.astype(jnp.float32), axis=1)
        cs_prev = jnp.pad(cs, ((0, 0), (w, 0), (0, 0)))[:, :S]
        mean = (cs - cs_prev) / jnp.minimum(count, float(w))
        outs.append((mean.astype(u.dtype) - ug) @ pool_w[g])
    return jnp.concatenate(outs, axis=-1) * pool_scale

def ssd_chunked(xh, dt, a, bm, cm):
    Bsz, S, H, P = xh.shape
    G, N = bm.shape[2], bm.shape[3]
    R = H // G
    nc = S // SSM_CHUNK
    L = SSM_CHUNK
    x = xh.reshape(Bsz, nc, L, G, R, P).astype(jnp.float32)
    dtc = dt.reshape(Bsz, nc, L, G, R)
    b = bm.reshape(Bsz, nc, L, G, N).astype(jnp.float32)
    c = cm.reshape(Bsz, nc, L, G, N).astype(jnp.float32)
    dA = dtc * a.reshape(G, R)
    cs = jnp.moveaxis(jnp.cumsum(dA, axis=2), 2, -1)
    xdt = x * dtc[..., None]
    causal = jnp.tril(jnp.ones((L, L), dtype=bool))
    diff = cs[..., :, None] - cs[..., None, :]
    decay = jnp.exp(jnp.where(causal, diff, -jnp.inf))
    cb = jnp.einsum('bclgn,bcsgn->bcgls', c, b)
    y_diag = jnp.einsum('bcgls,bcgrls,bcsgrp->bclgrp', cb, decay, xdt)
    decay_to_end = jnp.exp(cs[..., -1:] - cs)
    states = jnp.einsum('bclgn,bcgrl,bclgrp->bcgrpn', b, decay_to_end, xdt)
    chunk_decay = jnp.exp(cs[..., -1])

    def step(h, inp):
        st, dec = inp
        return dec[..., None, None] * h + st, h

    h0 = jnp.zeros((Bsz, G, R, P, N), jnp.float32)
    _, prev = lax.scan(step, h0, (jnp.moveaxis(states, 1, 0), jnp.moveaxis(chunk_decay, 1, 0)))
    prev = jnp.moveaxis(prev, 0, 1)
    y_off = jnp.einsum('bclgn,bcgrpn,bcgrl->bclgrp', c, prev, jnp.exp(cs))
    return (y_diag + y_off).reshape(Bsz, S, H, P)

def mixer_ab(h, w_in, pool_w, pool_scale, conv_w, conv_b, dt_bias, a_log, d_skip, norm_w, w_out):
    Bsz, S, _ = h.shape
    u = h @ w_in
    o1 = POOL_WIDTH
    o2 = o1 + SSM_INNER
    o3 = o2 + SSM_CONV_DIM
    pool_u, z, xbc, dt_raw = u[..., :o1], u[..., o1:o2], u[..., o2:o3], u[..., o3:]
    pool_out = pool_mixer(pool_u, pool_w, pool_scale)
    xbc = jax.nn.silu(causal_dwconv(xbc, conv_w) + conv_b)
    xs = xbc[..., :SSM_INNER]
    bm = xbc[..., SSM_INNER:SSM_INNER + SSM_GN].reshape(Bsz, S, SSM_GROUPS, SSM_STATE)
    cm = xbc[..., SSM_INNER + SSM_GN:].reshape(Bsz, S, SSM_GROUPS, SSM_STATE)
    dt = jax.nn.softplus((dt_raw + dt_bias).astype(jnp.float32))
    a = -jnp.exp(a_log.astype(jnp.float32))
    xh = xs.reshape(Bsz, S, SSM_HEADS, SSM_HEAD_DIM)
    y = ssd_chunked(xh, dt, a, bm, cm)
    y = y + d_skip.astype(jnp.float32)[:, None] * xh.astype(jnp.float32)
    gsz = SSM_INNER // SSM_GROUPS
    y = y.reshape(Bsz, S, SSM_GROUPS, gsz) * jax.nn.silu(z.astype(jnp.float32)).reshape(Bsz, S, SSM_GROUPS, gsz)
    y = y * lax.rsqrt(jnp.mean(y * y, axis=-1, keepdims=True) + RMS_EPS)
    y = y.reshape(Bsz, S, SSM_INNER) * norm_w.astype(jnp.float32)
    mix = jnp.concatenate([pool_out, y.astype(h.dtype)], axis=-1)
    return mix @ w_out

def mixer_cd(h, w_in, dw_w, dw_b, ln_g, ln_b, sc_w, w_out):
    u = h @ w_in
    v = u[..., :CONF_DIM] * jax.nn.sigmoid(u[..., CONF_DIM:2 * CONF_DIM])
    v = causal_dwconv(v, dw_w) + dw_b
    vf = v.astype(jnp.float32)
    mu = jnp.mean(vf, axis=-1, keepdims=True)
    var = jnp.mean(jnp.square(vf - mu), axis=-1, keepdims=True)
    vn = (vf - mu) * lax.rsqrt(var + LN_EPS) * ln_g.astype(jnp.float32) + ln_b.astype(jnp.float32)
    conf_out = jax.nn.silu(vn).astype(h.dtype)
    off = 2 * CONF_DIM
    bg = u[..., off:off + SC_DIM]
    cg = u[..., off + SC_DIM:off + 2 * SC_DIM]
    hh = u[..., off + 2 * SC_DIM:]
    sc_out = bg * causal_dwconv(cg * hh, sc_w)
    return jnp.concatenate([conf_out, sc_out], axis=-1) @ w_out

def cross_attn(h, mem, wq, wkv, wo):
    Bsz, S, D = h.shape
    M = mem.shape[1]
    q = (h @ wq).reshape(Bsz, S, XA_HEADS, XA_HEAD_DIM)
    kv = mem @ wkv
    k = kv[..., :D].reshape(Bsz, M, XA_HEADS, XA_HEAD_DIM)
    v = kv[..., D:].reshape(Bsz, M, XA_HEADS, XA_HEAD_DIM)
    s = jnp.einsum('bshd,bmhd->bhsm', q, k).astype(jnp.float32) / math.sqrt(XA_HEAD_DIM)
    p = jax.nn.softmax(s, axis=-1).astype(h.dtype)
    o = jnp.einsum('bhsm,bmhd->bshd', p, v).reshape(Bsz, S, D)
    return o @ wo

def sq_relu_mlp(h, w1, w2):
    r = jax.nn.relu(h @ w1)
    return (r * r) @ w2

def setup_inputs(seed: int = 0) -> dict:
    key = jax.random.key(seed)
    ks = jax.random.split(key, 26)
    f32 = jnp.float32

    def nrm(k, shape, scale):
        return scale * jax.random.normal(k, shape, f32)

    dt0 = jnp.exp(jax.random.uniform(ks[14], (N_EVEN, SSM_HEADS), f32, math.log(1e-3), math.log(1e-1)))
    return {
        'x': nrm(ks[0], (BATCH, SEQ, D_MODEL), 1.0),
        'mem': nrm(ks[1], (BATCH, N_MEM, D_MODEL), 1.0),
        'norm_gains': 1.0 + nrm(ks[2], (DEPTH, 6, D_MODEL), 0.05),
        'xa_wq': nrm(ks[3], (DEPTH, D_MODEL, D_MODEL), D_MODEL ** -0.5),
        'xa_wkv': nrm(ks[4], (DEPTH, D_MODEL, 2 * D_MODEL), D_MODEL ** -0.5),
        'xa_wo': nrm(ks[5], (DEPTH, D_MODEL, D_MODEL), D_MODEL ** -0.5),
        'mlp_w1': nrm(ks[6], (DEPTH, D_MODEL, MLP_HIDDEN), D_MODEL ** -0.5),
        'mlp_w2': nrm(ks[7], (DEPTH, MLP_HIDDEN, D_MODEL), MLP_HIDDEN ** -0.5),
        'ab_w_in': nrm(ks[8], (N_EVEN, D_MODEL, AB_IN), D_MODEL ** -0.5),
        'pool_w': nrm(ks[9], (N_EVEN, len(POOL_WINDOWS), POOL_GROUP_DIM, POOL_GROUP_DIM), POOL_GROUP_DIM ** -0.5),
        'pool_scale': 1.0 + nrm(ks[10], (N_EVEN, POOL_WIDTH), 0.1),
        'ssm_conv_w': nrm(ks[11], (N_EVEN, SSM_CONV, SSM_CONV_DIM), SSM_CONV ** -0.5),
        'ssm_conv_b': nrm(ks[12], (N_EVEN, SSM_CONV_DIM), 0.02),
        'ssm_dt_bias': dt0 + jnp.log(-jnp.expm1(-dt0)),
        'ssm_a_log': jnp.log(jax.random.uniform(ks[15], (N_EVEN, SSM_HEADS), f32, 1.0, 16.0)),
        'ssm_d': 1.0 + nrm(ks[16], (N_EVEN, SSM_HEADS), 0.1),
        'ssm_norm': 1.0 + nrm(ks[17], (N_EVEN, SSM_INNER), 0.05),
        'ab_w_out': nrm(ks[18], (N_EVEN, AB_OUT, D_MODEL), AB_OUT ** -0.5),
        'cd_w_in': nrm(ks[19], (N_ODD, D_MODEL, CD_IN), D_MODEL ** -0.5),
        'conf_dw_w': nrm(ks[20], (N_ODD, CONF_KERNEL, CONF_DIM), CONF_KERNEL ** -0.5),
        'conf_dw_b': nrm(ks[21], (N_ODD, CONF_DIM), 0.02),
        'conf_ln_g': 1.0 + nrm(ks[22], (N_ODD, CONF_DIM), 0.05),
        'conf_ln_b': nrm(ks[23], (N_ODD, CONF_DIM), 0.02),
        'sc_conv_w': nrm(ks[24], (N_ODD, SC_KERNEL, SC_DIM), SC_KERNEL ** -0.5),
        'cd_w_out': nrm(ks[25], (N_ODD, CD_OUT, D_MODEL), CD_OUT ** -0.5),
    }

def reference(x, mem, norm_gains, xa_wq, xa_wkv, xa_wo, mlp_w1, mlp_w2,
              ab_w_in, pool_w, pool_scale, ssm_conv_w, ssm_conv_b, ssm_dt_bias,
              ssm_a_log, ssm_d, ssm_norm, ab_w_out,
              cd_w_in, conf_dw_w, conf_dw_b, conf_ln_g, conf_ln_b, sc_conv_w, cd_w_out):
    for layer in range(DEPTH):
        g = norm_gains[layer]
        i = layer // 2
        h = rmsnorm(x, g[0])
        if layer % 2 == 0:
            m = mixer_ab(h, ab_w_in[i], pool_w[i], pool_scale[i], ssm_conv_w[i], ssm_conv_b[i],
                         ssm_dt_bias[i], ssm_a_log[i], ssm_d[i], ssm_norm[i], ab_w_out[i])
        else:
            m = mixer_cd(h, cd_w_in[i], conf_dw_w[i], conf_dw_b[i], conf_ln_g[i], conf_ln_b[i],
                         sc_conv_w[i], cd_w_out[i])
        x = x + rmsnorm(m, g[1])
        h = rmsnorm(x, g[2])
        x = x + rmsnorm(cross_attn(h, mem, xa_wq[layer], xa_wkv[layer], xa_wo[layer]), g[3])
        h = rmsnorm(x, g[4])
        x = x + rmsnorm(sq_relu_mlp(h, mlp_w1[layer], mlp_w2[layer]), g[5])
    return x


_drawn_inputs = setup_inputs


def setup_inputs(seed=0):
    import zlib

    import numpy as np

    out = dict(_drawn_inputs(seed))
    spreads = {}
    factors = {'ssm_conv_b': 3.001, 'conf_dw_b': 5.06, 'conf_ln_g': 3.861, 'conf_ln_b': 25.696}
    for name, (base, spread) in spreads.items():
        noise = np.random.default_rng([zlib.crc32(name.encode()), seed]).standard_normal(out[name].shape)
        drawn = base * np.exp(spread * noise) if base else spread * noise
        out[name] = __import__('jax').numpy.asarray(drawn.astype(out[name].dtype))
    for name, factor in factors.items():
        out[name] = (out[name] * factor).astype(out[name].dtype)
    return out
```

```python
from contextlib import ExitStack

import numpy as np
import concourse.bass as bass
from concourse import mybir

F32 = mybir.dt.float32
F32R = mybir.dt.float32r
ALU = mybir.AluOpType
ACT = mybir.ActivationFunctionType
AX = mybir.AxisListType

P = 128
RAW, SPLIT = 4, 4
POOL_WINDOWS = (2, 4, 8, 16)
RMS_EPS, LN_EPS = 1e-6, 1e-5


class Ledger:

    def __init__(self, known):
        self.count, self.at, self.known = {}, {}, known

    def tick(self, sem, *label):
        self.count[sem] = self.count.get(sem, 0) + 1
        if label:
            assert (sem, *label) not in self.at, label
            self.at[(sem, *label)] = self.count[sem]
        return 1

    def after(self, sem, *label):
        if self.known is None:
            return 1
        return self.known[(sem, *label)]

    def also(self, sem, *label):
        self.at[(sem, *label)] = self.count[sem]

    def now(self, sem):
        return self.count[sem]


def weight_plan():
    s = []
    for j in range(3):
        s.append((("xbc", j), "ab_in", 0, 0, 8, 1536 + 512 * j))
    for j in range(2):
        s.append((("z", j), "ab_in", 0, 0, 8, 512 + 512 * j))
    s.append((("pool", 0), "ab_in", 0, 0, 8, 0))
    for l in range(2):
        if l == 1:
            for name, c in (("gate", 1024), ("a", 0), ("gate", 1536), ("a", 512), ("cg", 3072), ("hh", 4096),
                            ("cg", 3584), ("hh", 4608), ("bg", 2048), ("bg", 2560)):
                s.append(((name, (c // 512) % 2), "cd_in", 0, 0, 8, c))
        for g in range(2):
            s.append((("K", l, g), "wkv", l, 0, 8, 512 * g))
        out, early, late = (("ab_out", (0, 4), (4, 8)), ("cd_out", (8, 8), (0, 8)))[l]
        for part, (k0, nk) in (("early", early), ("late", late)):
            for g in range(2):
                s.append((("out", l, part, g), out, 0, 128 * k0, nk, 512 * g))
        s.append((("V", l, 0), "wkv", l, 0, 8, 1024))
        for g in range(2):
            s.append((("q", l, g), "wq", l, 0, 8, 512 * g))
        s.append((("V", l, 1), "wkv", l, 0, 8, 1536))
        for g in range(2):
            s.append((("wo", l, g), "wo", l, 0, 8, 512 * g))
        for h in range(9):
            for i in ([0, 1] if h == 0 else [h + 1] if h < 7 else []):
                s.append((("w1", l, i), "w1", l, 0, 8, 512 * i))
            if h < 8:
                for g in range(2):
                    s.append((("w2", l, h, g), "w2", l, 512 * h, 4, 512 * g))
    return s


SETS = {0: dict(M0=(0, 1), M1=(2, 3), FI=(4, 5), T=(6, 7)),
        1: dict(M0=(2, 3), M1=(4, 5), FI=(0, 1), T=(6, 7))}


def bank_plan():
    u = []

    def pair(label, banks):
        u.extend([(label + (0,), banks[0]), (label + (1,), banks[1])])

    u.append((("vecs",), 4))
    for i in range(4):
        u.append((("xT", i), i))
    u.append((("R0",), 5))
    pair(("xbc", 0), (6, 7))
    u.append((("dt",), 4))
    for i in range(4):
        u.append((("memT", i), i))
    pair(("xbc", 1), (0, 1))
    u.append((("dtT",), 5))
    pair(("xbc", 2), (2, 3))
    u.append((("cs",), 6))
    pair(("z", 0), (0, 1))
    for i, b in enumerate((6, 7, 4, 5)):
        u.append((("xsT", i), b))
    pair(("z", 1), (2, 3))
    u.append((("cb", 0), 6))
    u.append((("cb", 1), 7))
    pair(("pool", 0), (0, 1))
    for i in range(8):
        if i == 3:
            pair(("K", 0, 0), (2, 3))
        if i == 7:
            pair(("K", 0, 1), (0, 1))
        u.append((("rows", i), 6 + i % 2))
        if i >= 2 and i % 2 == 1:
            u.append((("y", (i - 3) // 2), 4 + (i - 3) // 2 % 2))
    u.append((("y", 3), 5))
    u.append((("pooled", 0), 6))
    u.append((("pooled", 1), 7))
    u.append((("gstat",), 4))
    u.append((("grow",), 5))
    for l in range(2):
        b = SETS[l]
        M0, M1, FI, T = b["M0"], b["M1"], b["FI"], b["T"]
        if l == 1:
            cycle = [(2, 3), (4, 5), (0, 1)]
            names = [("gate", 0), ("a", 0), ("gate", 1), ("a", 1), ("cg", 0), ("hh", 0), ("cg", 1), ("hh", 1),
                     ("bg", 0), ("bg", 1), ("K", 1, 0), ("K", 1, 1)]
            for n, name in enumerate(names):
                pair(name, cycle[n % 3])
                if n == 0:
                    u.append((("xstat", 0), 6))
                    u.append((("R1",), 7))
            u.append((("mustat",), 0))
            u.append((("murow",), 1))
            u.append((("varstat",), 0))
            u.append((("varrow",), 1))
        pair(("out", l, 0), M0)
        pair(("out", l, 1), M1)
        pair(("V", l, 0), FI)
        u.append((("nstat", l, 0), T[0]))
        u.append((("nrow", l, 0), T[1]))
        pair(("q", l, 0), T)
        u.append((("astat", l), FI[0]))
        pair(("q", l, 1), M0)
        u.append((("scores", l, 0), FI[1]))
        u.append((("scores", l, 1), M1[0]))
        pair(("V", l, 1), T)
        u.append((("scores", l, 2), M1[1]))
        u.append((("scores", l, 3), FI[0]))
        u.append((("pT", l, 0), FI[1]))
        u.append((("pT", l, 1), M1[0]))
        u.append((("o", l, 0), M0[0]))
        u.append((("o", l, 1), M0[1]))
        u.append((("pT", l, 2), M1[1]))
        u.append((("pT", l, 3), FI[0]))
        u.append((("o", l, 2), FI[1]))
        u.append((("o", l, 3), M1[0]))
        pair(("wo", l, 0), T)
        pair(("wo", l, 1), M0)
        u.append((("nstat", l, 1), M1[0]))
        u.append((("nrow", l, 1), M1[1]))
        for h in range(8):
            pair(("w1", l, h), FI if h % 2 == 0 else M1)
            if h == 0:
                u.append((("hstat", l), T[0]))
        pair(("w2", l, 0), T)
        pair(("w2", l, 1), M0)
        u.append((("nstat", l, 2), FI[0]))
        u.append((("nrow", l, 2), FI[1]))
    for i, b in enumerate((M1[0], M1[1], FI[0], T[0])):
        u.append((("outT", i), b))
    return u


def trunk(nc, A, out, known):
    T = A["x"].shape[1]
    D = A["x"].shape[2]
    J = D // P
    HEADS = A["ssm_a_log"].shape[1]
    TT = T // P
    H2 = T * 2
    XA_SCALE = 1.0 / 16.0
    L = Ledger(known)
    tick, after, now = L.tick, L.after, L.now

    mats = {"ab_in": A["ab_w_in"], "ab_out": A["ab_w_out"], "cd_in": A["cd_w_in"], "cd_out": A["cd_w_out"],
            "wkv": A["xa_wkv"], "wq": A["xa_wq"], "wo": A["xa_wo"], "w1": A["mlp_w1"], "w2": A["mlp_w2"]}
    units, first, size = [], {}, {}
    for name, m, l, row, nk, col in weight_plan():
        first[name], size[name] = len(units), nk // 2
        for i in range(nk // 2):
            r = row + 256 * i
            units.append(mats[m][l, r:r + 256, col:col + 512].rearrange("(i p) c -> p i c", p=P))
    NU = len(units)
    pool_lo = [False] * NU
    for u in range(first[("xbc", 0)], first[("out", 0, "late", 0)]):
        pool_lo[u] = u % 2 == 1
    for u in range(first[("gate", 1)], first[("out", 1, "late", 0)]):
        pool_lo[u] = u % 8 != 7
    lo_count, nd, npl = [], 0, 0
    for u in range(NU):
        nd, npl = nd + (not pool_lo[u]), npl + pool_lo[u]
        lo_count.append(npl if pool_lo[u] else nd)

    use, by_use, uses = {}, {}, [0] * 8
    for label, b in bank_plan():
        assert label not in use, label
        use[label] = (b, uses[b])
        by_use[b, uses[b]] = label
        uses[b] += 1

    ctx = ExitStack()
    with ctx:
        def sb(name, shape, dt=F32, scope=ctx):
            return scope.enter_context(nc.sbuf_tensor(name, [P, *shape], dt))

        def sem(name):
            return ctx.enter_context(nc.semaphore(name))

        xT = sb("xT", [J, T])
        h_hi, h_lo = sb("h_hi", [J, T], F32R), sb("h_lo", [J, T], F32R)
        mem_hi, mem_lo = sb("mem_hi", [J, T], F32R), sb("mem_lo", [J, T], F32R)
        k_hi, k_lo = sb("k_hi", [J, T], F32R), sb("k_lo", [J, T], F32R)
        raw = sb("raw", [RAW, 2, 512])
        w_hi, w_lo = sb("w_hi", [SPLIT, 2, 512], F32R), sb("w_lo", [SPLIT, 2, 512], F32R)
        ident, ones, tri, cbmask = sb("ident", [P]), sb("ones", [P]), sb("tri", [P]), sb("cbmask", [3 * P])
        Rrow, Nrow = sb("Rrow", [T]), sb("Nrow", [T])
        vecs = sb("vecs", [512])
        sq = sb("sq", [2, H2])
        Ssum, S2 = sb("Ssum", [H2]), sb("S2", [T])
        stat = sb("stat", [16, 8])
        rfac = sb("rfac", [16, 8])
        mhalf = sb("mhalf", [8])
        tmp = sb("tmp", [2, T])
        with ExitStack() as s:
            v_hi, v_lo = sb("v_hi", [TT, D], F32R, s), sb("v_lo", [TT, D], F32R, s)
        with ExitStack() as s:
            my_hi, my_lo = sb("my_hi", [J, T], F32R, s), sb("my_lo", [J, T], F32R, s)
        with ExitStack() as s:
            cv, cv3 = sb("cv", [J, T], scope=s), sb("cv3", [J, T], scope=s)
            hold = s.pop_all()
        ctx.enter_context(hold)
        with ExitStack() as s:
            xtok, memtok = sb("xtok", [TT, D], scope=s), sb("memtok", [TT, D], scope=s)
            stage = sb("stage", [4, P], scope=s)
        with ExitStack() as s:
            xdt = sb("xdt", [TT, D], scope=s)
            mp_hi, mp_lo = sb("mp_hi", [4, T], F32R, s), sb("mp_lo", [4, T], F32R, s)
            E = sb("E", [4, 3 * P], scope=s)
            cbm = sb("cbm", [2, 3 * P], scope=s)
            zs = sb("zs", [J, T], scope=s)
            xc = sb("xc", [12, T], scope=s)
            upad = sb("upad", [2, 2, T + 3], scope=s)
            pu = sb("pu", [4, T + 16], scope=s)
            pw1, pw2 = sb("pw1", [T + 16], scope=s), sb("pw2", [T + 16], scope=s)
            pdiff = sb("pdiff", [4, T], scope=s)
            Sg = sb("Sg", [2, T], scope=s)
            Rg = sb("Rg", [2, T], scope=s)
            icnt = sb("icnt", [4, 16], scope=s)
            poolw = sb("poolw", [4, P], scope=s)
            wdt, wdtg = sb("wdt", [J, HEADS], scope=s), sb("wdtg", [J, HEADS], scope=s)
            dtT = sb("dtT", [T], scope=s)
            dtb, expA, dskip = sb("dtb", [HEADS], scope=s), sb("expA", [HEADS], scope=s), sb("dskip", [J], scope=s)
            sp = sb("sp", [10, 2 * HEADS], scope=s)
            cs = sb("cs", [4, HEADS], scope=s)
        with ExitStack() as s:
            vpad = sb("vpad", [J, T + 30], scope=s)
            ppad = sb("ppad", [J, T + 2], scope=s)
            sg = sb("sg", [4, T], scope=s)
            mh, ml = sb("mh", [2 * J, T], F32R, s), sb("ml", [2 * J, T], F32R, s)
            Rsq = sb("Rsq", [T], scope=s)
            sct = sb("sct", [2, H2], scope=s)
        with ExitStack() as s:
            q_hi, q_lo = sb("q_hi", [J, T], F32R, s), sb("q_lo", [J, T], F32R, s)
            prob = sb("prob", [4, TT, T], scope=s)
            pt_hi, pt_lo = sb("pt_hi", [4, TT, T], F32R, s), sb("pt_lo", [4, TT, T], F32R, s)
        with ExitStack() as s:
            r_hi, r_lo = sb("r_hi", [2, 4, T], F32R, s), sb("r_lo", [2, 4, T], F32R, s)
            relu, rsq = sb("relu", [2, H2], scope=s), sb("rsq", [2, H2], scope=s)
            otok = sb("otok", [TT, D], scope=s)
        ps = ctx.enter_context(nc.psum_tensor("ps", [P, 8, 512], F32))

        x_landed, mem_landed, vec_landed, ssm_landed, out_stored = (
            sem(n) for n in ("x_landed", "mem_landed", "vec_landed", "ssm_landed", "out_stored"))
        raw_landed = [sem(f"raw_landed{i}") for i in range(RAW)]
        hi_ready, lo_ready_dve, lo_ready_pool = (sem(n) for n in ("hi_ready", "lo_ready_dve", "lo_ready_pool"))
        pe_made, act_made, dve_made, pool_made = sem("pe_made"), sem("act_made"), sem("dve_made"), sem("pool_made")

        GAIN, MISC, DW = 0, 128, 256

        def gain(l, s, j):
            return vecs[:, GAIN + (l * 6 + s) * J + j:GAIN + (l * 6 + s) * J + j + 1]

        MISC_ROWS = [("convw", A["ssm_conv_w"].rearrange("a k (j p) -> (a k j) p", p=P)),
                     ("convb", A["ssm_conv_b"].rearrange("a (j p) -> (a j) p", p=P)),
                     ("ssmn", A["ssm_norm"].rearrange("a (j p) -> (a j) p", p=P)),
                     ("pscale", A["pool_scale"].rearrange("a (j p) -> (a j) p", p=P)),
                     ("dwb", A["conf_dw_b"].rearrange("a (j p) -> (a j) p", p=P)),
                     ("lng", A["conf_ln_g"].rearrange("a (j p) -> (a j) p", p=P)),
                     ("lnb", A["conf_ln_b"].rearrange("a (j p) -> (a j) p", p=P)),
                     ("scw", A["sc_conv_w"].rearrange("a k (j p) -> (a k j) p", p=P))]
        misc_at, n = {}, 0
        for name, v in MISC_ROWS:
            misc_at[name] = MISC + n
            n += v.shape[0]
        MISC_N = n

        def vec(name, j):
            return vecs[:, misc_at[name] + j:misc_at[name] + j + 1]

        def tap(k, j):
            return vecs[:, DW + k * J + j:DW + k * J + j + 1]

        dw_rows = A["conf_dw_w"].rearrange("a k (j p) -> (a k j) p", p=P)
        DWN = dw_rows.shape[0]

        def bank(label):
            return ps[:, use[label][0], :]

        def bank2(label):
            return ps[:, use[label][0], :].rearrange("p (c t) -> p c t", c=2)

        def full(label):
            return pe_made, after("pe", label)

        def freed(engine, label):
            L.at[("free", label)] = (engine, now(engine))

        def row2(r):
            return r[:, :].unsqueeze(1).broadcast_to([P, 2, T])

        def f(ap):
            return ap.bitcast(F32)

        def lo_wait(u):
            return (lo_ready_pool if pool_lo[u] else lo_ready_dve), lo_count[u]

        def mixer_out(l, kt):
            if l == 0:
                return (mp_hi[:, kt, :], mp_lo[:, kt, :]) if kt < 4 else (my_hi[:, kt - 4, :], my_lo[:, kt - 4, :])
            return mh[:, kt, :], ml[:, kt, :]

        block = ctx.enter_context(nc.Block())

        @block.sync
        def _(sp_):
            sp_.dma_start(xtok[:, :, :], A["x"][0].rearrange("(t p) d -> p t d", p=P)).then_inc(x_landed, 16)
            for u in range(NU):
                if u >= RAW:
                    sp_.wait_ge(*lo_wait(u - RAW))
                sp_.dma_start(raw[:, u % RAW, :, :], units[u]).then_inc(raw_landed[u % RAW], 16)
            for t in range(TT):
                for hf in range(2):
                    i = 2 * t + hf
                    sp_.wait_ge(act_made if hf == 0 else dve_made, after("act" if hf == 0 else "dve", "otok", i))
                    sp_.dma_start(out[0, t * P:(t + 1) * P, hf * 512:(hf + 1) * 512],
                                  otok[:, t, hf * 512:(hf + 1) * 512]).then_inc(out_stored, 16)
            sp_.wait_ge(out_stored, 16 * 2 * TT)

        @block.tensor
        def _(pe):
            done = [0] * 8
            def acquire(label):
                b, k = use[label]
                assert done[b] == k, label
                if k and known is not None:
                    engine, n = known[("free", by_use[b, k - 1])]
                    pe.wait_ge(act_made if engine == "act" else dve_made, n)

            def finish(label):
                b, k = use[label]
                assert done[b] == k, label
                done[b] += 1
                return pe_made, tick("pe", label)

            def three(dst, wt, x, start, stop):
                nc.tensor.matmul(dst, wt[0], x[0], start=start, stop=False, skip_group_check=True)
                nc.tensor.matmul(dst, wt[0], x[1], start=False, stop=False, skip_group_check=True)
                return nc.tensor.matmul(dst, wt[1], x[0], start=False, stop=stop, skip_group_check=True)

            def unit_w(u, i, n):
                c = slice(n * P, (n + 1) * P)
                return w_hi[:, u % SPLIT, i, c], w_lo[:, u % SPLIT, i, c]

            def project(seg, dest, src, k0=0, first_k=True, last_k=True, ready=None, only=None):
                nu = size[seg]
                us = range(nu) if only is None else only
                tail = 2 if last_k and us[-1] == nu - 1 and nu >= 2 else 0
                for ui in us:
                    if tail and ui >= nu - tail:
                        break
                    u = first[seg] + ui
                    pe.wait_ge(*lo_wait(u))
                    for i in range(2):
                        kt = k0 + 2 * ui + i
                        if ready:
                            ready(kt)
                        for n in range(4):
                            st = first_k and ui == 0 and i == 0 and n % 2 == 0
                            if st:
                                acquire(dest[n // 2])
                            mm = three(bank2(dest[n // 2])[:, n % 2, :], unit_w(u, i, n), src(kt), st, False)
                    mm.then_inc(pe_made, tick("pe", "unit", u))
                if tail:
                    u0 = first[seg] + nu - 2
                    pe.wait_ge(*lo_wait(u0))
                    pe.wait_ge(*lo_wait(u0 + 1))
                    if ready:
                        for kt in range(k0 + 2 * nu - 4, k0 + 2 * nu):
                            ready(kt)
                    for n in range(4):
                        for q in range(4):
                            kt = k0 + 2 * nu - 4 + q
                            st = first_k and nu == 2 and q == 0 and n % 2 == 0
                            if st:
                                acquire(dest[n // 2])
                            mm = three(bank2(dest[n // 2])[:, n % 2, :], unit_w(u0 + q // 2, q % 2, n), src(kt),
                                       st, q == 3)
                            if n == 3 and q == 1:
                                mm.then_inc(pe_made, tick("pe", "unit", u0))
                            if n == 1 and q == 3:
                                mm.then_inc(*finish(dest[0]))
                    mm.then_inc(*finish(dest[1]))
                    L.also("pe", "unit", u0 + 1)

            def h_src(kt):
                return h_hi[:, kt, :], h_lo[:, kt, :]

            def transposes(label, parts):
                acquire(label)
                for c, src, k in parts:
                    mm = nc.tensor.transpose(bank(label)[:, c:c + k], src, ident[0:k, 0:k])
                mm.then_inc(*finish(label))

            def token_sums(label, sources):
                acquire(label)
                for i, s_ in enumerate(sources):
                    mm = nc.tensor.matmul(bank(label)[:, i:i + 1], s_, ones[:, 0:1], start=True, stop=True)
                mm.then_inc(*finish(label))

            def rows(label, cols):
                acquire(label)
                for i, c in enumerate(cols):
                    mm = nc.tensor.matmul(bank(label)[:, i * P:(i + 1) * P], c.broadcast_to([P, P]), ident[:, :],
                                          start=True, stop=True)
                mm.then_inc(*finish(label))

            def halves(s_):
                return [s_[:, t * P:(t + 1) * P] for t in range(TT)]

            pe.wait_ge(pool_made, after("pool", "ident"))
            pe.wait_ge(vec_landed, 16 * (3 + len(MISC_ROWS)))
            transposes(("vecs",), [(0, stage[0:96, 0, :], 96), (P, stage[0:MISC_N, 1, :], MISC_N),
                                   (2 * P, stage[:, 2, :], P), (3 * P, stage[0:DWN - P, 3, :], DWN - P)])
            pe.wait_ge(x_landed, 16)
            for i in range(4):
                transposes(("xT", i), [((c * TT + t) * P, xtok[:, t, (2 * i + c) * P:(2 * i + c + 1) * P], P)
                                       for c in range(2) for t in range(TT)])
            pe.wait_ge(pool_made, after("pool", "r0"))
            rows(("R0",), [rfac[:, 0, t:t + 1] for t in range(TT)])

            def h_ready(tag):
                def ready(kt):
                    pe.wait_ge(dve_made, after("dve", "h", tag, kt))
                return ready

            project(("xbc", 0), [("xbc", 0, 0), ("xbc", 0, 1)], h_src, ready=h_ready("in0"))
            pe.wait_ge(dve_made, after("dve", "wdtg"))
            acquire(("dt",))
            for j in range(J):
                mm = nc.tensor.matmul(ps[0:HEADS, use[("dt",)][0], 0:T], wdtg[:, j, :], xT[:, j, :],
                                      start=(j == 0), stop=(j == J - 1))
            mm.then_inc(*finish(("dt",)))
            pe.wait_ge(mem_landed, 16)
            for i in range(4):
                transposes(("memT", i), [((c * TT + t) * P, memtok[:, t, (2 * i + c) * P:(2 * i + c + 1) * P], P)
                                         for c in range(2) for t in range(TT)])
            project(("xbc", 1), [("xbc", 1, 0), ("xbc", 1, 1)], h_src)
            pe.wait_ge(act_made, after("act", "dtT"))
            acquire(("dtT",))
            for t in range(TT):
                mm = nc.tensor.matmul(bank(("dtT",))[:, t * HEADS:(t + 1) * HEADS], dtT[0:HEADS, t * P:(t + 1) * P],
                                      ident[0:HEADS, 0:HEADS], start=True, stop=True)
            mm.then_inc(*finish(("dtT",)))
            project(("xbc", 2), [("xbc", 2, 0), ("xbc", 2, 1)], h_src)
            pe.wait_ge(dve_made, after("dve", "dA"))
            acquire(("cs",))
            dt_ = sp[:, 8, :].rearrange("p (t h) -> p t h", t=TT)
            dA = sp[:, 9, :].rearrange("p (t h) -> p t h", t=TT)
            for t in range(TT):
                nc.tensor.matmul(bank(("cs",))[:, t * HEADS:(t + 1) * HEADS], tri[:, :], dA[:, t, :],
                                 start=True, stop=True)
            nc.tensor.matmul(bank(("cs",))[:, 2 * HEADS:3 * HEADS], ones[:, :], dA[:, 0, :],
                             start=True, stop=True).then_inc(*finish(("cs",)))
            project(("z", 0), [("z", 0, 0), ("z", 0, 1)], h_src)
            pe.wait_ge(act_made, after("act", "xc", 3))
            for i in range(4):
                t, q = i // 2, i % 2
                transposes(("xsT", i), [(c * P, xc[:, 4 * q + c, t * P:(t + 1) * P], P) for c in range(4)])
            project(("z", 1), [("z", 1, 0), ("z", 1, 1)], h_src)
            pe.wait_ge(act_made, after("act", "xc", 5))
            for g in range(2):
                acquire(("cb", g))
                nc.tensor.matmul(bank(("cb", g))[:, 0:T], xc[:, 8 + g, 0:P], xc[:, 10 + g, :], start=True, stop=True)
                nc.tensor.matmul(bank(("cb", g))[:, T:T + P], xc[:, 8 + g, P:T], xc[:, 10 + g, P:T],
                                 start=True, stop=True).then_inc(*finish(("cb", g)))
            project(("pool", 0), [("pool", 0, 0), ("pool", 0, 1)], h_src)

            def mem_src(kt):
                return mem_hi[:, kt, :], mem_lo[:, kt, :]

            def y_pair(i):
                for h in (2 * i, 2 * i + 1):
                    yb = ("y", h // 4)
                    if h % 4 == 0:
                        acquire(yb)
                    pe.wait_ge(pool_made, after("pool", "E", h))
                    dst = ps[64 * (h % 2):64 * (h % 2) + 64, use[yb][0], :].rearrange("p (c t) -> p c t", c=2)
                    nc.tensor.matmul(dst[:, i % 2, :], xdt[:, 0, h * 64:(h + 1) * 64], E[:, h % 4, 0:T],
                                     start=True, stop=False, skip_group_check=True)
                    mm = nc.tensor.matmul(dst[:, i % 2, P:T], xdt[:, 1, h * 64:(h + 1) * 64], E[:, h % 4, T:T + P],
                                          start=False, stop=True, skip_group_check=True)
                    if h % 4 == 3:
                        mm.then_inc(*finish(yb))
                        L.also("pe", "head", h)
                    else:
                        mm.then_inc(pe_made, tick("pe", "head", h))

            for i in range(8):
                g = i // 4
                pe.wait_ge(dve_made, after("dve", "mem", 3))
                if i % 4 < 2:
                    project(("K", 0, g), [("K", 0, g, 0), ("K", 0, g, 1)], mem_src, only=[i % 4])
                elif i % 4 == 3:
                    project(("K", 0, g), [("K", 0, g, 0), ("K", 0, g, 1)], mem_src, only=[2, 3])
                if i == 0:
                    pe.wait_ge(dve_made, after("dve", "cs"))
                acquire(("rows", i))
                for hh in range(2):
                    for t in range(TT):
                        mm = nc.tensor.matmul(bank(("rows", i))[:, hh * T + t * P:hh * T + (t + 1) * P],
                                              dA[:, t, 2 * i + hh:2 * i + hh + 1].broadcast_to([P, P]), tri[:, :],
                                              start=True, stop=True)
                mm.then_inc(*finish(("rows", i)))
                if i == 2:
                    pe.wait_ge(dve_made, after("dve", "xdt", 3))
                if i >= 2:
                    y_pair(i - 2)
            y_pair(6)
            y_pair(7)
            pe.wait_ge(ssm_landed, 16 * 6)
            for i in range(2):
                acquire(("pooled", i))
                for c in range(2):
                    g = 2 * i + c
                    pe.wait_ge(pool_made, after("pool", "pdiff", g))
                    mm = nc.tensor.matmul(bank2(("pooled", i))[:, c, :], poolw[:, g, :], pdiff[:, g, :],
                                          start=True, stop=True)
                mm.then_inc(*finish(("pooled", i)))

            def mixer_src(l):
                return lambda kt: mixer_out(l, kt)

            def out_banks(l, g):
                return [("out", l, g, 0), ("out", l, g, 1)]

            def mix_ready(l):
                return lambda kt: pe.wait_ge(dve_made, after("dve", "mix", l, kt))

            def boundary(l, n, filler, x_tag):
                if filler:
                    filler()
                pe.wait_ge(dve_made, after("dve", "S2", l, n))
                token_sums(("nstat", l, n), halves(S2))
                pe.wait_ge(pool_made, after("pool", "nr", l, n))
                rows(("nrow", l, n), [rfac[:, 1 + 3 * l + n, t:t + 1] for t in range(TT)])

            def v_group(l, g):
                seg = ("V", l, g)
                for ui in range(4):
                    u = first[seg] + ui
                    pe.wait_ge(*lo_wait(u))
                    for i in range(2):
                        kt = 2 * ui + i
                        for t in range(TT):
                            if kt == 0:
                                acquire(seg + (t,))
                            ms = slice(t * P, (t + 1) * P)
                            wh, wl = w_hi[:, u % SPLIT, i, :], w_lo[:, u % SPLIT, i, :]
                            dst = bank(seg + (t,))
                            nc.tensor.matmul(dst, mem_hi[:, kt, ms], wh, start=(kt == 0), stop=False)
                            nc.tensor.matmul(dst, mem_hi[:, kt, ms], wl, start=False, stop=False)
                            mm = nc.tensor.matmul(dst, mem_lo[:, kt, ms], wh, start=False, stop=(kt == J - 1))
                            if kt == J - 1:
                                mm.then_inc(*finish(seg + (t,)))
                    if ui == 3:
                        L.also("pe", "unit", u)
                    else:
                        mm.then_inc(pe_made, tick("pe", "unit", u))

            def scores(l, h):
                acquire(("scores", l, h))
                pe.wait_ge(dve_made, after("dve", "q", l, h))
                if h == 0:
                    pe.wait_ge(dve_made, after("dve", "K", l, 3))
                for t in range(TT):
                    for c in range(2):
                        j = 2 * h + c
                        mm = three(bank2(("scores", l, h))[:, t, :],
                                   (q_hi[:, j, t * P:(t + 1) * P], q_lo[:, j, t * P:(t + 1) * P]),
                                   (k_hi[:, j, :], k_lo[:, j, :]), t == 0 and c == 0, c == 1)
                mm.then_inc(*finish(("scores", l, h)))

            def prob_T(l, h):
                pe.wait_ge(dve_made, after("dve", "prob", l, h))
                transposes(("pT", l, h), [((m * TT + t) * P, prob[:, h, t, m * P:(m + 1) * P], P)
                                          for m in range(TT) for t in range(TT)])

            def attend(l, h):
                acquire(("o", l, h))
                pe.wait_ge(dve_made, after("dve", "pT", l, h))
                pe.wait_ge(dve_made, after("dve", "V", l, h // 2, 1))
                for c in range(2):
                    for m in range(TT):
                        col = slice(h * T + c * P, h * T + (c + 1) * P)
                        mm = three(bank2(("o", l, h))[:, c, :], (v_hi[:, m, col], v_lo[:, m, col]),
                                   (pt_hi[:, h, m, :], pt_lo[:, h, m, :]), c == 0 and m == 0, m == 1)
                mm.then_inc(*finish(("o", l, h)))

            for l in range(2):
                if l == 1:
                    for n, name in enumerate([("gate", 0), ("a", 0), ("gate", 1), ("a", 1), ("cg", 0), ("hh", 0),
                                              ("cg", 1), ("hh", 1), ("bg", 0), ("bg", 1)]):
                        project(name, [name + (0,), name + (1,)], h_src, ready=h_ready("in1") if n == 0 else None)
                        if n == 0:
                            pe.wait_ge(pool_made, after("pool", "Sx", "in1"))
                            token_sums(("xstat", 0), halves(S2))
                            pe.wait_ge(pool_made, after("pool", "r1"))
                            rows(("R1",), [rfac[:, 7, t:t + 1] for t in range(TT)])
                    for g in range(2):
                        project(("K", 1, g), [("K", 1, g, 0), ("K", 1, g, 1)], mem_src)
                ke, kl = ((0, 4), (8, 0))[l]
                if l == 0:
                    for g in range(2):
                        project(("out", 0, "early", g), out_banks(0, g), mixer_src(0), k0=ke, last_k=False,
                                ready=mix_ready(0) if g == 0 else None)
                    pe.wait_ge(dve_made, after("dve", "Sg", 1))
                    token_sums(("gstat",), halves(Sg[:, 0, :]) + halves(Sg[:, 1, :]))
                    pe.wait_ge(pool_made, after("pool", "gr"))
                    rows(("grow",), [rfac[:, 8, i:i + 1] for i in range(4)])
                else:
                    project(("out", 1, "early", 0), out_banks(1, 0), mixer_src(1), k0=ke, last_k=False,
                            ready=mix_ready(1))
                    pe.wait_ge(dve_made, after("dve", "S2", "mu"))
                    token_sums(("mustat",), halves(S2))
                    pe.wait_ge(dve_made, after("dve", "negmu"))
                    rows(("murow",), [rfac[:, 9, t:t + 1] for t in range(TT)])
                    project(("out", 1, "early", 1), out_banks(1, 1), mixer_src(1), k0=ke, last_k=False)
                    pe.wait_ge(dve_made, after("dve", "S2", "var"))
                    token_sums(("varstat",), halves(S2))
                    pe.wait_ge(pool_made, after("pool", "lnr"))
                    rows(("varrow",), [rfac[:, 10, t:t + 1] for t in range(TT)])
                for g in range(2):
                    project(("out", l, "late", g), out_banks(l, g), mixer_src(l), k0=kl, first_k=False,
                            ready=mix_ready(l) if g == 0 else None)
                boundary(l, 0, lambda: v_group(l, 0), None)
                project(("q", l, 0), [("q", l, 0, 0), ("q", l, 0, 1)], h_src, ready=h_ready(f"q{l}"))
                pe.wait_ge(pool_made, after("pool", "Sx", f"q{l}"))
                token_sums(("astat", l), halves(S2))
                project(("q", l, 1), [("q", l, 1, 0), ("q", l, 1, 1)], h_src)
                scores(l, 0)
                scores(l, 1)
                v_group(l, 1)
                scores(l, 2)
                scores(l, 3)
                prob_T(l, 0)
                prob_T(l, 1)
                attend(l, 0)
                attend(l, 1)
                prob_T(l, 2)
                prob_T(l, 3)
                attend(l, 2)
                attend(l, 3)
                o_ready = lambda kt: pe.wait_ge(dve_made, after("dve", "o", l, kt // 2))
                for g in range(2):
                    project(("wo", l, g), [("wo", l, g, 0), ("wo", l, g, 1)], h_src, ready=o_ready if g == 0 else None)
                boundary(l, 1, None, None)

                def w1(h):
                    project(("w1", l, h), [("w1", l, h, 0), ("w1", l, h, 1)], h_src,
                            ready=h_ready(f"mlp{l}") if h == 0 else None)

                def w2(h):
                    for g in range(2):
                        project(("w2", l, h, g), [("w2", l, g, 0), ("w2", l, g, 1)],
                                lambda kt: (r_hi[:, h % 2, kt, :], r_lo[:, h % 2, kt, :]),
                                first_k=h == 0, last_k=h == 7,
                                ready=(lambda kt: pe.wait_ge(dve_made, after("dve", "r", l, h, kt // 2))) if g == 0
                                else None)

                w1(0)
                pe.wait_ge(pool_made, after("pool", "Sx", f"mlp{l}"))
                token_sums(("hstat", l), halves(S2))
                w1(1)
                for h in range(8):
                    w2(h)
                    if h < 6:
                        w1(h + 2)
                boundary(l, 2, None, None)
            for i in range(4):
                t, hf = i // 2, i % 2
                for q in range(4):
                    pe.wait_ge(dve_made, after("dve", "x", "out", 4 * hf + q))
                transposes(("outT", i), [(q * P, xT[:, 4 * hf + q, t * P:(t + 1) * P], P) for q in range(4)])

        @block.scalar
        def _(act):
            nu = [0]

            def round_to(u):
                while nu[0] <= min(u, NU - 1):
                    v = nu[0]
                    act.wait_ge(raw_landed[v % RAW], 16 * (v // RAW + 1))
                    if v >= SPLIT:
                        act.wait_ge(pe_made, after("pe", "unit", v - SPLIT))
                    nc.scalar.activation(w_hi[:, v % SPLIT, :, :], raw[:, v % RAW, :, :], ACT.Copy)\
                        .then_inc(hi_ready, 1)
                    nu[0] += 1

            def own():
                act.wait_ge(act_made, now("act"))

            act.dma_start(stage[0:96, 0, :], A["norm_gains"].rearrange("l s (j p) -> (l s j) p", p=P))\
                .then_inc(vec_landed, 16)
            for name, v in MISC_ROWS:
                r0 = misc_at[name] - MISC
                act.dma_start(stage[r0:r0 + v.shape[0], 1, :], v).then_inc(vec_landed, 16)
            act.dma_start(stage[:, 2, :], dw_rows[0:P, :]).then_inc(vec_landed, 16)
            act.dma_start(stage[0:DWN - P, 3, :], dw_rows[P:DWN, :]).then_inc(vec_landed, 16)
            act.dma_start(wdt[:, :, :], A["ab_w_in"][0, :, 3072:3088].rearrange("(j p) h -> p j h", p=P))\
                .then_inc(ssm_landed, 16)
            act.dma_start(dtb[:, :], A["ssm_dt_bias"].broadcast_to([P, HEADS])).then_inc(ssm_landed, 16)
            act.dma_start(expA[:, :], A["ssm_a_log"].broadcast_to([P, HEADS])).then_inc(ssm_landed, 16)
            for hf in range(2):
                act.dma_start(dskip[64 * hf:64 * hf + 64, :],
                              A["ssm_d"].rearrange("a (j two) -> a two j", two=2)[:, hf, :].broadcast_to([64, J]),
                              allow_slow_non_contiguous=True)\
                    .then_inc(ssm_landed, 16)
            act.dma_start(poolw[:, :, :], A["pool_w"][0].rearrange("g i o -> i g o")).then_inc(ssm_landed, 16)
            act.dma_start(memtok[:, :, :], A["mem"][0].rearrange("(t p) d -> p t d", p=P)).then_inc(mem_landed, 16)

            act.wait_ge(x_landed, 16)
            for t in range(TT):
                if t:
                    own()
                nc.scalar.activation(sq[:, :, :].rearrange("p a b -> p (a b)"), xtok[:, t, :], ACT.Square,
                                     accum_out=stat[:, 0, t:t + 1]).then_inc(act_made, tick("act", "ss0", t))
            act.wait_ge(*full(("vecs",)))
            for c, k in ((GAIN, 96), (MISC, MISC_N), (DW, DWN)):
                nc.scalar.activation(vecs[:, c:c + k], bank(("vecs",))[:, c:c + k], ACT.Copy)\
                    .then_inc(act_made, tick("act", *(("vecs",) if c == DW else ())))
            freed("act", ("vecs",))

            def h_part(tag, l, s, j):
                act.wait_ge(dve_made, after("dve", "x", tag, j))
                nc.scalar.activation(h_hi[:, j, :], xT[:, j, :], ACT.Identity, scale=gain(l, s, j))\
                    .then_inc(act_made, tick("act", "h", tag, j))

            for j in range(J):
                h_part("in0", 0, 0, j)
                round_to(j // 2)
            act.wait_ge(*full(("R0",)))
            nc.scalar.activation(Rrow[:, :], bank(("R0",))[:, 0:T], ACT.Copy).then_inc(act_made, tick("act", "Rrow", 0))
            freed("act", ("R0",))
            act.wait_ge(ssm_landed, 16 * 6)
            nc.scalar.activation(expA[:, :], expA[:, :], ACT.Exp).then_inc(act_made, tick("act", "expA"))

            def silu_pair(i):
                act.wait_ge(dve_made, after("dve", "conv", i))
                nc.scalar.activation(xc[:, 2 * i:2 * i + 2, :], xc[:, 2 * i:2 * i + 2, :], ACT.Silu)\
                    .then_inc(act_made, tick("act", "xc", i))

            F_ = first
            round_to(F_[("xbc", 0)] + 3)
            act.wait_ge(*full(("dt",)))
            nc.scalar.activation(dtT[0:HEADS, :], ps[0:HEADS, use[("dt",)][0], 0:T], ACT.Copy)\
                .then_inc(act_made, tick("act", "dtT"))
            freed("act", ("dt",))
            for i in range(4):
                act.wait_ge(*full(("memT", i)))
                nc.scalar.activation(mem_hi[:, 2 * i:2 * i + 2, :], bank2(("memT", i)), ACT.Copy)\
                    .then_inc(act_made, tick("act", "mem", i))
                round_to(F_[("xbc", 1)] + i)
            for i in range(2):
                silu_pair(i)
                round_to(F_[("xbc", 2)] + 2 * i + 1)
            act.wait_ge(dve_made, after("dve", "spabs"))
            nc.scalar.activation(sp[:, 2, :], sp[:, 1, :], ACT.Exp, scale=-1.0).then_inc(act_made, tick("act", "spexp"))
            act.wait_ge(dve_made, after("dve", "sp1"))
            nc.scalar.activation(sp[:, 4, :], sp[:, 3, :], ACT.Ln).then_inc(act_made, tick("act", "spln"))
            for i in range(2, 4):
                silu_pair(i)
                round_to(F_[("z", 0)] + 2 * (i - 2) + 1)
            for i in range(4, 6):
                silu_pair(i)
                round_to(F_[("z", 1)] + 2 * (i - 4) + 1)
            for i in range(4):
                act.wait_ge(dve_made, after("dve", "z", i))
                nc.scalar.activation(zs[:, 2 * i:2 * i + 2, :], zs[:, 2 * i:2 * i + 2, :], ACT.Silu)\
                    .then_inc(act_made, tick("act", "z", i))
                if i < 2:
                    round_to(F_[("pool", 0)] + 2 * i + 1)
                else:
                    round_to(F_[("K", 0, 0)] + 2 * (i - 2) + 1)

            def hi_of(dst, label, *name, wait=None):
                act.wait_ge(*full(label))
                if wait:
                    act.wait_ge(*wait)
                nc.scalar.activation(dst, bank2(label) if len(dst.shape) == 3 else bank(label), ACT.Copy)\
                    .then_inc(act_made, tick("act", *name))

            def square(i, src, *name):
                if i >= 2:
                    act.wait_ge(*sq_read[0](i - 2))
                nc.scalar.activation(sq[:, i % 2, :].rearrange("p (c t) -> p c t", c=2), src, ACT.Square)\
                    .then_inc(act_made, tick("act", *name))

            sq_read = [None]

            def y_squares(i):
                act.wait_ge(dve_made, after("dve", "yg", i))
                square(i, zs[:, 2 * i:2 * i + 2, :], "ysq", i)

            sq_read[0] = lambda i: (dve_made, after("dve", "Sg", 0))
            for i in range(8):
                for h in (2 * i, 2 * i + 1):
                    act.wait_ge(dve_made, after("dve", "E", h))
                    nc.scalar.activation(E[:, h % 4, :], E[:, h % 4, :], ACT.Exp)\
                        .then_inc(act_made, tick("act", "E", h))
                if i == 4:
                    for q in range(2):
                        hi_of(k_hi[:, 2 * q:2 * q + 2, :], ("K", 0, 0, q), "K", 0, q)
                round_to(F_[("K", 0, 1)] + i if i < 4 else F_[("out", 0, "early", 0)] + i - 4)
                if i == 5:
                    y_squares(0)
                if i == 7:
                    y_squares(1)
            for q in range(2):
                hi_of(k_hi[:, 4 + 2 * q:6 + 2 * q, :], ("K", 0, 1, q), "K", 0, 2 + q)
            for i in range(2):
                for c in range(2):
                    g = 2 * i + c
                    if c == 0:
                        act.wait_ge(*full(("pooled", i)))
                    nc.scalar.activation(mp_hi[:, g, :], bank2(("pooled", i))[:, c, :], ACT.Identity,
                                         scale=vec("pscale", g)).then_inc(act_made, tick("act", "mp", g))
            y_squares(2)
            y_squares(3)
            act.wait_ge(*full(("grow",)))
            nc.scalar.activation(Rg[:, :, :], bank2(("grow",)), ACT.Copy).then_inc(act_made, tick("act", "Rg"))
            freed("act", ("grow",))
            for c in range(J):
                act.wait_ge(dve_made, after("dve", "yn", c))
                nc.scalar.activation(my_hi[:, c, :], zs[:, c, :], ACT.Copy).then_inc(act_made, tick("act", "mix", 0, 4 + c))
                if c % 2 == 1:
                    round_to(F_[("out", 0, "late", 0)] + c // 2)


            def attention(l):
                q0 = F_[("q", l, 0)]
                round_to(F_[("q", l, 1)])
                for h in range(2):
                    hi_of(q_hi[:, 2 * h:2 * h + 2, :], ("q", l, 0, h), "q", l, h)
                    round_to(F_[("q", l, 1)] + 1 + h)
                round_to(F_[("V", l, 1)] + 0)
                for h in range(2, 4):
                    hi_of(q_hi[:, 2 * h:2 * h + 2, :], ("q", l, 1, h - 2), "q", l, h)

                def exp(h):
                    for t in range(TT):
                        act.wait_ge(dve_made, after("dve", "nmax", l, h))
                        nc.scalar.activation(prob[:, h, t, :], bank2(("scores", l, h))[:, t, :], ACT.Exp,
                                             bias=stat[:, 8 + h, 2 + t:3 + t], scale=rfac[:, 11 + l, 2 + t:3 + t],
                                             accum_out=stat[:, 8 + h, 4 + t:5 + t])\
                            .then_inc(act_made, tick("act", "exp", l, h, t))
                    freed("act", ("scores", l, h))

                exp(0)
                round_to(F_[("V", l, 1)] + 2)
                exp(1)
                round_to(F_[("V", l, 1)] + 3)
                exp(2)
                round_to(F_[("wo", l, 0)])
                exp(3)
                for t in range(TT):
                    hi_of(v_hi[:, t, 512:1024], ("V", l, 1, t), "V", l, 1, t)
                round_to(F_[("wo", l, 0)] + 2)
                hi_of(pt_hi[:, 0, :, :], ("pT", l, 0), "pT", l, 0)
                hi_of(pt_hi[:, 1, :, :], ("pT", l, 1), "pT", l, 1)
                hi_of(h_hi[:, 0:2, :], ("o", l, 0), "o", l, 0)
                hi_of(h_hi[:, 2:4, :], ("o", l, 1), "o", l, 1)
                hi_of(pt_hi[:, 2, :, :], ("pT", l, 2), "pT", l, 2)
                hi_of(pt_hi[:, 3, :, :], ("pT", l, 3), "pT", l, 3)
                hi_of(h_hi[:, 4:6, :], ("o", l, 2), "o", l, 2)
                hi_of(h_hi[:, 6:8, :], ("o", l, 3), "o", l, 3)
                round_to(F_[("w1", l, 0)] + 0)

            def mlp(l):
                for h in range(8):
                    base = F_[("w1", l, h)]
                    round_to(base + 5)
                    for q in range(2):
                        act.wait_ge(*full(("w1", l, h, q)))
                        i = 2 * h + q
                        if i >= 2:
                            act.wait_ge(dve_made, after("dve", "rsq", l, i - 2))
                        nc.scalar.activation(relu[:, q, :], bank(("w1", l, h, q)), ACT.Relu)\
                            .then_inc(act_made, tick("act", "relu", l, i))
                        act.wait_ge(dve_made, after("dve", "rsq", l, i))
                        nc.scalar.activation(r_hi[:, h % 2, 2 * q:2 * q + 2, :],
                                             rsq[:, q, :].rearrange("p (c t) -> p c t", c=2), ACT.Copy)\
                            .then_inc(act_made, tick("act", "r", l, h, q))
                        round_to(base + 6 + q)

            round_to(F_[("V", 0, 0)] - 1)
            for l in range(2):
                m_out = [("out", l, g, q) for g in range(2) for q in range(2)]
                if l == 1:
                    act.wait_ge(*full(("R1",)))
                    nc.scalar.activation(Rrow[:, :], bank(("R1",))[:, 0:T], ACT.Copy)\
                        .then_inc(act_made, tick("act", "Rrow", 1))
                    freed("act", ("R1",))
                    for g in range(2):
                        base = F_[("gate", g)]
                        for q in range(2):
                            act.wait_ge(dve_made, after("dve", "gate", g, q))
                            nc.scalar.activation(sg[:, 2 * q:2 * q + 2, :], sg[:, 2 * q:2 * q + 2, :], ACT.Sigmoid)\
                                .then_inc(act_made, tick("act", "sig", g, q))
                            round_to(base + 4 + 2 * q + 1)
                        round_to(F_[("a", g)] + 7)
                    for g in range(2):
                        for q in range(2):
                            i = 2 * g + q
                            round_to(F_[("bg", g)] + 4 + q)
                            act.wait_ge(dve_made, after("dve", "sc", i))
                            nc.scalar.activation(mh[:, J + 2 * i:J + 2 * i + 2, :],
                                                 sct[:, i % 2, :].rearrange("p (c t) -> p c t", c=2), ACT.Copy)\
                                .then_inc(act_made, tick("act", "mix", 1, J + 2 * i))
                    for g in range(2):
                        round_to(F_[("K", 1, g)] + 6)
                        for q in range(2):
                            hi_of(k_hi[:, 4 * g + 2 * q:4 * g + 2 * q + 2, :], ("K", 1, g, q), "K", 1, 2 * g + q)
                    round_to(F_[("out", 1, "early", 1)] + 1)
                    act.wait_ge(*full(("murow",)))
                    nc.scalar.activation(Nrow[:, :], bank(("murow",))[:, 0:T], ACT.Copy)\
                        .then_inc(act_made, tick("act", "murow"))
                    freed("act", ("murow",))
                    for i in range(4):
                        act.wait_ge(dve_made, after("dve", "vc", i))
                        if i >= 2:
                            act.wait_ge(dve_made, after("dve", "Sv", 0 if i == 2 else 1))
                        nc.scalar.activation(sq[:, i % 2, :].rearrange("p (c t) -> p c t", c=2),
                                             cv[:, 2 * i:2 * i + 2, :], ACT.Square)\
                            .then_inc(act_made, tick("act", "vsq", i))
                        if i % 2 == 1:
                            round_to(F_[("out", 1, "early", 1)] + 2 + i // 2)
                    round_to(F_[("out", 1, "late", 0)] + 1)
                    act.wait_ge(*full(("varrow",)))
                    nc.scalar.activation(Rrow[:, :], bank(("varrow",))[:, 0:T], ACT.Copy)\
                        .then_inc(act_made, tick("act", "varrow"))
                    freed("act", ("varrow",))
                    for c in range(J):
                        act.wait_ge(dve_made, after("dve", "vn", c))
                        nc.scalar.activation(cv[:, c, :], cv[:, c, :], ACT.Silu, bias=vec("lnb", c))\
                            .then_inc(act_made, tick("act", "vs", c))
                        own()
                        nc.scalar.activation(mh[:, c, :], cv[:, c, :], ACT.Copy).then_inc(act_made, tick("act", "mix", 1, c))
                        if c % 2 == 1:
                            round_to(F_[("out", 1, "late", 0)] + 1 + c // 2)
                round_to(F_[("V", l, 0)] + 2)
                m = m_out
                for i in range(4):
                    act.wait_ge(*full(m[i]))
                    if i >= 2:
                        act.wait_ge(dve_made, after("dve", "Ssum", l, 0, 1 if i == 2 else 2))
                    nc.scalar.activation(sq[:, i % 2, :].rearrange("p (c t) -> p c t", c=2), bank2(m[i]), ACT.Square)\
                        .then_inc(act_made, tick("act", "nsq", l, 0, i))
                round_to(F_[("q", l, 0)])
                for t in range(TT):
                    hi_of(v_hi[:, t, 0:512], ("V", l, 0, t), "V", l, 0, t)
                round_to(F_[("q", l, 0)] + 1)
                act.wait_ge(*full(("nrow", l, 0)))
                nc.scalar.activation(Nrow[:, :], bank(("nrow", l, 0))[:, 0:T], ACT.Copy)\
                    .then_inc(act_made, tick("act", "Nrow", l, 0))
                freed("act", ("nrow", l, 0))

                def new_h(tag, gl, gs, base):
                    for j in range(J):
                        h_part(tag, gl, gs, j)
                        if j % 2 == 1:
                            i = j // 2
                            if i >= 2:
                                act.wait_ge(pool_made, after("pool", "Sx", tag, 0 if i == 2 else 1))
                            nc.scalar.activation(sq[:, i % 2, :].rearrange("p (c t) -> p c t", c=2),
                                                 xT[:, j - 1:j + 1, :], ACT.Square)\
                                .then_inc(act_made, tick("act", "xsq", tag, i))
                            round_to(base + i)

                new_h(f"q{l}", l, 2, F_[("q", l, 0)] + 0)
                attention(l)

                def plain_boundary(n, m, tag, gl, gs, base):
                    round_to(base - 1)
                    for i in range(4):
                        act.wait_ge(*full(m[i]))
                        if i >= 2:
                            act.wait_ge(dve_made, after("dve", "Ssum", l, n, 1 if i == 2 else 2))
                        nc.scalar.activation(sq[:, i % 2, :].rearrange("p (c t) -> p c t", c=2), bank2(m[i]),
                                             ACT.Square).then_inc(act_made, tick("act", "nsq", l, n, i))
                        if i < 3:
                            round_to(base + i)
                    act.wait_ge(*full(("nrow", l, n)))
                    nc.scalar.activation(Nrow[:, :], bank(("nrow", l, n))[:, 0:T], ACT.Copy)\
                        .then_inc(act_made, tick("act", "Nrow", l, n))
                    freed("act", ("nrow", l, n))
                    if tag:
                        new_h(tag, gl, gs, base)

                round_to(F_[("wo", l, 1)] + 3)
                plain_boundary(1, [("wo", l, g, q) for g in range(2) for q in range(2)], f"mlp{l}", l, 4,
                               F_[("w1", l, 0)])
                mlp(l)
                round_to(F_[("w2", l, 7, 1)] + 1)
                plain_boundary(2, [("w2", l, g, q) for g in range(2) for q in range(2)],
                               "in1" if l == 0 else None, 1, 0, F_[("gate", 0)] if l == 0 else NU)
                if l == 0:
                    round_to(F_[("gate", 0)] + 3)
            for i in (0, 2):
                act.wait_ge(*full(("outT", i)))
                nc.scalar.activation(otok[:, i // 2, 0:512], bank(("outT", i)), ACT.Copy)\
                    .then_inc(act_made, tick("act", "otok", i))

        @block.vector
        def _(dve):
            V = nc.vector
            nu = [0]

            def low_to(u):
                while nu[0] <= min(u, NU - 1):
                    v = nu[0]
                    if not pool_lo[v]:
                        dve.wait_ge(hi_ready, v + 1)
                        V.tensor_tensor(w_lo[:, v % SPLIT, :, :], raw[:, v % RAW, :, :], f(w_hi[:, v % SPLIT, :, :]),
                                        ALU.subtract).then_inc(lo_ready_dve, 1)
                    nu[0] += 1

            def own():
                dve.wait_ge(dve_made, now("dve"))

            F_ = first

            def low_h(tag, l, s, j):
                dve.wait_ge(act_made, after("act", "h", tag, j))
                V.scalar_tensor_tensor(out=h_lo[:, j, :], in0=xT[:, j, :], scalar=gain(l, s, j), in1=f(h_hi[:, j, :]),
                                       op0=ALU.mult, op1=ALU.subtract).then_inc(dve_made, tick("dve", "h", tag, j))

            V.memset(mhalf[:, :], -0.5).then_inc(dve_made, tick("dve", "mhalf"))
            V.memset(upad[:, :, :, 0:3], 0.0).then_inc(dve_made, tick("dve"))
            V.memset(pu[:, :, 0:16], 0.0).then_inc(dve_made, tick("dve", "pads"))
            for t in range(TT):
                dve.wait_ge(act_made, after("act", "ss0", t))
            V.tensor_scalar(stat[:, 1, 0:2], stat[:, 0, 0:2], 1.0 / D, RMS_EPS, ALU.mult, ALU.add)\
                .then_inc(dve_made, tick("dve", "v0"))
            dve.wait_ge(act_made, after("act", "vecs"))
            for i in range(4):
                dve.wait_ge(*full(("xT", i)))
                V.tensor_copy(xT[:, 2 * i:2 * i + 2, :], bank2(("xT", i))).then_inc(dve_made, tick("dve", "xTc", i))
                freed("dve", ("xT", i))
                for c in range(2):
                    L.also("dve", "x", "in0", 2 * i + c)
            for j in range(J):
                low_h("in0", 0, 0, j)
                if j % 2 == 1:
                    low_to(j // 2)
            dve.wait_ge(ssm_landed, 16 * 6)
            for j in range(J):
                V.tensor_scalar(wdtg[:, j, :], wdt[:, j, :], gain(0, 0, j), None, ALU.mult)\
                    .then_inc(dve_made, tick("dve", *(("wdtg",) if j == J - 1 else ())))

            def scaled(dst, label, row, *name):
                dve.wait_ge(*full(label))
                V.tensor_tensor(dst, bank2(label), row2(row), ALU.mult)\
                    .then_inc(dve_made, tick("dve", *name))
                freed("dve", label)

            def low_of(dst, hi, label, *name):
                dve.wait_ge(act_made, after("act", *name))
                src = bank2(label) if len(dst.shape) == 3 else bank(label)
                V.tensor_tensor(dst, src, f(hi), ALU.subtract).then_inc(dve_made, tick("dve", *name))
                freed("dve", label)

            dve.wait_ge(act_made, after("act", "Rrow", 0))

            def conv4(i):
                for k in range(4):
                    own()
                    for c in range(2):
                        j = 2 * i + c
                        src = upad[:, i % 2, c, k:k + T]
                        if k == 0:
                            V.tensor_scalar(xc[:, j, :], src, vec("convw", k * 12 + j), vec("convb", j),
                                            ALU.mult, ALU.add).then_inc(dve_made, tick("dve"))
                        else:
                            V.scalar_tensor_tensor(out=xc[:, j, :], in0=src, scalar=vec("convw", k * 12 + j),
                                                   in1=xc[:, j, :], op0=ALU.mult, op1=ALU.add)\
                                .then_inc(dve_made, tick("dve", *(("conv", i) if k == 3 and c == 1 else ())))

            low_to(F_[("xbc", 0)] + 3)
            for i in range(2):
                scaled(upad[:, i % 2, :, 3:3 + T], ("xbc", 0, i), Rrow, "u", i)
                low_to(F_[("xbc", 1)] + i)
                conv4(i)
            for i in range(4):
                low_of(mem_lo[:, 2 * i:2 * i + 2, :], mem_hi[:, 2 * i:2 * i + 2, :], ("memT", i), "mem", i)
                if i % 2:
                    low_to(F_[("xbc", 1)] + 2 + i // 2)
            for i in range(2, 4):
                scaled(upad[:, i % 2, :, 3:3 + T], ("xbc", 1, i - 2), Rrow, "u", i)
                low_to(F_[("xbc", 2)] + 2 * (i - 2))
                conv4(i)
                low_to(F_[("xbc", 2)] + 2 * (i - 2) + 1)
            dve.wait_ge(*full(("dtT",)))
            for t in range(TT):
                V.scalar_tensor_tensor(out=sp[:, 0, t * HEADS:(t + 1) * HEADS],
                                       in0=bank(("dtT",))[:, t * HEADS:(t + 1) * HEADS], scalar=rfac[:, 0, t:t + 1],
                                       in1=dtb[:, :], op0=ALU.mult, op1=ALU.add).then_inc(dve_made, tick("dve"))
            freed("dve", ("dtT",))
            own()
            V.scalar_tensor_tensor(out=sp[:, 1, :], in0=sp[:, 0, :], scalar=-1.0, in1=sp[:, 0, :],
                                   op0=ALU.mult, op1=ALU.max).then_inc(dve_made, tick("dve", "spabs"))
            dve.wait_ge(act_made, after("act", "spexp"))
            V.tensor_scalar(sp[:, 3, :], sp[:, 2, :], 1.0, None, ALU.add).then_inc(dve_made, tick("dve", "sp1"))
            own()
            V.tensor_scalar(sp[:, 5, :], sp[:, 3, :], -1.0, None, ALU.add).then_inc(dve_made, tick("dve"))
            own()
            V.tensor_scalar(sp[:, 6, :], sp[:, 5, :], 0.0, None, ALU.is_equal).then_inc(dve_made, tick("dve"))
            own()
            V.tensor_tensor(sp[:, 5, :], sp[:, 5, :], sp[:, 6, :], ALU.add).then_inc(dve_made, tick("dve"))
            own()
            V.reciprocal(sp[:, 7, :], sp[:, 5, :]).then_inc(dve_made, tick("dve"))
            dve.wait_ge(act_made, after("act", "spln"))
            V.tensor_tensor(sp[:, 4, :], sp[:, 4, :], sp[:, 6, :], ALU.add).then_inc(dve_made, tick("dve"))
            own()
            V.tensor_tensor(sp[:, 4, :], sp[:, 4, :], sp[:, 7, :], ALU.mult).then_inc(dve_made, tick("dve"))
            own()
            V.tensor_tensor(sp[:, 4, :], sp[:, 4, :], sp[:, 2, :], ALU.mult).then_inc(dve_made, tick("dve"))
            own()
            V.scalar_tensor_tensor(out=sp[:, 8, :], in0=sp[:, 0, :], scalar=0.0, in1=sp[:, 4, :],
                                   op0=ALU.max, op1=ALU.add).then_inc(dve_made, tick("dve", "dt"))
            own()
            dve.wait_ge(act_made, after("act", "expA"))
            dt_ = sp[:, 8, :].rearrange("p (t h) -> p t h", t=TT)
            V.scalar_tensor_tensor(out=sp[:, 9, :].rearrange("p (t h) -> p t h", t=TT), in0=dt_, scalar=-1.0,
                                   in1=expA[:, :].unsqueeze(1).broadcast_to([P, TT, HEADS]),
                                   op0=ALU.mult, op1=ALU.mult).then_inc(dve_made, tick("dve", "dA"))
            low_to(F_[("z", 0)])
            for i in range(4, 6):
                scaled(upad[:, i % 2, :, 3:3 + T], ("xbc", 2, i - 4), Rrow, "u", i)
                low_to(F_[("z", 0)] + 2 * (i - 4))
                conv4(i)
                low_to(F_[("z", 0)] + 2 * (i - 4) + 1)
            dve.wait_ge(*full(("cs",)))
            V.tensor_copy(cs[:, 0:3, :], bank(("cs",))[:, 0:3 * HEADS].rearrange("p (a h) -> p a h", a=3))\
                .then_inc(dve_made, tick("dve"))
            freed("dve", ("cs",))
            own()
            V.tensor_tensor(cs[:, 3, :], cs[:, 0, :], cs[:, 2, :], ALU.subtract).then_inc(dve_made, tick("dve", "cs"))
            low_to(F_[("z", 1)])
            for i in range(2):
                scaled(zs[:, 2 * i:2 * i + 2, :], ("z", 0, i), Rrow, "z", i)
            for i in range(4):
                t, q = i // 2, i % 2
                dve.wait_ge(*full(("xsT", i)))
                V.tensor_tensor(xdt[:, t, q * 512:(q + 1) * 512].rearrange("p (h c) -> p h c", c=64),
                                bank(("xsT", i)).rearrange("p (h c) -> p h c", c=64),
                                dt_[:, t, 8 * q:8 * q + 8].unsqueeze(2).broadcast_to([P, 8, 64]), ALU.mult)\
                    .then_inc(dve_made, tick("dve", "xdt", i))
                freed("dve", ("xsT", i))
                low_to(F_[("z", 1)] + i)
            low_to(F_[("pool", 0)])
            for i in range(2, 4):
                scaled(zs[:, 2 * i:2 * i + 2, :], ("z", 1, i - 2), Rrow, "z", i)
            low_to(F_[("pool", 0)] + 1)
            dve.wait_ge(pool_made, after("pool", "cbmask"))
            for g in range(2):
                dve.wait_ge(*full(("cb", g)))
                V.tensor_tensor(cbm[:, g, :], bank(("cb", g))[:, 0:3 * P], cbmask[:, :], ALU.mult)\
                    .then_inc(dve_made, tick("dve", "cbm", g))
                freed("dve", ("cb", g))
                low_to(F_[("pool", 0)] + 2 + g)
            low_to(F_[("K", 0, 0)])
            for i in range(2):
                scaled(pu[:, 2 * i:2 * i + 2, 16:16 + T], ("pool", 0, i), Rrow, "pu", i)
            low_to(F_[("K", 0, 0)] + 1)

            def gate_y(i):
                dve.wait_ge(*full(("y", i)))
                dve.wait_ge(act_made, after("act", "z", i))
                if i:
                    dve.wait_ge(dve_made, after("dve", "yg", i - 1))
                for c in range(2):
                    j = 2 * i + c
                    V.scalar_tensor_tensor(out=tmp[:, c, :], in0=xc[:, j, :], scalar=dskip[:, j:j + 1],
                                           in1=bank2(("y", i))[:, c, :], op0=ALU.mult, op1=ALU.add)\
                        .then_inc(dve_made, tick("dve"))
                freed("dve", ("y", i))
                own()
                V.tensor_tensor(zs[:, 2 * i:2 * i + 2, :], zs[:, 2 * i:2 * i + 2, :], tmp[:, :, :], ALU.mult)\
                    .then_inc(dve_made, tick("dve", "yg", i))

            def group_sum(g):
                dve.wait_ge(act_made, after("act", "ysq", 2 * g + 1))
                V.tensor_tensor(Ssum[:, :], sq[:, 0, :], sq[:, 1, :], ALU.add).then_inc(dve_made, tick("dve"))
                own()
                V.tensor_tensor(Sg[:, g, :], Ssum[:, 0:T], Ssum[:, T:H2], ALU.add)\
                    .then_inc(dve_made, tick("dve", "Sg", g))

            for i in range(8):
                dve.wait_ge(*full(("rows", i)))
                for hh in range(2):
                    h = 2 * i + hh
                    if h >= 4:
                        dve.wait_ge(pe_made, after("pe", "head", h - 4))
                    r = bank2(("rows", i))[:, hh, :]
                    for dst, src, c in ((0, 0, 0), (P, P, 3), (2 * P, P, 1)):
                        V.tensor_scalar(E[:, h % 4, dst:dst + P], r[:, src:src + P], cs[:, c, h:h + 1], 0.0,
                                        ALU.subtract, ALU.min)\
                            .then_inc(dve_made, tick("dve", *(("E", h) if dst == 2 * P else ())))
                freed("dve", ("rows", i))
                low_to(F_[("K", 0, 0)] + 2 + i)
                if i == 4:
                    for q in range(2):
                        low_of(k_lo[:, 2 * q:2 * q + 2, :], k_hi[:, 2 * q:2 * q + 2, :], ("K", 0, 0, q), "K", 0, q)
                if i == 5:
                    gate_y(0)
                if i == 7:
                    gate_y(1)
                    group_sum(0)
            low_to(F_[("out", 0, "early", 0)] + 2)
            for q in range(2):
                low_of(k_lo[:, 4 + 2 * q:6 + 2 * q, :], k_hi[:, 4 + 2 * q:6 + 2 * q, :], ("K", 0, 1, q), "K", 0, 2 + q)
            for g in range(4):
                dve.wait_ge(act_made, after("act", "mp", g | 1))
                V.scalar_tensor_tensor(out=mp_lo[:, g, :], in0=bank2(("pooled", g // 2))[:, g % 2, :],
                                       scalar=vec("pscale", g), in1=f(mp_hi[:, g, :]), op0=ALU.mult,
                                       op1=ALU.subtract).then_inc(dve_made, tick("dve", "mix", 0, g))
                if g % 2 == 1:
                    freed("dve", ("pooled", g // 2))
            gate_y(2)
            gate_y(3)
            group_sum(1)
            low_to(F_[("out", 0, "early", 1)] + 1)
            dve.wait_ge(*full(("gstat",)))
            V.tensor_scalar(stat[:, 8, 0:4], bank(("gstat",))[:, 0:4], 2.0 / D, RMS_EPS, ALU.mult, ALU.add)\
                .then_inc(dve_made, tick("dve", "gv"))
            freed("dve", ("gstat",))
            dve.wait_ge(act_made, after("act", "Rg"))
            for c in range(J):
                V.scalar_tensor_tensor(out=zs[:, c, :], in0=zs[:, c, :], scalar=vec("ssmn", c), in1=Rg[:, c // 4, :],
                                       op0=ALU.mult, op1=ALU.mult).then_inc(dve_made, tick("dve", "yn", c))
                if c >= 1:
                    dve.wait_ge(act_made, after("act", "mix", 0, 4 + c - 1))
                    V.tensor_tensor(my_lo[:, c - 1, :], zs[:, c - 1, :], f(my_hi[:, c - 1, :]), ALU.subtract)\
                        .then_inc(dve_made, tick("dve", "mix", 0, 4 + c - 1))
                if c % 2 == 1:
                    low_to(F_[("out", 0, "late", 0)] + c // 2)
            dve.wait_ge(act_made, after("act", "mix", 0, 4 + J - 1))
            V.tensor_tensor(my_lo[:, J - 1, :], zs[:, J - 1, :], f(my_hi[:, J - 1, :]), ALU.subtract)\
                .then_inc(dve_made, tick("dve", "mix", 0, 4 + J - 1))

            def norm_sum(l, n, m):
                dve.wait_ge(act_made, after("act", "nsq", l, n, 1))
                V.tensor_tensor(Ssum[:, :], sq[:, 0, :], sq[:, 1, :], ALU.add)\
                    .then_inc(dve_made, tick("dve", "Ssum", l, n, 1))
                L.also("dve", "Ssum", l, n, 2)
                for i in (2, 3):
                    dve.wait_ge(act_made, after("act", "nsq", l, n, i))
                    own()
                    V.tensor_tensor(Ssum[:, :], Ssum[:, :], sq[:, i % 2, :], ALU.add).then_inc(dve_made, tick("dve"))
                own()
                V.tensor_tensor(S2[:, :], Ssum[:, 0:T], Ssum[:, T:H2], ALU.add).then_inc(dve_made, tick("dve", "S2", l, n))

            def factor(l, n):
                dve.wait_ge(*full(("nstat", l, n)))
                s_ = 1 + 3 * l + n
                if n < 2:
                    V.tensor_scalar(stat[:, s_, 0:2], bank(("nstat", l, n))[:, 0:2], 1.0 / D, RMS_EPS,
                                    ALU.mult, ALU.add).then_inc(dve_made, tick("dve", "nv", l, n))
                else:
                    dve.wait_ge(pool_made, after("pool", "r4", l))
                    V.tensor_scalar(stat[:, s_, 2:4], bank(("nstat", l, n))[:, 0:2], 1.0 / D, None, ALU.mult)\
                        .then_inc(dve_made, tick("dve"))
                    own()
                    V.tensor_tensor(stat[:, s_, 4:6], stat[:, s_, 2:4], rfac[:, 13 + l, 4:6], ALU.mult)\
                        .then_inc(dve_made, tick("dve"))
                    own()
                    V.tensor_scalar(stat[:, s_, 0:2], stat[:, s_, 4:6], RMS_EPS, None, ALU.add)\
                        .then_inc(dve_made, tick("dve", "nv", l, n))
                freed("dve", ("nstat", l, n))

            def new_x(l, n, m, tag, gl, gs, base):
                dve.wait_ge(act_made, after("act", "Nrow", l, n))
                for j in range(J):
                    V.scalar_tensor_tensor(out=tmp[:, j % 2, :], in0=bank2(m[j // 2])[:, j % 2, :],
                                           scalar=gain(l, 2 * n + 1, j), in1=Nrow[:, :], op0=ALU.mult, op1=ALU.mult)\
                        .then_inc(dve_made, tick("dve"))
                    if j % 2 == 1:
                        freed("dve", m[j // 2])
                    own()
                    V.tensor_tensor(xT[:, j, :], xT[:, j, :], tmp[:, j % 2, :], ALU.add)\
                        .then_inc(dve_made, tick("dve", "x", tag or "out", j))
                    if tag and j >= 1:
                        low_h(tag, gl, gs, j - 1)
                    if tag and j % 2 == 1:
                        low_to(base + j // 2)
                if tag:
                    low_h(tag, gl, gs, J - 1)

            def x_factor(label, s_, *name):
                dve.wait_ge(*full(label))
                V.tensor_scalar(stat[:, s_, 0:2], bank(label)[:, 0:2], 1.0 / D, RMS_EPS, ALU.mult, ALU.add)\
                    .then_inc(dve_made, tick("dve", *name))
                freed("dve", label)

            cur = [0]

            def conv31(n):
                for _ in range(n):
                    if cur[0] >= 31 * J:
                        return
                    i, k, c = cur[0] // 62, cur[0] % 62 // 2, cur[0] % 2
                    j = 2 * i + c
                    acc = ps[:, 6 + c, 0:T]
                    src = vpad[:, j, k:k + T]
                    if k == 0:
                        dve.wait_ge(dve_made, after("dve", "v", i))
                        if i:
                            dve.wait_ge(dve_made, L.at[("dve", "tap", cur[0] - 2)])
                        V.tensor_scalar(acc, src, tap(k, j), vec("dwb", j), ALU.mult, ALU.add)\
                            .then_inc(dve_made, tick("dve", "tap", cur[0]))
                    else:
                        dve.wait_ge(dve_made, L.at[("dve", "tap", cur[0] - 2)])
                        V.scalar_tensor_tensor(out=acc if k < 30 else cv[:, j, :], in0=src, scalar=tap(k, j), in1=acc,
                                               op0=ALU.mult, op1=ALU.add)\
                            .then_inc(dve_made, tick("dve", "tap", cur[0]))
                    cur[0] += 1

            def attention(l):
                low_to(F_[("q", l, 1)])
                for h in range(2):
                    low_of(q_lo[:, 2 * h:2 * h + 2, :], q_hi[:, 2 * h:2 * h + 2, :], ("q", l, 0, h), "q", l, h)
                    low_to(F_[("q", l, 1)] + 1 + h)
                x_factor(("astat", l), 7, "av", l)
                dve.wait_ge(pool_made, after("pool", "ar", l))
                V.tensor_scalar(rfac[:, 11 + l, 2:4], rfac[:, 11 + l, 0:2], XA_SCALE, None, ALU.mult)\
                    .then_inc(dve_made, tick("dve"))
                V.tensor_scalar(rfac[:, 11 + l, 4:6], rfac[:, 11 + l, 0:2], -XA_SCALE, None, ALU.mult)\
                    .then_inc(dve_made, tick("dve"))
                low_to(F_[("V", l, 1)] + 0)
                for h in range(2, 4):
                    low_of(q_lo[:, 2 * h:2 * h + 2, :], q_hi[:, 2 * h:2 * h + 2, :], ("q", l, 1, h - 2), "q", l, h)

                def maxes(h):
                    dve.wait_ge(*full(("scores", l, h)))
                    V.tensor_reduce(stat[:, 8 + h, 0:2], bank2(("scores", l, h)), AX.X, ALU.max)\
                        .then_inc(dve_made, tick("dve"))
                    own()
                    V.tensor_tensor(stat[:, 8 + h, 2:4], stat[:, 8 + h, 0:2], rfac[:, 11 + l, 4:6], ALU.mult)\
                        .then_inc(dve_made, tick("dve", "nmax", l, h))

                def probs(h):
                    for t in range(TT):
                        dve.wait_ge(act_made, after("act", "exp", l, h, t))
                    V.reciprocal(stat[:, 8 + h, 6:8], stat[:, 8 + h, 4:6]).then_inc(dve_made, tick("dve"))
                    own()
                    for t in range(TT):
                        V.tensor_scalar(prob[:, h, t, :], prob[:, h, t, :], stat[:, 8 + h, 6 + t:7 + t], None, ALU.mult)\
                            .then_inc(dve_made, tick("dve", *(("prob", l, h) if t == TT - 1 else ())))

                def low_o(h):
                    low_of(h_lo[:, 2 * h:2 * h + 2, :], h_hi[:, 2 * h:2 * h + 2, :], ("o", l, h), "o", l, h)

                def low_pt(h):
                    low_of(pt_lo[:, h, :, :], pt_hi[:, h, :, :], ("pT", l, h), "pT", l, h)

                maxes(0)
                low_to(F_[("V", l, 1)] + 1)
                maxes(1)
                probs(0)
                low_to(F_[("V", l, 1)] + 2)
                probs(1)
                low_to(F_[("V", l, 1)] + 3)
                maxes(2)
                low_to(F_[("wo", l, 0)])
                maxes(3)
                for t in range(TT):
                    low_of(v_lo[:, t, 512:1024], v_hi[:, t, 512:1024], ("V", l, 1, t), "V", l, 1, t)
                probs(2)
                probs(3)
                low_pt(0)
                low_pt(1)
                low_to(F_[("wo", l, 0)] + 2)
                low_o(0)
                low_o(1)
                low_pt(2)
                low_pt(3)
                low_o(2)
                low_o(3)

            def mlp(l):
                for h in range(8):
                    base = F_[("w1", l, h)]
                    low_to(base + 5)
                    for q in range(2):
                        i = 2 * h + q
                        dve.wait_ge(act_made, after("act", "relu", l, i))
                        if i >= 2:
                            dve.wait_ge(act_made, after("act", "r", l, (i - 2) // 2, q))
                        V.scalar_tensor_tensor(out=rsq[:, q, :], in0=bank(("w1", l, h, q)), scalar=0.0,
                                               in1=relu[:, q, :], op0=ALU.max, op1=ALU.mult)\
                            .then_inc(dve_made, tick("dve", "rsq", l, i))
                        freed("dve", ("w1", l, h, q))
                        if q == 1:
                            low_r(l, h, 0)
                    low_r(l, h, 1)
                    if h == 0:
                        x_factor(("hstat", l), 15, "hv", l)
                    low_to(base + 7)

            def low_r(l, h, q):
                dve.wait_ge(act_made, after("act", "r", l, h, q))
                V.tensor_tensor(r_lo[:, h % 2, 2 * q:2 * q + 2, :], rsq[:, q, :].rearrange("p (c t) -> p c t", c=2),
                                f(r_hi[:, h % 2, 2 * q:2 * q + 2, :]), ALU.subtract)\
                    .then_inc(dve_made, tick("dve", "r", l, h, q))

            for l in range(2):
                if l == 1:
                    x_factor(("xstat", 0), 7, "r1v")
                    dve.wait_ge(act_made, after("act", "Rrow", 1))
                    V.tensor_tensor(Rsq[:, :], Rrow[:, :], Rrow[:, :], ALU.mult).then_inc(dve_made, tick("dve", "Rsq"))
                    V.memset(vpad[:, :, 0:30], 0.0).then_inc(dve_made, tick("dve"))
                    V.memset(ppad[:, :, 0:2], 0.0).then_inc(dve_made, tick("dve"))
                    own()
                    for g in range(2):
                        for q in range(2):
                            scaled(sg[:, 2 * q:2 * q + 2, :], ("gate", g, q), Rrow, "gate", g, q)
                            low_to(F_[("gate", g)] + 4 + 2 * q)
                            if g == 1:
                                conv31(8)
                            low_to(F_[("gate", g)] + 4 + 2 * q + 1)
                            if g == 1:
                                conv31(8)
                        for q in range(2):
                            i = 2 * g + q
                            dve.wait_ge(pool_made, after("pool", "sg", g, q))
                            dve.wait_ge(*full(("a", g, q)))
                            V.tensor_tensor(vpad[:, 2 * i:2 * i + 2, 30:30 + T], bank2(("a", g, q)),
                                            sg[:, 2 * q:2 * q + 2, :], ALU.mult).then_inc(dve_made, tick("dve", "v", i))
                            freed("dve", ("a", g, q))
                            low_to(F_[("a", g)] + 4 + 2 * q)
                            conv31(6)
                            low_to(F_[("a", g)] + 4 + 2 * q + 1)
                            conv31(6)
                    for g in range(2):
                        for q in range(2):
                            scaled(sg[:, 2 * q:2 * q + 2, :], ("cg", g, q), Rsq, "cg", g, q)
                            conv31(8)
                            low_to(F_[("cg", g)] + 4 + 2 * q + 1)
                        for q in range(2):
                            i = 2 * g + q
                            own()
                            dve.wait_ge(*full(("hh", g, q)))
                            V.tensor_tensor(ppad[:, 2 * i:2 * i + 2, 2:2 + T], bank2(("hh", g, q)),
                                            sg[:, 2 * q:2 * q + 2, :], ALU.mult).then_inc(dve_made, tick("dve"))
                            freed("dve", ("hh", g, q))
                            for k in range(3):
                                own()
                                for c in range(2):
                                    j = 2 * i + c
                                    src = ppad[:, j, k:k + T]
                                    if k == 0:
                                        V.tensor_scalar(cv3[:, j, :], src, vec("scw", k * J + j), None, ALU.mult)\
                                            .then_inc(dve_made, tick("dve"))
                                    else:
                                        V.scalar_tensor_tensor(out=cv3[:, j, :], in0=src, scalar=vec("scw", k * J + j),
                                                               in1=cv3[:, j, :], op0=ALU.mult, op1=ALU.add)\
                                            .then_inc(dve_made, tick("dve", *(("cv3", i) if k == 2 and c == 1 else ())))
                            low_to(F_[("hh", g)] + 4 + 2 * q)
                            conv31(5)
                            low_to(F_[("hh", g)] + 4 + 2 * q + 1)
                    for g in range(2):
                        for q in range(2):
                            i = 2 * g + q
                            dve.wait_ge(*full(("bg", g, q)))
                            dve.wait_ge(pool_made, after("pool", "cv3R", i))
                            if i >= 2:
                                dve.wait_ge(act_made, after("act", "mix", 1, J + 2 * (i - 2)))
                            V.tensor_tensor(sct[:, i % 2, :].rearrange("p (c t) -> p c t", c=2), bank2(("bg", g, q)),
                                            cv3[:, 2 * i:2 * i + 2, :], ALU.mult).then_inc(dve_made, tick("dve", "sc", i))
                            freed("dve", ("bg", g, q))
                            conv31(5)
                            dve.wait_ge(act_made, after("act", "mix", 1, J + 2 * i))
                            V.tensor_tensor(ml[:, J + 2 * i:J + 2 * i + 2, :],
                                            sct[:, i % 2, :].rearrange("p (c t) -> p c t", c=2),
                                            f(mh[:, J + 2 * i:J + 2 * i + 2, :]), ALU.subtract)\
                                .then_inc(dve_made, tick("dve", "mix", 1, J + 2 * i))
                            L.at[("dve", "mix", 1, J + 2 * i + 1)] = L.at[("dve", "mix", 1, J + 2 * i)]
                            conv31(4)
                            low_to(F_[("bg", g)] + 4 + 2 * q + 1)
                    for g in range(2):
                        for q in range(2):
                            low_of(k_lo[:, 4 * g + 2 * q:4 * g + 2 * q + 2, :], k_hi[:, 4 * g + 2 * q:4 * g + 2 * q + 2, :],
                                   ("K", 1, g, q), "K", 1, 2 * g + q)
                            conv31(12)
                            low_to(F_[("K", 1, g)] + 4 + 2 * q + 1)
                    conv31(31 * J)
                    own()
                    V.tensor_tensor(Ssum[:, :].rearrange("p (c t) -> p c t", c=2), cv[:, 0:2, :], cv[:, 2:4, :], ALU.add)\
                        .then_inc(dve_made, tick("dve"))
                    for i in (2, 3):
                        own()
                        V.tensor_tensor(Ssum[:, :].rearrange("p (c t) -> p c t", c=2),
                                        Ssum[:, :].rearrange("p (c t) -> p c t", c=2), cv[:, 2 * i:2 * i + 2, :], ALU.add)\
                            .then_inc(dve_made, tick("dve"))
                    own()
                    V.tensor_tensor(S2[:, :], Ssum[:, 0:T], Ssum[:, T:H2], ALU.add).then_inc(dve_made, tick("dve", "S2", "mu"))
                    low_to(F_[("out", 1, "early", 1)] + 0)
                    dve.wait_ge(*full(("mustat",)))
                    V.tensor_scalar(rfac[:, 9, 0:2], bank(("mustat",))[:, 0:2], 1.0 / D, None, ALU.mult)\
                        .then_inc(dve_made, tick("dve", "negmu"))
                    freed("dve", ("mustat",))
                    low_to(F_[("out", 1, "early", 1)] + 1)
                    dve.wait_ge(act_made, after("act", "murow"))
                    for i in range(4):
                        V.tensor_tensor(cv[:, 2 * i:2 * i + 2, :], cv[:, 2 * i:2 * i + 2, :], row2(Nrow), ALU.subtract)\
                            .then_inc(dve_made, tick("dve", "vc", i))
                    dve.wait_ge(act_made, after("act", "vsq", 1))
                    V.tensor_tensor(Ssum[:, :], sq[:, 0, :], sq[:, 1, :], ALU.add).then_inc(dve_made, tick("dve", "Sv", 0))
                    L.also("dve", "Sv", 1)
                    low_to(F_[("out", 1, "early", 1)] + 2)
                    for i in (2, 3):
                        dve.wait_ge(act_made, after("act", "vsq", i))
                        own()
                        V.tensor_tensor(Ssum[:, :], Ssum[:, :], sq[:, i % 2, :], ALU.add).then_inc(dve_made, tick("dve"))
                    own()
                    V.tensor_tensor(S2[:, :], Ssum[:, 0:T], Ssum[:, T:H2], ALU.add)\
                        .then_inc(dve_made, tick("dve", "S2", "var"))
                    low_to(F_[("out", 1, "late", 0)] + 0)
                    dve.wait_ge(*full(("varstat",)))
                    V.tensor_scalar(stat[:, 9, 0:2], bank(("varstat",))[:, 0:2], 1.0 / D, LN_EPS, ALU.mult, ALU.add)\
                        .then_inc(dve_made, tick("dve", "lnv"))
                    freed("dve", ("varstat",))
                    low_to(F_[("out", 1, "late", 0)] + 1)
                    dve.wait_ge(act_made, after("act", "varrow"))
                    for c in range(J + 1):
                        if c < J:
                            V.scalar_tensor_tensor(out=cv[:, c, :], in0=cv[:, c, :], scalar=vec("lng", c), in1=Rrow[:, :],
                                                   op0=ALU.mult, op1=ALU.mult).then_inc(dve_made, tick("dve", "vn", c))
                        if c >= 1:
                            dve.wait_ge(act_made, after("act", "mix", 1, c - 1))
                            V.tensor_tensor(ml[:, c - 1, :], cv[:, c - 1, :], f(mh[:, c - 1, :]), ALU.subtract)\
                                .then_inc(dve_made, tick("dve", "mix", 1, c - 1))
                        if c % 2 == 1:
                            low_to(F_[("out", 1, "late", 0)] + 1 + c // 2)
                m = [("out", l, g, q) for g in range(2) for q in range(2)]
                low_to(F_[("V", l, 0)] + 2)
                norm_sum(l, 0, m)
                low_to(F_[("q", l, 0)])
                for t in range(TT):
                    low_of(v_lo[:, t, 0:512], v_hi[:, t, 0:512], ("V", l, 0, t), "V", l, 0, t)
                factor(l, 0)
                low_to(F_[("q", l, 0)] + 1)
                new_x(l, 0, m, f"q{l}", l, 2, F_[("q", l, 0)])
                attention(l)
                m = [("wo", l, g, q) for g in range(2) for q in range(2)]
                low_to(F_[("w1", l, 0)] + 1)
                norm_sum(l, 1, m)
                factor(l, 1)
                new_x(l, 1, m, f"mlp{l}", l, 4, F_[("w1", l, 0)])
                mlp(l)
                m = [("w2", l, g, q) for g in range(2) for q in range(2)]
                low_to(F_[("gate", 0)] + 1 if l == 0 else NU)
                norm_sum(l, 2, m)
                factor(l, 2)
                new_x(l, 2, m, "in1" if l == 0 else None, 1, 0, F_[("gate", 0)])
            for i in (1, 3):
                dve.wait_ge(*full(("outT", i)))
                V.tensor_copy(otok[:, i // 2, 512:1024], bank(("outT", i))).then_inc(dve_made, tick("dve", "otok", i))

        @block.gpsimd
        def _(pool):
            G = nc.gpsimd
            nu = [0]

            def low_to(u):
                while nu[0] <= min(u, NU - 1):
                    v = nu[0]
                    if pool_lo[v]:
                        pool.wait_ge(hi_ready, v + 1)
                        G.tensor_tensor(w_lo[:, v % SPLIT, :, :], raw[:, v % RAW, :, :], f(w_hi[:, v % SPLIT, :, :]),
                                        ALU.subtract).then_inc(lo_ready_pool, 1)
                    nu[0] += 1

            def own():
                pool.wait_ge(pool_made, now("pool"))

            F_ = first
            G.memset(ident[:, :], 0.0).then_inc(pool_made, tick("pool"))
            G.memset(ones[:, :], 1.0).then_inc(pool_made, tick("pool"))
            own()
            G.affine_select(out=ident[:, :], in_=ident[:, :], compare_op=ALU.not_equal, fill=1.0, base=0,
                            pattern=[[-1, P]], channel_multiplier=1).then_inc(pool_made, tick("pool", "ident"))
            G.affine_select(out=tri[:, :], in_=ones[:, :], compare_op=ALU.is_ge, fill=0.0, base=0,
                            pattern=[[1, P]], channel_multiplier=-1).then_inc(pool_made, tick("pool"))
            own()
            G.tensor_copy(cbmask[:, 0:P], tri[:, :]).then_inc(pool_made, tick("pool"))
            G.memset(cbmask[:, P:2 * P], 1.0).then_inc(pool_made, tick("pool"))
            G.tensor_copy(cbmask[:, 2 * P:3 * P], tri[:, :]).then_inc(pool_made, tick("pool", "cbmask"))
            pool.wait_ge(dve_made, after("dve", "mhalf"))

            def rsqrt(dst, src, *name):
                G.tensor_tensor(dst, src, mhalf[:, 0:dst.shape[1]], ALU.pow).then_inc(pool_made, tick("pool", *name))

            pool.wait_ge(dve_made, after("dve", "v0"))
            rsqrt(rfac[:, 0, 0:2], stat[:, 1, 0:2], "r0")
            for g, w in enumerate(POOL_WINDOWS):
                G.memset(icnt[:, g, :], 1.0 / w).then_inc(pool_made, tick("pool"))
                own()
                for c in range(w - 1):
                    G.memset(icnt[:, g, c:c + 1], 1.0 / (c + 1)).then_inc(pool_made, tick("pool"))
            low_to(F_[("pool", 0)] + 3)

            def heads(i):
                for h in (2 * i, 2 * i + 1):
                    pool.wait_ge(act_made, after("act", "E", h))
                    if h == 0:
                        pool.wait_ge(dve_made, after("dve", "cbm", 1))
                    G.tensor_tensor(E[:, h % 4, :], E[:, h % 4, :], cbm[:, h // 8, :], ALU.mult)\
                        .then_inc(pool_made, tick("pool", "E", h))

            def window(g):
                w = POOL_WINDOWS[g]
                pool.wait_ge(dve_made, after("dve", "pu", g // 2))
                src, step, k = pu[:, g, :], 1, 0
                N = T + 16
                bufs = (pw1, pw2)
                while step < w:
                    dst = bufs[k % 2]
                    own()
                    G.tensor_tensor(dst[:, step:N], src[:, step:N], src[:, 0:N - step], ALU.add)\
                        .then_inc(pool_made, tick("pool"))
                    G.memset(dst[:, 0:step], 0.0).then_inc(pool_made, tick("pool"))
                    src, step, k = dst[:, :], step * 2, k + 1
                own()
                dst = bufs[k % 2]
                G.tensor_scalar(dst[:, 32:N], src[:, 32:N], 1.0 / w, None, ALU.mult).then_inc(pool_made, tick("pool"))
                G.tensor_tensor(dst[:, 16:32], src[:, 16:32], icnt[:, g, :], ALU.mult).then_inc(pool_made, tick("pool"))
                own()
                G.tensor_tensor(pdiff[:, g, :], dst[:, 16:N], pu[:, g, 16:N], ALU.subtract)\
                    .then_inc(pool_made, tick("pool", "pdiff", g))

            for i in range(8):
                low_to(F_[("K", 0, 0)] + i)
                heads(i)
                if i >= 4:
                    window(i - 4)
            low_to(F_[("out", 0, "early", 1)] + 1)
            pool.wait_ge(dve_made, after("dve", "gv"))
            rsqrt(rfac[:, 8, 0:4], stat[:, 8, 0:4], "gr")
            low_to(F_[("V", 0, 0)])

            def x_sums(tag):
                pool.wait_ge(act_made, after("act", "xsq", tag, 1))
                G.tensor_tensor(Ssum[:, :], sq[:, 0, :], sq[:, 1, :], ALU.add).then_inc(pool_made, tick("pool", "Sx", tag, 0))
                L.also("pool", "Sx", tag, 1)
                for i in (2, 3):
                    pool.wait_ge(act_made, after("act", "xsq", tag, i))
                    own()
                    G.tensor_tensor(Ssum[:, :], Ssum[:, :], sq[:, i % 2, :], ALU.add).then_inc(pool_made, tick("pool"))
                own()
                G.tensor_tensor(S2[:, :], Ssum[:, 0:T], Ssum[:, T:H2], ALU.add).then_inc(pool_made, tick("pool", "Sx", tag))

            for l in range(2):
                if l == 1:
                    pool.wait_ge(dve_made, after("dve", "r1v"))
                    rsqrt(rfac[:, 7, 0:2], stat[:, 7, 0:2], "r1")
                    pool.wait_ge(act_made, after("act", "Rrow", 1))
                    for g in range(2):
                        for q in range(2):
                            low_to(F_[("gate", g)] + 4 + 2 * q - 1)
                            pool.wait_ge(act_made, after("act", "sig", g, q))
                            G.tensor_tensor(sg[:, 2 * q:2 * q + 2, :], sg[:, 2 * q:2 * q + 2, :], row2(Rrow), ALU.mult)\
                                .then_inc(pool_made, tick("pool", "sg", g, q))
                            low_to(F_[("gate", g)] + 4 + 2 * q + 1)
                        low_to(F_[("a", g)] + 7)
                    for g in range(2):
                        for q in range(2):
                            i = 2 * g + q
                            low_to(F_[("hh", g)] + 3 + 2 * q)
                            pool.wait_ge(dve_made, after("dve", "cv3", i))
                            G.tensor_tensor(cv3[:, 2 * i:2 * i + 2, :], cv3[:, 2 * i:2 * i + 2, :], row2(Rrow), ALU.mult)\
                                .then_inc(pool_made, tick("pool", "cv3R", i))
                    low_to(F_[("out", 1, "early", 1)] + 3)
                    pool.wait_ge(dve_made, after("dve", "lnv"))
                    rsqrt(rfac[:, 10, 0:2], stat[:, 9, 0:2], "lnr")
                    low_to(F_[("V", 1, 0)])
                pool.wait_ge(dve_made, after("dve", "nv", l, 0))
                rsqrt(rfac[:, 1 + 3 * l, 0:2], stat[:, 1 + 3 * l, 0:2], "nr", l, 0)
                x_sums(f"q{l}")
                pool.wait_ge(dve_made, after("dve", "av", l))
                rsqrt(rfac[:, 11 + l, 0:2], stat[:, 7, 0:2], "ar", l)
                pool.wait_ge(dve_made, after("dve", "nv", l, 1))
                rsqrt(rfac[:, 2 + 3 * l, 0:2], stat[:, 2 + 3 * l, 0:2], "nr", l, 1)
                x_sums(f"mlp{l}")
                pool.wait_ge(dve_made, after("dve", "hv", l))
                rsqrt(rfac[:, 13 + l, 0:2], stat[:, 15, 0:2])
                own()
                G.tensor_tensor(rfac[:, 13 + l, 2:4], rfac[:, 13 + l, 0:2], rfac[:, 13 + l, 0:2], ALU.mult)\
                    .then_inc(pool_made, tick("pool"))
                own()
                G.tensor_tensor(rfac[:, 13 + l, 4:6], rfac[:, 13 + l, 2:4], rfac[:, 13 + l, 2:4], ALU.mult)\
                    .then_inc(pool_made, tick("pool", "r4", l))
                pool.wait_ge(dve_made, after("dve", "nv", l, 2))
                s_ = 3 + 3 * l
                rsqrt(rfac[:, s_, 2:4], stat[:, s_, 0:2])
                own()
                G.tensor_tensor(rfac[:, s_, 0:2], rfac[:, s_, 2:4], rfac[:, 13 + l, 2:4], ALU.mult)\
                    .then_inc(pool_made, tick("pool", "nr", l, 2))
                if l == 0:
                    x_sums("in1")

    return L.at


INPUTS = ["x", "mem", "norm_gains", "xa_wq", "xa_wkv", "xa_wo", "mlp_w1", "mlp_w2", "ab_w_in", "pool_w",
          "pool_scale", "ssm_conv_w", "ssm_conv_b", "ssm_dt_bias", "ssm_a_log", "ssm_d", "ssm_norm", "ab_w_out",
          "cd_w_in", "conf_dw_w", "conf_dw_b", "conf_ln_g", "conf_ln_b", "sc_conv_w", "cd_w_out"]


def kernel(**inputs):
    import concourse.bacc as bacc
    from concourse.bass_utils import run_bass_kernel_spmd

    arrays = {f"in_{n}": np.ascontiguousarray(inputs[n]) for n in INPUTS}
    counts = None
    for _ in range(2):
        nc = bacc.Bacc("TRN2", target_bir_lowering=False, num_devices=1)
        A = {n: nc.dram_tensor(f"in_{n}", inputs[n].shape, F32, kind="ExternalInput").ap() for n in INPUTS}
        out = nc.dram_tensor("out_0", inputs["x"].shape, F32, kind="ExternalOutput").ap()
        counts = trunk(nc, A, out, counts)
    return run_bass_kernel_spmd(nc, [arrays], core_ids=[0]).results[0]["out_0"]
```

```python
from contextlib import ExitStack

import numpy as np
import concourse.bass as bass
from concourse import mybir

F32 = mybir.dt.float32
F32R = mybir.dt.float32r
ALU = mybir.AluOpType
ACT = mybir.ActivationFunctionType
AX = mybir.AxisListType

P = 128
SLOTS = 6
POOL_WINDOWS = (2, 4, 8, 16)
RMS_EPS, LN_EPS = 1e-6, 1e-5


class Ledger:

    def __init__(self, known):
        self.count, self.at, self.known = {}, {}, known

    def tick(self, sem, *label):
        self.count[sem] = self.count.get(sem, 0) + 1
        if label:
            assert (sem, *label) not in self.at, label
            self.at[(sem, *label)] = self.count[sem]
        return 1

    def after(self, sem, *label):
        if self.known is None:
            return 1
        return self.known[(sem, *label)]

    def also(self, sem, *label):
        self.at[(sem, *label)] = self.count[sem]

    def now(self, sem):
        return self.count[sem]


def weight_plan():
    s = []
    for j in range(3):
        s.append((("xbc", j), "ab_in", 0, 0, 8, 1536 + 512 * j))
    for j in range(2):
        s.append((("z", j), "ab_in", 0, 0, 8, 512 + 512 * j))
    s.append((("pool", 0), "ab_in", 0, 0, 8, 0))
    for l in range(2):
        if l == 1:
            for name, c in (("gate", 1024), ("a", 0), ("gate", 1536), ("a", 512), ("cg", 3072), ("hh", 4096),
                            ("cg", 3584), ("hh", 4608), ("bg", 2048), ("bg", 2560)):
                s.append(((name, (c // 512) % 2), "cd_in", 0, 0, 8, c))
        for g in range(2 if l == 0 else 1):
            s.append((("K", l, g), "wkv", l, 0, 8, 512 * g))
        out, early, late = (("ab_out", (0, 4), (4, 8)), ("cd_out", (8, 8), (0, 8)))[l]
        for part, (k0, nk) in (("early", early), ("late", late)):
            for g in range(2):
                s.append((("out", l, part, g), out, 0, 128 * k0, nk, 512 * g))
        s.append((("V", 0, 0), "wkv", 0, 0, 8, 1024) if l == 0 else (("K", 1, 1), "wkv", 1, 0, 8, 512))
        for g in range(2):
            s.append((("q", l, g), "wq", l, 0, 8, 512 * g))
        if l == 0:
            s.append((("V", 0, 1), "wkv", 0, 0, 8, 1536))
        for g in range(2):
            s.append((("wo", l, g), "wo", l, 0, 8, 512 * g))
        if l == 0:
            s.append((("V", 1, 0), "wkv", 1, 0, 8, 1024))
        for h in range(9):
            for i in ([0, 1] if h == 0 else [h + 1] if h < 7 else []):
                s.append((("w1", l, i), "w1", l, 0, 8, 512 * i))
            if h < 8:
                for g in range(2):
                    s.append((("w2", l, h, g), "w2", l, 512 * h, 4, 512 * g))
        if l == 0:
            s.append((("V", 1, 1), "wkv", 1, 0, 8, 1536))
    return s


SETS = {0: dict(M0=(0, 1), M1=(2, 3), FI=(4, 5), T=(6, 7)),
        1: dict(M0=(2, 3), M1=(4, 5), FI=(0, 1), T=(6, 7))}


def bank_plan():
    u = []

    def pair(label, banks):
        u.extend([(label + (0,), banks[0]), (label + (1,), banks[1])])

    u.append((("vecs",), 4))
    for i in range(4):
        u.append((("xT", i), i))
    u.append((("R0",), 5))
    pair(("xbc", 0), (6, 7))
    u.append((("dt",), 4))
    for i in range(4):
        u.append((("memT", i), i))
    pair(("xbc", 1), (0, 1))
    u.append((("dtT",), 5))
    pair(("xbc", 2), (2, 3))
    u.append((("cs",), 6))
    pair(("z", 0), (0, 1))
    for i, b in enumerate((6, 7, 4, 5)):
        u.append((("xsT", i), b))
    pair(("z", 1), (2, 3))
    u.append((("cb", 0), 6))
    u.append((("cb", 1), 7))
    pair(("pool", 0), (0, 1))
    for i in range(8):
        if i == 3:
            pair(("K", 0, 0), (2, 3))
        if i == 7:
            pair(("K", 0, 1), (0, 1))
        u.append((("rows", i), 6 + i % 2))
        if i >= 2 and i % 2 == 1:
            u.append((("y", (i - 3) // 2), 4 + (i - 3) // 2 % 2))
    u.append((("y", 3), 5))
    u.append((("pooled", 0), 6))
    u.append((("pooled", 1), 7))
    u.append((("gstat",), 4))
    u.append((("grow",), 5))
    for l in range(2):
        b = SETS[l]
        M0, M1, FI, T = b["M0"], b["M1"], b["FI"], b["T"]
        if l == 1:
            cycle = [(4, 5), (0, 1), (2, 3)]
            names = [("gate", 0), ("a", 0), ("gate", 1), ("a", 1), ("cg", 0), ("hh", 0), ("cg", 1), ("hh", 1),
                     ("bg", 0), ("bg", 1), ("K", 1, 0)]
            for n, name in enumerate(names):
                pair(name, cycle[n % 3])
                if n == 0:
                    u.append((("xstat", 0), 6))
                    u.append((("R1",), 7))
            u.append((("conv7",), 7))
            u.append((("mustat",), 0))
            u.append((("murow",), 1))
            u.append((("varstat",), 0))
            u.append((("varrow",), 1))
        pair(("out", l, 0), M0)
        pair(("out", l, 1), M1)
        pair(("V", 0, 0) if l == 0 else ("K", 1, 1), FI)
        u.append((("nstat", l, 0), T[0]))
        u.append((("nrow", l, 0), T[1]))
        pair(("q", l, 0), T)
        u.append((("astat", l), FI[0]))
        pair(("q", l, 1), M0)
        u.append((("scores", l, 0), FI[1]))
        u.append((("scores", l, 1), M1[0]))
        if l == 0:
            pair(("V", 0, 1), T)
        u.append((("scores", l, 2), M1[1]))
        u.append((("scores", l, 3), FI[0]))
        u.append((("pT", l, 0), FI[1]))
        u.append((("pT", l, 1), M1[0]))
        u.append((("o", l, 0), M0[0]))
        u.append((("o", l, 1), M0[1]))
        u.append((("pT", l, 2), M1[1]))
        u.append((("pT", l, 3), FI[0]))
        u.append((("o", l, 2), FI[1]))
        u.append((("o", l, 3), M1[0]))
        pair(("wo", l, 0), T)
        pair(("wo", l, 1), M0)
        if l == 0:
            pair(("V", 1, 0), M1)
        u.append((("nstat", l, 1), FI[0]))
        u.append((("nrow", l, 1), FI[1]))
        for h in range(8):
            pair(("w1", l, h), FI if h % 2 == 0 else M1)
            if h == 0:
                u.append((("hstat", l), T[0]))
        pair(("w2", l, 0), T)
        pair(("w2", l, 1), M0)
        if l == 0:
            pair(("V", 1, 1), M1)
        u.append((("nstat", l, 2), FI[0]))
        u.append((("nrow", l, 2), FI[1]))
    for i, b in enumerate((M1[0], M1[1], FI[0], T[0])):
        u.append((("outT", i), b))
    return u


POOL_LO = []


def trunk(nc, A, out, known):
    T = A["x"].shape[1]
    D = A["x"].shape[2]
    J = D // P
    HEADS = A["ssm_a_log"].shape[1]
    TT = T // P
    H2 = T * 2
    XA_SCALE = 1.0 / 16.0
    L = Ledger(known)
    tick, after, now = L.tick, L.after, L.now

    mats = {"ab_in": A["ab_w_in"], "ab_out": A["ab_w_out"], "cd_in": A["cd_w_in"], "cd_out": A["cd_w_out"],
            "wkv": A["xa_wkv"], "wq": A["xa_wq"], "wo": A["xa_wo"], "w1": A["mlp_w1"], "w2": A["mlp_w2"]}
    units, first, size = [], {}, {}
    for name, m, l, row, nk, col in weight_plan():
        first[name], size[name] = len(units), nk // 2
        for i in range(nk // 2):
            r = row + 256 * i
            units.append(mats[m][l, r:r + 256, col:col + 512].rearrange("(i p) c -> p i c", p=P))
    NU = len(units)
    pool_lo = [False] * NU
    for u in range(first[("xbc", 0)], first[("out", 0, "late", 0)]):
        pool_lo[u] = u % 2 == 1
    for u in range(first[("gate", 1)], first[("out", 1, "late", 0)]):
        pool_lo[u] = u % 8 != 7
    for seg in [("q", 0, 0), ("q", 1, 0), ("w1", 0, 0), ("w1", 1, 0), ("gate", 0)]:
        pool_lo[first[seg] + 1] = pool_lo[first[seg] + 3] = True
    for seg in [("V", 0, 1), ("wo", 0, 0), ("wo", 0, 1), ("wo", 1, 0), ("wo", 1, 1)]:
        pool_lo[first[seg] + 1] = pool_lo[first[seg] + 3] = True
    POOL_LO[:] = pool_lo
    lo_count, nd, npl = [], 0, 0
    for u in range(NU):
        nd, npl = nd + (not pool_lo[u]), npl + pool_lo[u]
        lo_count.append(npl if pool_lo[u] else nd)

    use, by_use, uses = {}, {}, [0] * 8
    for label, b in bank_plan():
        assert label not in use, label
        use[label] = (b, uses[b])
        by_use[b, uses[b]] = label
        uses[b] += 1

    ctx = ExitStack()
    with ctx:
        def sb(name, shape, dt=F32, scope=ctx):
            return scope.enter_context(nc.sbuf_tensor(name, [P, *shape], dt))

        def sem(name):
            return ctx.enter_context(nc.semaphore(name))

        xT = sb("xT", [J, T])
        h_hi, h_lo = sb("h_hi", [J, T], F32R), sb("h_lo", [J, T], F32R)
        mem_hi, mem_lo = sb("mem_hi", [J, T], F32R), sb("mem_lo", [J, T], F32R)
        k_hi, k_lo = sb("k_hi", [J, T], F32R), sb("k_lo", [J, T], F32R)
        w_hi = sb("w_hi", [SLOTS, 2, 512], F32R)
        with ExitStack() as s:
            raw = sb("raw", [SLOTS, 2, 512], scope=s)
        w_lo = sb("w_lo", [SLOTS, 2, 512], F32R)
        ident, ones, tri, cbmask = sb("ident", [P]), sb("ones", [P]), sb("tri", [P]), sb("cbmask", [3 * P])
        Rrow, Nrow = sb("Rrow", [T]), sb("Nrow", [T])
        vecs = sb("vecs", [512])
        sq = sb("sq", [2, H2])
        Ssum, S2 = sb("Ssum", [H2]), sb("S2", [T])
        stat = sb("stat", [16, 8])
        rfac = sb("rfac", [16, 8])
        mhalf = sb("mhalf", [8])
        tmp = sb("tmp", [2, T])
        with ExitStack() as s:
            v_hi, v_lo = sb("v_hi", [TT, D], F32R, s), sb("v_lo", [TT, D], F32R, s)
        with ExitStack() as s:
            my_hi, my_lo = sb("my_hi", [J, T], F32R, s), sb("my_lo", [J, T], F32R, s)
            hold = s.pop_all()
        ctx.enter_context(hold)
        with ExitStack() as s:
            xtok, memtok = sb("xtok", [TT, D], scope=s), sb("memtok", [TT, D], scope=s)
            stage = sb("stage", [4, P], scope=s)
        with ExitStack() as s:
            xdt = sb("xdt", [TT, D], scope=s)
            mp_hi, mp_lo = sb("mp_hi", [4, T], F32R, s), sb("mp_lo", [4, T], F32R, s)
            E = sb("E", [4, 3 * P], scope=s)
            cbm = sb("cbm", [2, 3 * P], scope=s)
            zs = sb("zs", [J, T], scope=s)
            xc = sb("xc", [12, T], scope=s)
            upad = sb("upad", [2, 2, T + 3], scope=s)
            pu = sb("pu", [4, T + 16], scope=s)
            pw1, pw2 = sb("pw1", [T + 16], scope=s), sb("pw2", [T + 16], scope=s)
            pdiff = sb("pdiff", [4, T], scope=s)
            Sg = sb("Sg", [2, T], scope=s)
            Rg = sb("Rg", [2, T], scope=s)
            icnt = sb("icnt", [4, 16], scope=s)
            poolw = sb("poolw", [4, P], scope=s)
            wdt, wdtg = sb("wdt", [J, HEADS], scope=s), sb("wdtg", [J, HEADS], scope=s)
            dtT = sb("dtT", [T], scope=s)
            dtb, expA, dskip = sb("dtb", [HEADS], scope=s), sb("expA", [HEADS], scope=s), sb("dskip", [J], scope=s)
            sp = sb("sp", [10, 2 * HEADS], scope=s)
            cs = sb("cs", [4, HEADS], scope=s)
        with ExitStack() as s:
            vpad = sb("vpad", [J, T + 30], scope=s)
            cv, cv3 = sb("cv", [J, T], scope=s), sb("cv3", [J, T], scope=s)
            ppad = sb("ppad", [2, 2, T + 2], scope=s)
            sg = sb("sg", [4, T], scope=s)
            mh, ml = sb("mh", [2 * J, T], F32R, s), sb("ml", [2 * J, T], F32R, s)
            Rsq = sb("Rsq", [T], scope=s)
            sct = sb("sct", [2, H2], scope=s)
        with ExitStack() as s:
            q_hi, q_lo = sb("q_hi", [J, T], F32R, s), sb("q_lo", [J, T], F32R, s)
            prob = sb("prob", [4, TT, T], scope=s)
            pt_hi, pt_lo = sb("pt_hi", [4, TT, T], F32R, s), sb("pt_lo", [4, TT, T], F32R, s)
        with ExitStack() as s:
            r_hi, r_lo = sb("r_hi", [2, 4, T], F32R, s), sb("r_lo", [2, 4, T], F32R, s)
            relu, rsq = sb("relu", [2, H2], scope=s), sb("rsq", [2, H2], scope=s)
            otok = sb("otok", [TT, D], scope=s)
        ps = ctx.enter_context(nc.psum_tensor("ps", [P, 8, 512], F32))

        x_landed, mem_landed, vec_landed, ssm_landed, out_stored = (
            sem(n) for n in ("x_landed", "mem_landed", "vec_landed", "ssm_landed", "out_stored"))
        raw_landed = [sem(f"raw_landed{i}") for i in range(SLOTS)]
        hi_ready, lo_ready_dve, lo_ready_pool = (sem(n) for n in ("hi_ready", "lo_ready_dve", "lo_ready_pool"))
        pe_made, act_made, dve_made, pool_made = sem("pe_made"), sem("act_made"), sem("dve_made"), sem("pool_made")

        GAIN, MISC, DW = 0, 128, 256

        def gain(l, s, j):
            return vecs[:, GAIN + (l * 6 + s) * J + j:GAIN + (l * 6 + s) * J + j + 1]

        MISC_ROWS = [("convw", A["ssm_conv_w"].rearrange("a k (j p) -> (a k j) p", p=P)),
                     ("convb", A["ssm_conv_b"].rearrange("a (j p) -> (a j) p", p=P)),
                     ("ssmn", A["ssm_norm"].rearrange("a (j p) -> (a j) p", p=P)),
                     ("pscale", A["pool_scale"].rearrange("a (j p) -> (a j) p", p=P)),
                     ("dwb", A["conf_dw_b"].rearrange("a (j p) -> (a j) p", p=P)),
                     ("lng", A["conf_ln_g"].rearrange("a (j p) -> (a j) p", p=P)),
                     ("lnb", A["conf_ln_b"].rearrange("a (j p) -> (a j) p", p=P)),
                     ("scw", A["sc_conv_w"].rearrange("a k (j p) -> (a k j) p", p=P))]
        misc_at, n = {}, 0
        for name, v in MISC_ROWS:
            misc_at[name] = MISC + n
            n += v.shape[0]
        MISC_N = n

        def vec(name, j):
            return vecs[:, misc_at[name] + j:misc_at[name] + j + 1]

        def tap(k, j):
            return vecs[:, DW + k * J + j:DW + k * J + j + 1]

        dw_rows = A["conf_dw_w"].rearrange("a k (j p) -> (a k j) p", p=P)
        DWN = dw_rows.shape[0]

        def bank(label):
            return ps[:, use[label][0], :]

        def bank2(label):
            return ps[:, use[label][0], :].rearrange("p (c t) -> p c t", c=2)

        def full(label):
            return pe_made, after("pe", label)

        def freed(engine, label):
            L.at[("free", label)] = (engine, now(engine))

        def row2(r):
            return r[:, :].unsqueeze(1).broadcast_to([P, 2, T])

        def f(ap):
            return ap.bitcast(F32)

        def lo_wait(u):
            return (lo_ready_pool if pool_lo[u] else lo_ready_dve), lo_count[u]

        def mixer_out(l, kt):
            if l == 0:
                return (mp_hi[:, kt, :], mp_lo[:, kt, :]) if kt < 4 else (my_hi[:, kt - 4, :], my_lo[:, kt - 4, :])
            return mh[:, kt, :], ml[:, kt, :]

        FILL = {(0, 0): ("V", 0, 0), (0, 1): ("V", 1, 0), (0, 2): ("V", 1, 1), (1, 0): ("K", 1, 1)}

        def fill_dst(seg, q):
            if seg[0] == "V":
                c = slice(512 * seg[2], 512 * seg[2] + 512)
                return v_hi[:, q, c], v_lo[:, q, c]
            c = slice(4 * seg[2] + 2 * q, 4 * seg[2] + 2 * q + 2)
            return k_hi[:, c, :], k_lo[:, c, :]

        def fill_name(seg, q):
            return seg + (q,) if seg[0] == "V" else ("K", seg[1], 2 * seg[2] + q)

        def diag(k):
            return tmp[:, k % 4 // 2, k % 2 * P:(k % 2 + 1) * P]

        block = ctx.enter_context(nc.Block())

        @block.sync
        def _(sp_):
            sp_.dma_start(xtok[:, :, :], A["x"][0].rearrange("(t p) d -> p t d", p=P)).then_inc(x_landed, 16)
            for u in range(NU):
                if u >= SLOTS:
                    sp_.wait_ge(pe_made, after("pe", "unit", u - SLOTS))
                sp_.dma_start(raw[:, u % SLOTS, :, :], units[u]).then_inc(raw_landed[u % SLOTS], 16)
            for t in range(TT):
                for hf in range(2):
                    i = 2 * t + hf
                    sp_.wait_ge(act_made if hf == 0 else dve_made, after("act" if hf == 0 else "dve", "otok", i))
                    sp_.dma_start(out[0, t * P:(t + 1) * P, hf * 512:(hf + 1) * 512],
                                  otok[:, t, hf * 512:(hf + 1) * 512]).then_inc(out_stored, 16)
            sp_.wait_ge(out_stored, 16 * 2 * TT)

        @block.tensor
        def _(pe):
            done = [0] * 8
            def acquire(label):
                b, k = use[label]
                assert done[b] == k, label
                if k and known is not None:
                    engine, n = known[("free", by_use[b, k - 1])]
                    pe.wait_ge(act_made if engine == "act" else dve_made, n)

            def finish(label):
                b, k = use[label]
                assert done[b] == k, label
                done[b] += 1
                return pe_made, tick("pe", label)

            def three(dst, wt, x, start, stop):
                nc.tensor.matmul(dst, wt[0], x[0], start=start, stop=False, skip_group_check=True)
                nc.tensor.matmul(dst, wt[0], x[1], start=False, stop=False, skip_group_check=True)
                return nc.tensor.matmul(dst, wt[1], x[0], start=False, stop=stop, skip_group_check=True)

            def unit_w(u, i, n):
                c = slice(n * P, (n + 1) * P)
                return w_hi[:, u % SLOTS, i, c], w_lo[:, u % SLOTS, i, c]

            def project(seg, dest, src, k0=0, first_k=True, last_k=True, ready=None, only=None, tail=2):
                nu = size[seg]
                us = range(nu) if only is None else only
                if not last_k or us[-1] != nu - 1:
                    tail = 0
                for ui in us:
                    if tail and ui >= nu - tail:
                        break
                    u = first[seg] + ui
                    pe.wait_ge(*lo_wait(u))
                    for i in range(2):
                        kt = k0 + 2 * ui + i
                        if ready:
                            ready(kt)
                        for n in range(4):
                            st = first_k and ui == 0 and i == 0 and n % 2 == 0
                            if st:
                                acquire(dest[n // 2])
                            ends = last_k and ui == nu - 1 and i == 1
                            mm = three(bank2(dest[n // 2])[:, n % 2, :], unit_w(u, i, n), src(kt), st, ends)
                            if ends and n == 1:
                                mm.then_inc(*finish(dest[0]))
                    if ends:
                        mm.then_inc(*finish(dest[1]))
                        L.also("pe", "unit", u)
                    else:
                        mm.then_inc(pe_made, tick("pe", "unit", u))
                if tail:
                    u0 = first[seg] + nu - tail
                    for u in range(u0, u0 + tail):
                        pe.wait_ge(*lo_wait(u))
                    kts = 2 * tail
                    if ready:
                        for q in range(kts):
                            ready(k0 + 2 * nu - kts + q)
                    for n in range(4):
                        for q in range(kts):
                            st = first_k and nu == tail and q == 0 and n % 2 == 0
                            if st:
                                acquire(dest[n // 2])
                            mm = three(bank2(dest[n // 2])[:, n % 2, :], unit_w(u0 + q // 2, q % 2, n),
                                       src(k0 + 2 * nu - kts + q), st, q == kts - 1)
                            if n == 3 and q % 2 == 1 and q < kts - 1:
                                mm.then_inc(pe_made, tick("pe", "unit", u0 + q // 2))
                            if n == 1 and q == kts - 1:
                                mm.then_inc(*finish(dest[0]))
                    mm.then_inc(*finish(dest[1]))
                    L.also("pe", "unit", u0 + tail - 1)

            def h_src(kt):
                return h_hi[:, kt, :], h_lo[:, kt, :]

            def transposes(label, parts):
                acquire(label)
                for c, src, k in parts:
                    mm = nc.tensor.transpose(bank(label)[:, c:c + k], src, ident[0:k, 0:k])
                mm.then_inc(*finish(label))

            def token_sums(label, sources):
                acquire(label)
                for i, s_ in enumerate(sources):
                    mm = nc.tensor.matmul(bank(label)[:, i:i + 1], s_, ones[:, 0:1], start=True, stop=True)
                mm.then_inc(*finish(label))

            def rows(label, cols):
                acquire(label)
                for i, c in enumerate(cols):
                    mm = nc.tensor.matmul(bank(label)[:, i * P:(i + 1) * P], c.broadcast_to([P, P]), ident[:, :],
                                          start=True, stop=True)
                mm.then_inc(*finish(label))

            def halves(s_):
                return [s_[:, t * P:(t + 1) * P] for t in range(TT)]

            pe.wait_ge(pool_made, after("pool", "ident"))
            pe.wait_ge(vec_landed, 16 * (3 + len(MISC_ROWS)))
            transposes(("vecs",), [(0, stage[0:96, 0, :], 96), (P, stage[0:MISC_N, 1, :], MISC_N),
                                   (2 * P, stage[:, 2, :], P), (3 * P, stage[0:DWN - P, 3, :], DWN - P)])
            pe.wait_ge(x_landed, 16)
            for i in range(4):
                transposes(("xT", i), [((c * TT + t) * P, xtok[:, t, (2 * i + c) * P:(2 * i + c + 1) * P], P)
                                       for c in range(2) for t in range(TT)])
            pe.wait_ge(pool_made, after("pool", "r0"))
            rows(("R0",), [rfac[:, 0, t:t + 1] for t in range(TT)])

            def h_ready(tag):
                def ready(kt):
                    pe.wait_ge(dve_made, after("dve", "h", tag, kt))
                return ready

            project(("xbc", 0), [("xbc", 0, 0), ("xbc", 0, 1)], h_src, ready=h_ready("in0"), tail=0)
            pe.wait_ge(dve_made, after("dve", "wdtg"))
            acquire(("dt",))
            for j in range(J):
                mm = nc.tensor.matmul(ps[0:HEADS, use[("dt",)][0], 0:T], wdtg[:, j, :], xT[:, j, :],
                                      start=(j == 0), stop=(j == J - 1))
            mm.then_inc(*finish(("dt",)))
            pe.wait_ge(mem_landed, 16)
            for i in range(4):
                transposes(("memT", i), [((c * TT + t) * P, memtok[:, t, (2 * i + c) * P:(2 * i + c + 1) * P], P)
                                         for c in range(2) for t in range(TT)])
            project(("xbc", 1), [("xbc", 1, 0), ("xbc", 1, 1)], h_src)
            pe.wait_ge(act_made, after("act", "dtT"))
            acquire(("dtT",))
            for t in range(TT):
                mm = nc.tensor.matmul(bank(("dtT",))[:, t * HEADS:(t + 1) * HEADS], dtT[0:HEADS, t * P:(t + 1) * P],
                                      ident[0:HEADS, 0:HEADS], start=True, stop=True)
            mm.then_inc(*finish(("dtT",)))
            project(("xbc", 2), [("xbc", 2, 0), ("xbc", 2, 1)], h_src)
            pe.wait_ge(dve_made, after("dve", "dA"))
            acquire(("cs",))
            dt_ = sp[:, 8, :].rearrange("p (t h) -> p t h", t=TT)
            dA = sp[:, 9, :].rearrange("p (t h) -> p t h", t=TT)
            for t in range(TT):
                nc.tensor.matmul(bank(("cs",))[:, t * HEADS:(t + 1) * HEADS], tri[:, :], dA[:, t, :],
                                 start=True, stop=True)
            nc.tensor.matmul(bank(("cs",))[:, 2 * HEADS:3 * HEADS], ones[:, :], dA[:, 0, :],
                             start=True, stop=True).then_inc(*finish(("cs",)))
            project(("z", 0), [("z", 0, 0), ("z", 0, 1)], h_src)
            pe.wait_ge(act_made, after("act", "xc", 3))
            for i in range(4):
                t, q = i // 2, i % 2
                transposes(("xsT", i), [(c * P, xc[:, 4 * q + c, t * P:(t + 1) * P], P) for c in range(4)])
            project(("z", 1), [("z", 1, 0), ("z", 1, 1)], h_src)
            pe.wait_ge(act_made, after("act", "xc", 5))
            for g in range(2):
                acquire(("cb", g))
                nc.tensor.matmul(bank(("cb", g))[:, 0:T], xc[:, 8 + g, 0:P], xc[:, 10 + g, :], start=True, stop=True)
                nc.tensor.matmul(bank(("cb", g))[:, T:T + P], xc[:, 8 + g, P:T], xc[:, 10 + g, P:T],
                                 start=True, stop=True).then_inc(*finish(("cb", g)))
            project(("pool", 0), [("pool", 0, 0), ("pool", 0, 1)], h_src)

            def mem_src(kt):
                return mem_hi[:, kt, :], mem_lo[:, kt, :]

            def y_pair(i):
                for h in (2 * i, 2 * i + 1):
                    yb = ("y", h // 4)
                    if h % 4 == 0:
                        acquire(yb)
                    pe.wait_ge(pool_made, after("pool", "E", h))
                    dst = ps[64 * (h % 2):64 * (h % 2) + 64, use[yb][0], :].rearrange("p (c t) -> p c t", c=2)
                    nc.tensor.matmul(dst[:, i % 2, :], xdt[:, 0, h * 64:(h + 1) * 64], E[:, h % 4, 0:T],
                                     start=True, stop=False, skip_group_check=True)
                    mm = nc.tensor.matmul(dst[:, i % 2, P:T], xdt[:, 1, h * 64:(h + 1) * 64], E[:, h % 4, T:T + P],
                                          start=False, stop=True, skip_group_check=True)
                    if h % 4 == 3:
                        mm.then_inc(*finish(yb))
                        L.also("pe", "head", h)
                    else:
                        mm.then_inc(pe_made, tick("pe", "head", h))

            for i in range(8):
                g = i // 4
                pe.wait_ge(dve_made, after("dve", "mem", 3))
                if i % 4 < 2:
                    project(("K", 0, g), [("K", 0, g, 0), ("K", 0, g, 1)], mem_src, only=[i % 4])
                elif i % 4 == 3:
                    project(("K", 0, g), [("K", 0, g, 0), ("K", 0, g, 1)], mem_src, only=[2, 3])
                if i == 0:
                    pe.wait_ge(dve_made, after("dve", "cs"))
                acquire(("rows", i))
                for hh in range(2):
                    for t in range(TT):
                        mm = nc.tensor.matmul(bank(("rows", i))[:, hh * T + t * P:hh * T + (t + 1) * P],
                                              dA[:, t, 2 * i + hh:2 * i + hh + 1].broadcast_to([P, P]), tri[:, :],
                                              start=True, stop=True)
                mm.then_inc(*finish(("rows", i)))
                if i == 2:
                    pe.wait_ge(dve_made, after("dve", "xdt", 3))
                if i >= 2:
                    y_pair(i - 2)
            y_pair(6)
            y_pair(7)
            pe.wait_ge(ssm_landed, 16 * 6)
            for i in range(2):
                acquire(("pooled", i))
                for c in range(2):
                    g = 2 * i + c
                    pe.wait_ge(pool_made, after("pool", "pdiff", g))
                    mm = nc.tensor.matmul(bank2(("pooled", i))[:, c, :], poolw[:, g, :], pdiff[:, g, :],
                                          start=True, stop=True)
                mm.then_inc(*finish(("pooled", i)))

            def mixer_src(l):
                return lambda kt: mixer_out(l, kt)

            def out_banks(l, g):
                return [("out", l, g, 0), ("out", l, g, 1)]

            def mix_ready(l):
                return lambda kt: pe.wait_ge(dve_made, after("dve", "mix", l, kt))

            def boundary(l, n, filler):
                filler([0, 1])
                pe.wait_ge(dve_made, after("dve", "S2", l, n))
                token_sums(("nstat", l, n), halves(S2))
                filler([2])
                pe.wait_ge(pool_made, after("pool", "nr", l, n))
                rows(("nrow", l, n), [rfac[:, 1 + 3 * l + n, t:t + 1] for t in range(TT)])
                filler([3])

            def v_group(l, g, only):
                seg = ("V", l, g)
                for ui in only:
                    u = first[seg] + ui
                    pe.wait_ge(*lo_wait(u))
                    for i in range(2):
                        kt = 2 * ui + i
                        for t in range(TT):
                            if kt == 0:
                                acquire(seg + (t,))
                            ms = slice(t * P, (t + 1) * P)
                            wh, wl = w_hi[:, u % SLOTS, i, :], w_lo[:, u % SLOTS, i, :]
                            dst = bank(seg + (t,))
                            nc.tensor.matmul(dst, mem_hi[:, kt, ms], wh, start=(kt == 0), stop=False)
                            nc.tensor.matmul(dst, mem_hi[:, kt, ms], wl, start=False, stop=False)
                            mm = nc.tensor.matmul(dst, mem_lo[:, kt, ms], wh, start=False, stop=(kt == J - 1))
                            if kt == J - 1:
                                mm.then_inc(*finish(seg + (t,)))
                    if ui == 3:
                        L.also("pe", "unit", u)
                    else:
                        mm.then_inc(pe_made, tick("pe", "unit", u))

            def scores(l, h):
                acquire(("scores", l, h))
                pe.wait_ge(dve_made, after("dve", "q", l, h))
                pe.wait_ge(dve_made, after("dve", "K", l, h))
                for t in range(TT):
                    for c in range(2):
                        j = 2 * h + c
                        mm = three(bank2(("scores", l, h))[:, t, :],
                                   (q_hi[:, j, t * P:(t + 1) * P], q_lo[:, j, t * P:(t + 1) * P]),
                                   (k_hi[:, j, :], k_lo[:, j, :]), t == 0 and c == 0, c == 1)
                mm.then_inc(*finish(("scores", l, h)))

            def prob_T(l, h):
                pe.wait_ge(dve_made, after("dve", "prob", l, h))
                transposes(("pT", l, h), [((m * TT + t) * P, prob[:, h, t, m * P:(m + 1) * P], P)
                                          for m in range(TT) for t in range(TT)])

            def attend(l, h):
                acquire(("o", l, h))
                pe.wait_ge(dve_made, after("dve", "pT", l, h))
                pe.wait_ge(dve_made, after("dve", "V", l, h // 2, 1))
                for c in range(2):
                    for m in range(TT):
                        col = slice(h * T + c * P, h * T + (c + 1) * P)
                        mm = three(bank2(("o", l, h))[:, c, :], (v_hi[:, m, col], v_lo[:, m, col]),
                                   (pt_hi[:, h, m, :], pt_lo[:, h, m, :]), c == 0 and m == 0, m == 1)
                mm.then_inc(*finish(("o", l, h)))

            def nothing(us):
                pass

            for l in range(2):
                if l == 1:
                    for n, name in enumerate([("gate", 0), ("a", 0), ("gate", 1), ("a", 1), ("cg", 0), ("hh", 0),
                                              ("cg", 1), ("hh", 1), ("bg", 0), ("bg", 1)]):
                        project(name, [name + (0,), name + (1,)], h_src, ready=h_ready("in1") if n == 0 else None,
                                tail=2 if n else 0)
                        if n == 0:
                            pe.wait_ge(pool_made, after("pool", "Sx", "in1"))
                            token_sums(("xstat", 0), halves(S2))
                            pe.wait_ge(pool_made, after("pool", "r1"))
                            rows(("R1",), [rfac[:, 7, t:t + 1] for t in range(TT)])
                    project(("K", 1, 0), [("K", 1, 0, 0), ("K", 1, 0, 1)], mem_src)
                ke, kl = ((0, 4), (8, 0))[l]
                if l == 0:
                    for g in range(2):
                        project(("out", 0, "early", g), out_banks(0, g), mixer_src(0), k0=ke, last_k=False,
                                ready=mix_ready(0) if g == 0 else None)
                    pe.wait_ge(dve_made, after("dve", "Sg", 1))
                    token_sums(("gstat",), halves(Sg[:, 0, :]) + halves(Sg[:, 1, :]))
                    pe.wait_ge(pool_made, after("pool", "gr"))
                    rows(("grow",), [rfac[:, 8, i:i + 1] for i in range(4)])
                else:
                    project(("out", 1, "early", 0), out_banks(1, 0), mixer_src(1), k0=ke, last_k=False,
                            ready=mix_ready(1))
                    acquire(("conv7",))
                    pe.wait_ge(dve_made, after("dve", "v", 3))
                    for k in range(31):
                        pe.wait_ge(act_made, after("act", "diag", k))
                        mm = nc.tensor.matmul(bank(("conv7",))[:, 0:T], diag(k), vpad[:, J - 1, k:k + T],
                                              start=(k == 0), stop=(k == 30))
                        mm.then_inc(*(finish(("conv7",)) if k == 30 else (pe_made, tick("pe", "tap", k))))
                    pe.wait_ge(dve_made, after("dve", "S2", "mu"))
                    token_sums(("mustat",), halves(S2))
                    pe.wait_ge(dve_made, after("dve", "negmu"))
                    rows(("murow",), [rfac[:, 9, t:t + 1] for t in range(TT)])
                    project(("out", 1, "early", 1), out_banks(1, 1), mixer_src(1), k0=ke, last_k=False)
                    pe.wait_ge(dve_made, after("dve", "S2", "var"))
                    token_sums(("varstat",), halves(S2))
                    pe.wait_ge(pool_made, after("pool", "lnr"))
                    rows(("varrow",), [rfac[:, 10, t:t + 1] for t in range(TT)])
                for g in range(2):
                    project(("out", l, "late", g), out_banks(l, g), mixer_src(l), k0=kl, first_k=False,
                            ready=mix_ready(l) if g == 0 else None, tail=2 * g)
                boundary(l, 0, (lambda us: v_group(0, 0, us)) if l == 0 else
                         (lambda us: project(("K", 1, 1), [("K", 1, 1, 0), ("K", 1, 1, 1)], mem_src, only=us, tail=1)))
                project(("q", l, 0), [("q", l, 0, 0), ("q", l, 0, 1)], h_src, ready=h_ready(f"q{l}"), tail=0)
                q1 = [("q", l, 1, 0), ("q", l, 1, 1)]
                project(("q", l, 1), q1, h_src, only=[0])
                pe.wait_ge(pool_made, after("pool", "Sx", f"q{l}"))
                token_sums(("astat", l), halves(S2))
                project(("q", l, 1), q1, h_src, only=[1])
                scores(l, 0)
                scores(l, 1)
                project(("q", l, 1), q1, h_src, only=[2, 3])
                if l == 0:
                    v_group(0, 1, [0, 1])
                scores(l, 2)
                scores(l, 3)
                if l == 0:
                    v_group(0, 1, [2, 3])
                prob_T(l, 0)
                prob_T(l, 1)
                attend(l, 0)
                attend(l, 1)
                prob_T(l, 2)
                prob_T(l, 3)
                attend(l, 2)
                attend(l, 3)
                o_ready = lambda kt: pe.wait_ge(dve_made, after("dve", "o", l, kt // 2))
                for g in range(2):
                    project(("wo", l, g), [("wo", l, g, 0), ("wo", l, g, 1)], h_src, ready=o_ready if g == 0 else None)
                boundary(l, 1, (lambda us: v_group(1, 0, us)) if l == 0 else nothing)

                def w1(h):
                    project(("w1", l, h), [("w1", l, h, 0), ("w1", l, h, 1)], h_src,
                            ready=h_ready(f"mlp{l}") if h == 0 else None, tail=2 if h else 0)

                def w2(h):
                    for g in range(2):
                        project(("w2", l, h, g), [("w2", l, g, 0), ("w2", l, g, 1)],
                                lambda kt: (r_hi[:, h % 2, kt, :], r_lo[:, h % 2, kt, :]),
                                first_k=h == 0, last_k=h == 7,
                                ready=(lambda kt: pe.wait_ge(dve_made, after("dve", "r", l, h, kt // 2))) if g == 0
                                else None)

                w1(0)
                pe.wait_ge(pool_made, after("pool", "Sx", f"mlp{l}"))
                token_sums(("hstat", l), halves(S2))
                w1(1)
                for h in range(8):
                    w2(h)
                    if h < 6:
                        w1(h + 2)
                boundary(l, 2, (lambda us: v_group(1, 1, us)) if l == 0 else nothing)
            for i in range(4):
                t, hf = i // 2, i % 2
                for q in range(4):
                    pe.wait_ge(dve_made, after("dve", "x", "out", 4 * hf + q))
                transposes(("outT", i), [(q * P, xT[:, 4 * hf + q, t * P:(t + 1) * P], P) for q in range(4)])

        @block.scalar
        def _(act):
            nu = [0]

            def round_to(u):
                while nu[0] <= min(u, NU - 1):
                    v = nu[0]
                    act.wait_ge(raw_landed[v % SLOTS], 16 * (v // SLOTS + 1))
                    nc.scalar.activation(w_hi[:, v % SLOTS, :, :], raw[:, v % SLOTS, :, :], ACT.Copy)\
                        .then_inc(hi_ready, 1)
                    nu[0] += 1

            def own():
                act.wait_ge(act_made, now("act"))

            act.dma_start(stage[0:96, 0, :], A["norm_gains"].rearrange("l s (j p) -> (l s j) p", p=P))\
                .then_inc(vec_landed, 16)
            for name, v in MISC_ROWS:
                r0 = misc_at[name] - MISC
                act.dma_start(stage[r0:r0 + v.shape[0], 1, :], v).then_inc(vec_landed, 16)
            act.dma_start(stage[:, 2, :], dw_rows[0:P, :]).then_inc(vec_landed, 16)
            act.dma_start(stage[0:DWN - P, 3, :], dw_rows[P:DWN, :]).then_inc(vec_landed, 16)
            act.dma_start(wdt[:, :, :], A["ab_w_in"][0, :, 3072:3088].rearrange("(j p) h -> p j h", p=P))\
                .then_inc(ssm_landed, 16)
            act.dma_start(dtb[:, :], A["ssm_dt_bias"].broadcast_to([P, HEADS])).then_inc(ssm_landed, 16)
            act.dma_start(expA[:, :], A["ssm_a_log"].broadcast_to([P, HEADS])).then_inc(ssm_landed, 16)
            for hf in range(2):
                act.dma_start(dskip[64 * hf:64 * hf + 64, :],
                              A["ssm_d"].rearrange("a (j two) -> a two j", two=2)[:, hf, :].broadcast_to([64, J]),
                              allow_slow_non_contiguous=True)\
                    .then_inc(ssm_landed, 16)
            act.dma_start(poolw[:, :, :], A["pool_w"][0].rearrange("g i o -> i g o")).then_inc(ssm_landed, 16)
            act.dma_start(memtok[:, :, :], A["mem"][0].rearrange("(t p) d -> p t d", p=P)).then_inc(mem_landed, 16)

            act.wait_ge(x_landed, 16)
            for t in range(TT):
                if t:
                    own()
                nc.scalar.activation(sq[:, :, :].rearrange("p a b -> p (a b)"), xtok[:, t, :], ACT.Square,
                                     accum_out=stat[:, 0, t:t + 1]).then_inc(act_made, tick("act", "ss0", t))
            act.wait_ge(*full(("vecs",)))
            for c, k in ((GAIN, 96), (MISC, MISC_N), (DW, DWN)):
                nc.scalar.activation(vecs[:, c:c + k], bank(("vecs",))[:, c:c + k], ACT.Copy)\
                    .then_inc(act_made, tick("act", *(("vecs",) if c == DW else ())))
            freed("act", ("vecs",))

            def h_part(tag, l, s, j):
                act.wait_ge(dve_made, after("dve", "x", tag, j))
                nc.scalar.activation(h_hi[:, j, :], xT[:, j, :], ACT.Identity, scale=gain(l, s, j))\
                    .then_inc(act_made, tick("act", "h", tag, j))

            for j in range(J):
                h_part("in0", 0, 0, j)
                round_to(j // 2 + 2)
            act.wait_ge(*full(("R0",)))
            nc.scalar.activation(Rrow[:, :], bank(("R0",))[:, 0:T], ACT.Copy).then_inc(act_made, tick("act", "Rrow", 0))
            freed("act", ("R0",))
            act.wait_ge(ssm_landed, 16 * 6)
            nc.scalar.activation(expA[:, :], expA[:, :], ACT.Exp).then_inc(act_made, tick("act", "expA"))

            def silu_pair(i):
                act.wait_ge(dve_made, after("dve", "conv", i))
                nc.scalar.activation(xc[:, 2 * i:2 * i + 2, :], xc[:, 2 * i:2 * i + 2, :], ACT.Silu)\
                    .then_inc(act_made, tick("act", "xc", i))

            F_ = first
            round_to(F_[("xbc", 0)] + 5)
            act.wait_ge(*full(("dt",)))
            nc.scalar.activation(dtT[0:HEADS, :], ps[0:HEADS, use[("dt",)][0], 0:T], ACT.Copy)\
                .then_inc(act_made, tick("act", "dtT"))
            freed("act", ("dt",))
            for i in range(4):
                act.wait_ge(*full(("memT", i)))
                nc.scalar.activation(mem_hi[:, 2 * i:2 * i + 2, :], bank2(("memT", i)), ACT.Copy)\
                    .then_inc(act_made, tick("act", "mem", i))
                round_to(F_[("xbc", 1)] + i + 2)
            for i in range(2):
                silu_pair(i)
                round_to(F_[("xbc", 2)] + 2 * i + 3)
            act.wait_ge(dve_made, after("dve", "spabs"))
            nc.scalar.activation(sp[:, 2, :], sp[:, 1, :], ACT.Exp, scale=-1.0).then_inc(act_made, tick("act", "spexp"))
            act.wait_ge(dve_made, after("dve", "sp1"))
            nc.scalar.activation(sp[:, 4, :], sp[:, 3, :], ACT.Ln).then_inc(act_made, tick("act", "spln"))
            for i in range(2, 4):
                silu_pair(i)
                round_to(F_[("z", 0)] + 2 * (i - 2) + 3)
            for i in range(4, 6):
                silu_pair(i)
                round_to(F_[("z", 1)] + 2 * (i - 4) + 3)
            for i in range(4):
                act.wait_ge(dve_made, after("dve", "z", i))
                nc.scalar.activation(zs[:, 2 * i:2 * i + 2, :], zs[:, 2 * i:2 * i + 2, :], ACT.Silu)\
                    .then_inc(act_made, tick("act", "z", i))
                if i < 2:
                    round_to(F_[("pool", 0)] + 2 * i + 3)
                else:
                    round_to(F_[("K", 0, 0)] + 2 * (i - 2) + 3)

            def hi_of(dst, label, *name, wait=None):
                act.wait_ge(*full(label))
                if wait:
                    act.wait_ge(*wait)
                nc.scalar.activation(dst, bank2(label) if len(dst.shape) == 3 else bank(label), ACT.Copy)\
                    .then_inc(act_made, tick("act", *name))

            def square(i, src, *name):
                if i >= 2:
                    act.wait_ge(*sq_read[0](i - 2))
                nc.scalar.activation(sq[:, i % 2, :].rearrange("p (c t) -> p c t", c=2), src, ACT.Square)\
                    .then_inc(act_made, tick("act", *name))

            sq_read = [None]

            def y_squares(i):
                act.wait_ge(dve_made, after("dve", "yg", i))
                square(i, zs[:, 2 * i:2 * i + 2, :], "ysq", i)

            sq_read[0] = lambda i: (dve_made, after("dve", "Sg", 0))
            for i in range(8):
                for h in (2 * i, 2 * i + 1):
                    act.wait_ge(dve_made, after("dve", "E", h))
                    nc.scalar.activation(E[:, h % 4, :], E[:, h % 4, :], ACT.Exp)\
                        .then_inc(act_made, tick("act", "E", h))
                if i == 4:
                    for q in range(2):
                        hi_of(k_hi[:, 2 * q:2 * q + 2, :], ("K", 0, 0, q), "K", 0, q)
                round_to((F_[("K", 0, 1)] + i if i < 4 else F_[("out", 0, "early", 0)] + i - 4) + 2)
                if i == 5:
                    y_squares(0)
                if i == 7:
                    y_squares(1)
            for q in range(2):
                hi_of(k_hi[:, 4 + 2 * q:6 + 2 * q, :], ("K", 0, 1, q), "K", 0, 2 + q)
            for i in range(2):
                for c in range(2):
                    g = 2 * i + c
                    if c == 0:
                        act.wait_ge(*full(("pooled", i)))
                    nc.scalar.activation(mp_hi[:, g, :], bank2(("pooled", i))[:, c, :], ACT.Identity,
                                         scale=vec("pscale", g)).then_inc(act_made, tick("act", "mp", g))
            y_squares(2)
            y_squares(3)
            act.wait_ge(*full(("grow",)))
            nc.scalar.activation(Rg[:, :, :], bank2(("grow",)), ACT.Copy).then_inc(act_made, tick("act", "Rg"))
            freed("act", ("grow",))
            for c in range(J):
                act.wait_ge(dve_made, after("dve", "yn", c))
                nc.scalar.activation(my_hi[:, c, :], zs[:, c, :], ACT.Copy).then_inc(act_made, tick("act", "mix", 0, 4 + c))
                if c % 2 == 1:
                    round_to(F_[("out", 0, "late", 0)] + c // 2 + 2)


            def attention(l):
                W = F_[("wo", l, 0)]
                end = F_[("q", l, 1)] + 4
                round_to(F_[("q", l, 1)] + 3)
                for h in range(2):
                    hi_of(q_hi[:, 2 * h:2 * h + 2, :], ("q", l, 0, h), "q", l, h)
                round_to(end + 1)

                def exp(h):
                    for t in range(TT):
                        act.wait_ge(dve_made, after("dve", "nmax", l, h))
                        nc.scalar.activation(prob[:, h, t, :], bank2(("scores", l, h))[:, t, :], ACT.Exp,
                                             bias=stat[:, 8 + h, 2 + t:3 + t], scale=rfac[:, 11 + l, 2 + t:3 + t],
                                             accum_out=stat[:, 8 + h, 4 + t:5 + t])\
                            .then_inc(act_made, tick("act", "exp", l, h, t))
                    freed("act", ("scores", l, h))

                exp(0)
                round_to(end + 2)
                exp(1)
                round_to(end + 3)
                for h in range(2, 4):
                    hi_of(q_hi[:, 2 * h:2 * h + 2, :], ("q", l, 1, h - 2), "q", l, h)
                round_to(end + 5)
                if l == 0:
                    round_to(end + 7)
                exp(2)
                exp(3)
                if l == 0:
                    for t in range(TT):
                        hi_of(v_hi[:, t, 512:1024], ("V", 0, 1, t), "V", 0, 1, t)
                    round_to(W + 5)
                hi_of(pt_hi[:, 0, :, :], ("pT", l, 0), "pT", l, 0)
                hi_of(pt_hi[:, 1, :, :], ("pT", l, 1), "pT", l, 1)
                hi_of(h_hi[:, 0:2, :], ("o", l, 0), "o", l, 0)
                hi_of(h_hi[:, 2:4, :], ("o", l, 1), "o", l, 1)
                hi_of(pt_hi[:, 2, :, :], ("pT", l, 2), "pT", l, 2)
                hi_of(pt_hi[:, 3, :, :], ("pT", l, 3), "pT", l, 3)
                hi_of(h_hi[:, 4:6, :], ("o", l, 2), "o", l, 2)
                hi_of(h_hi[:, 6:8, :], ("o", l, 3), "o", l, 3)
                round_to(W + 6)

            def mlp(l):
                for h in range(8):
                    base = F_[("w1", l, h)]
                    round_to(base + 7)
                    for q in range(2):
                        act.wait_ge(*full(("w1", l, h, q)))
                        i = 2 * h + q
                        if i >= 2:
                            act.wait_ge(dve_made, after("dve", "rsq", l, i - 2))
                        nc.scalar.activation(relu[:, q, :], bank(("w1", l, h, q)), ACT.Relu)\
                            .then_inc(act_made, tick("act", "relu", l, i))
                        act.wait_ge(dve_made, after("dve", "rsq", l, i))
                        nc.scalar.activation(r_hi[:, h % 2, 2 * q:2 * q + 2, :],
                                             rsq[:, q, :].rearrange("p (c t) -> p c t", c=2), ACT.Copy)\
                            .then_inc(act_made, tick("act", "r", l, h, q))
                        round_to(base + 6 + q + 2)

            round_to(F_[("V", 0, 0)] + 1)
            for l in range(2):
                m_out = [("out", l, g, q) for g in range(2) for q in range(2)]
                if l == 1:
                    act.wait_ge(*full(("R1",)))
                    nc.scalar.activation(Rrow[:, :], bank(("R1",))[:, 0:T], ACT.Copy)\
                        .then_inc(act_made, tick("act", "Rrow", 1))
                    freed("act", ("R1",))
                    for g in range(2):
                        base = F_[("gate", g)]
                        for q in range(2):
                            act.wait_ge(dve_made, after("dve", "gate", g, q))
                            nc.scalar.activation(sg[:, 2 * q:2 * q + 2, :], sg[:, 2 * q:2 * q + 2, :], ACT.Sigmoid)\
                                .then_inc(act_made, tick("act", "sig", g, q))
                            round_to(base + 4 + 2 * q + 3)
                        round_to(F_[("a", g)] + 9)
                    for g in range(2):
                        for q in range(2):
                            i = 2 * g + q
                            round_to(F_[("bg", g)] + 4 + q + 2)
                            act.wait_ge(dve_made, after("dve", "sc", i))
                            nc.scalar.activation(mh[:, J + 2 * i:J + 2 * i + 2, :],
                                                 sct[:, i % 2, :].rearrange("p (c t) -> p c t", c=2), ACT.Copy)\
                                .then_inc(act_made, tick("act", "mix", 1, J + 2 * i))
                    for g in range(1):
                        round_to(F_[("K", 1, g)] + 8)
                        for q in range(2):
                            hi_of(k_hi[:, 4 * g + 2 * q:4 * g + 2 * q + 2, :], ("K", 1, g, q), "K", 1, 2 * g + q)
                    round_to(F_[("out", 1, "early", 0)] + 3)
                    for k in range(31):
                        if k >= 4:
                            act.wait_ge(pe_made, after("pe", "tap", k - 4))
                        nc.scalar.activation(diag(k), ident[:, :], ACT.Copy, scale=tap(k, J - 1))\
                            .then_inc(act_made, tick("act", "diag", k))
                    round_to(F_[("out", 1, "early", 1)] + 1)
                    act.wait_ge(*full(("conv7",)))
                    nc.scalar.activation(cv[:, J - 1, :], bank(("conv7",))[:, 0:T], ACT.Identity,
                                         bias=vec("dwb", J - 1)).then_inc(act_made, tick("act", "conv7"))
                    freed("act", ("conv7",))
                    round_to(F_[("out", 1, "early", 1)] + 3)
                    act.wait_ge(*full(("murow",)))
                    nc.scalar.activation(Nrow[:, :], bank(("murow",))[:, 0:T], ACT.Copy)\
                        .then_inc(act_made, tick("act", "murow"))
                    freed("act", ("murow",))
                    for i in range(4):
                        act.wait_ge(dve_made, after("dve", "vc", i))
                        if i >= 2:
                            act.wait_ge(dve_made, after("dve", "Sv", 0 if i == 2 else 1))
                        nc.scalar.activation(sq[:, i % 2, :].rearrange("p (c t) -> p c t", c=2),
                                             cv[:, 2 * i:2 * i + 2, :], ACT.Square)\
                            .then_inc(act_made, tick("act", "vsq", i))
                        if i % 2 == 1:
                            round_to(F_[("out", 1, "early", 1)] + 2 + i // 2 + 2)
                    round_to(F_[("out", 1, "late", 0)] + 3)
                    act.wait_ge(*full(("varrow",)))
                    nc.scalar.activation(Rrow[:, :], bank(("varrow",))[:, 0:T], ACT.Copy)\
                        .then_inc(act_made, tick("act", "varrow"))
                    freed("act", ("varrow",))
                    for c in range(J):
                        act.wait_ge(dve_made, after("dve", "vn", c))
                        nc.scalar.activation(cv[:, c, :], cv[:, c, :], ACT.Silu, bias=vec("lnb", c))\
                            .then_inc(act_made, tick("act", "vs", c))
                        own()
                        nc.scalar.activation(mh[:, c, :], cv[:, c, :], ACT.Copy).then_inc(act_made, tick("act", "mix", 1, c))
                        if c % 2 == 1:
                            round_to(F_[("out", 1, "late", 0)] + 1 + c // 2 + 2)
                def new_h(tag, gl, gs, base):
                    for j in range(J):
                        h_part(tag, gl, gs, j)
                        if j % 2 == 1:
                            i = j // 2
                            if i >= 2:
                                act.wait_ge(pool_made, after("pool", "Sx", tag, 0 if i == 2 else 1))
                            nc.scalar.activation(sq[:, i % 2, :].rearrange("p (c t) -> p c t", c=2),
                                                 xT[:, j - 1:j + 1, :], ACT.Square)\
                                .then_inc(act_made, tick("act", "xsq", tag, i))
                            round_to(base + i + 2)

                def boundary(n, m, tag, gl, gs, nxt):
                    fill = FILL.get((l, n))
                    x = nxt - 4 if fill else nxt
                    round_to(x + 2)
                    for i in range(4):
                        act.wait_ge(*full(m[i]))
                        if i >= 2:
                            act.wait_ge(dve_made, after("dve", "Ssum", l, n, 1 if i == 2 else 2))
                        nc.scalar.activation(sq[:, i % 2, :].rearrange("p (c t) -> p c t", c=2), bank2(m[i]),
                                             ACT.Square).then_inc(act_made, tick("act", "nsq", l, n, i))
                        if i == 0:
                            round_to(x + 3)
                    if fill:
                        round_to(nxt + 2)
                    act.wait_ge(*full(("nrow", l, n)))
                    nc.scalar.activation(Nrow[:, :], bank(("nrow", l, n))[:, 0:T], ACT.Copy)\
                        .then_inc(act_made, tick("act", "Nrow", l, n))
                    freed("act", ("nrow", l, n))
                    round_to(nxt + 3)
                    if tag:
                        new_h(tag, gl, gs, nxt)
                    if fill:
                        for q in range(2):
                            hi_of(fill_dst(fill, q)[0], fill + (q,), *fill_name(fill, q))

                boundary(0, m_out, f"q{l}", l, 2, F_[("q", l, 0)])
                attention(l)
                round_to(F_[("wo", l, 1)] + 3)
                boundary(1, [("wo", l, g, q) for g in range(2) for q in range(2)], f"mlp{l}", l, 4, F_[("w1", l, 0)])
                mlp(l)
                round_to(F_[("w2", l, 7, 1)] + 1)
                boundary(2, [("w2", l, g, q) for g in range(2) for q in range(2)],
                         "in1" if l == 0 else None, 1, 0, F_[("gate", 0)] if l == 0 else NU)
            for i in (0, 2):
                act.wait_ge(*full(("outT", i)))
                nc.scalar.activation(otok[:, i // 2, 0:512], bank(("outT", i)), ACT.Copy)\
                    .then_inc(act_made, tick("act", "otok", i))

        @block.vector
        def _(dve):
            V = nc.vector
            nu = [0]

            def low_to(u):
                while nu[0] <= min(u, NU - 1):
                    v = nu[0]
                    if not pool_lo[v]:
                        dve.wait_ge(hi_ready, v + 1)
                        V.tensor_tensor(w_lo[:, v % SLOTS, :, :], raw[:, v % SLOTS, :, :], f(w_hi[:, v % SLOTS, :, :]),
                                        ALU.subtract).then_inc(lo_ready_dve, 1)
                    nu[0] += 1

            def own():
                dve.wait_ge(dve_made, now("dve"))

            F_ = first

            def low_h(tag, l, s, j):
                dve.wait_ge(act_made, after("act", "h", tag, j))
                V.scalar_tensor_tensor(out=h_lo[:, j, :], in0=xT[:, j, :], scalar=gain(l, s, j), in1=f(h_hi[:, j, :]),
                                       op0=ALU.mult, op1=ALU.subtract).then_inc(dve_made, tick("dve", "h", tag, j))

            V.memset(mhalf[:, :], -0.5).then_inc(dve_made, tick("dve", "mhalf"))
            V.memset(upad[:, :, :, 0:3], 0.0).then_inc(dve_made, tick("dve"))
            V.memset(pu[:, :, 0:16], 0.0).then_inc(dve_made, tick("dve", "pads"))
            for t in range(TT):
                dve.wait_ge(act_made, after("act", "ss0", t))
            V.tensor_scalar(stat[:, 1, 0:2], stat[:, 0, 0:2], 1.0 / D, RMS_EPS, ALU.mult, ALU.add)\
                .then_inc(dve_made, tick("dve", "v0"))
            dve.wait_ge(act_made, after("act", "vecs"))
            for i in range(4):
                dve.wait_ge(*full(("xT", i)))
                V.tensor_copy(xT[:, 2 * i:2 * i + 2, :], bank2(("xT", i))).then_inc(dve_made, tick("dve", "xTc", i))
                freed("dve", ("xT", i))
                for c in range(2):
                    L.also("dve", "x", "in0", 2 * i + c)
            for j in range(J):
                low_h("in0", 0, 0, j)
                if j % 2 == 1:
                    low_to(j // 2 + 2)
            dve.wait_ge(ssm_landed, 16 * 6)
            for j in range(J):
                V.tensor_scalar(wdtg[:, j, :], wdt[:, j, :], gain(0, 0, j), None, ALU.mult)\
                    .then_inc(dve_made, tick("dve", *(("wdtg",) if j == J - 1 else ())))

            def scaled(dst, label, row, *name):
                dve.wait_ge(*full(label))
                V.tensor_tensor(dst, bank2(label), row2(row), ALU.mult)\
                    .then_inc(dve_made, tick("dve", *name))
                freed("dve", label)

            def low_of(dst, hi, label, *name):
                dve.wait_ge(act_made, after("act", *name))
                src = bank2(label) if len(dst.shape) == 3 else bank(label)
                V.tensor_tensor(dst, src, f(hi), ALU.subtract).then_inc(dve_made, tick("dve", *name))
                freed("dve", label)

            dve.wait_ge(act_made, after("act", "Rrow", 0))

            def conv4(i):
                for k in range(4):
                    own()
                    for c in range(2):
                        j = 2 * i + c
                        src = upad[:, i % 2, c, k:k + T]
                        if k == 0:
                            V.tensor_scalar(xc[:, j, :], src, vec("convw", k * 12 + j), vec("convb", j),
                                            ALU.mult, ALU.add).then_inc(dve_made, tick("dve"))
                        else:
                            V.scalar_tensor_tensor(out=xc[:, j, :], in0=src, scalar=vec("convw", k * 12 + j),
                                                   in1=xc[:, j, :], op0=ALU.mult, op1=ALU.add)\
                                .then_inc(dve_made, tick("dve", *(("conv", i) if k == 3 and c == 1 else ())))

            low_to(F_[("xbc", 0)] + 5)
            for i in range(2):
                scaled(upad[:, i % 2, :, 3:3 + T], ("xbc", 0, i), Rrow, "u", i)
                low_to(F_[("xbc", 1)] + i + 2)
                conv4(i)
            for i in range(4):
                low_of(mem_lo[:, 2 * i:2 * i + 2, :], mem_hi[:, 2 * i:2 * i + 2, :], ("memT", i), "mem", i)
                if i % 2:
                    low_to(F_[("xbc", 1)] + 2 + i // 2 + 2)
            for i in range(2, 4):
                scaled(upad[:, i % 2, :, 3:3 + T], ("xbc", 1, i - 2), Rrow, "u", i)
                low_to(F_[("xbc", 2)] + 2 * (i - 2) + 2)
                conv4(i)
                low_to(F_[("xbc", 2)] + 2 * (i - 2) + 3)
            dve.wait_ge(*full(("dtT",)))
            for t in range(TT):
                V.scalar_tensor_tensor(out=sp[:, 0, t * HEADS:(t + 1) * HEADS],
                                       in0=bank(("dtT",))[:, t * HEADS:(t + 1) * HEADS], scalar=rfac[:, 0, t:t + 1],
                                       in1=dtb[:, :], op0=ALU.mult, op1=ALU.add).then_inc(dve_made, tick("dve"))
            freed("dve", ("dtT",))
            own()
            V.scalar_tensor_tensor(out=sp[:, 1, :], in0=sp[:, 0, :], scalar=-1.0, in1=sp[:, 0, :],
                                   op0=ALU.mult, op1=ALU.max).then_inc(dve_made, tick("dve", "spabs"))
            dve.wait_ge(act_made, after("act", "spexp"))
            V.tensor_scalar(sp[:, 3, :], sp[:, 2, :], 1.0, None, ALU.add).then_inc(dve_made, tick("dve", "sp1"))
            own()
            V.tensor_scalar(sp[:, 5, :], sp[:, 3, :], -1.0, None, ALU.add).then_inc(dve_made, tick("dve"))
            own()
            V.tensor_scalar(sp[:, 6, :], sp[:, 5, :], 0.0, None, ALU.is_equal).then_inc(dve_made, tick("dve"))
            own()
            V.tensor_tensor(sp[:, 5, :], sp[:, 5, :], sp[:, 6, :], ALU.add).then_inc(dve_made, tick("dve"))
            own()
            V.reciprocal(sp[:, 7, :], sp[:, 5, :]).then_inc(dve_made, tick("dve"))
            dve.wait_ge(act_made, after("act", "spln"))
            V.tensor_tensor(sp[:, 4, :], sp[:, 4, :], sp[:, 6, :], ALU.add).then_inc(dve_made, tick("dve"))
            own()
            V.tensor_tensor(sp[:, 4, :], sp[:, 4, :], sp[:, 7, :], ALU.mult).then_inc(dve_made, tick("dve"))
            own()
            V.tensor_tensor(sp[:, 4, :], sp[:, 4, :], sp[:, 2, :], ALU.mult).then_inc(dve_made, tick("dve"))
            own()
            V.scalar_tensor_tensor(out=sp[:, 8, :], in0=sp[:, 0, :], scalar=0.0, in1=sp[:, 4, :],
                                   op0=ALU.max, op1=ALU.add).then_inc(dve_made, tick("dve", "dt"))
            own()
            dve.wait_ge(act_made, after("act", "expA"))
            dt_ = sp[:, 8, :].rearrange("p (t h) -> p t h", t=TT)
            V.scalar_tensor_tensor(out=sp[:, 9, :].rearrange("p (t h) -> p t h", t=TT), in0=dt_, scalar=-1.0,
                                   in1=expA[:, :].unsqueeze(1).broadcast_to([P, TT, HEADS]),
                                   op0=ALU.mult, op1=ALU.mult).then_inc(dve_made, tick("dve", "dA"))
            low_to(F_[("z", 0)] + 2)
            for i in range(4, 6):
                scaled(upad[:, i % 2, :, 3:3 + T], ("xbc", 2, i - 4), Rrow, "u", i)
                low_to(F_[("z", 0)] + 2 * (i - 4) + 2)
                conv4(i)
                low_to(F_[("z", 0)] + 2 * (i - 4) + 3)
            dve.wait_ge(*full(("cs",)))
            V.tensor_copy(cs[:, 0:3, :], bank(("cs",))[:, 0:3 * HEADS].rearrange("p (a h) -> p a h", a=3))\
                .then_inc(dve_made, tick("dve"))
            freed("dve", ("cs",))
            own()
            V.tensor_tensor(cs[:, 3, :], cs[:, 0, :], cs[:, 2, :], ALU.subtract).then_inc(dve_made, tick("dve", "cs"))
            low_to(F_[("z", 1)] + 2)
            for i in range(2):
                scaled(zs[:, 2 * i:2 * i + 2, :], ("z", 0, i), Rrow, "z", i)
            for i in range(4):
                t, q = i // 2, i % 2
                dve.wait_ge(*full(("xsT", i)))
                V.tensor_tensor(xdt[:, t, q * 512:(q + 1) * 512].rearrange("p (h c) -> p h c", c=64),
                                bank(("xsT", i)).rearrange("p (h c) -> p h c", c=64),
                                dt_[:, t, 8 * q:8 * q + 8].unsqueeze(2).broadcast_to([P, 8, 64]), ALU.mult)\
                    .then_inc(dve_made, tick("dve", "xdt", i))
                freed("dve", ("xsT", i))
                low_to(F_[("z", 1)] + i + 2)
            low_to(F_[("pool", 0)] + 2)
            for i in range(2, 4):
                scaled(zs[:, 2 * i:2 * i + 2, :], ("z", 1, i - 2), Rrow, "z", i)
            low_to(F_[("pool", 0)] + 3)
            dve.wait_ge(pool_made, after("pool", "cbmask"))
            for g in range(2):
                dve.wait_ge(*full(("cb", g)))
                V.tensor_tensor(cbm[:, g, :], bank(("cb", g))[:, 0:3 * P], cbmask[:, :], ALU.mult)\
                    .then_inc(dve_made, tick("dve", "cbm", g))
                freed("dve", ("cb", g))
                low_to(F_[("pool", 0)] + 2 + g + 2)
            low_to(F_[("K", 0, 0)] + 2)
            for i in range(2):
                scaled(pu[:, 2 * i:2 * i + 2, 16:16 + T], ("pool", 0, i), Rrow, "pu", i)
            low_to(F_[("K", 0, 0)] + 3)

            def gate_y(i):
                dve.wait_ge(*full(("y", i)))
                dve.wait_ge(act_made, after("act", "z", i))
                if i:
                    dve.wait_ge(dve_made, after("dve", "yg", i - 1))
                for c in range(2):
                    j = 2 * i + c
                    V.scalar_tensor_tensor(out=tmp[:, c, :], in0=xc[:, j, :], scalar=dskip[:, j:j + 1],
                                           in1=bank2(("y", i))[:, c, :], op0=ALU.mult, op1=ALU.add)\
                        .then_inc(dve_made, tick("dve"))
                freed("dve", ("y", i))
                own()
                V.tensor_tensor(zs[:, 2 * i:2 * i + 2, :], zs[:, 2 * i:2 * i + 2, :], tmp[:, :, :], ALU.mult)\
                    .then_inc(dve_made, tick("dve", "yg", i))

            def group_sum(g):
                dve.wait_ge(act_made, after("act", "ysq", 2 * g + 1))
                V.tensor_tensor(Ssum[:, :], sq[:, 0, :], sq[:, 1, :], ALU.add).then_inc(dve_made, tick("dve"))
                own()
                V.tensor_tensor(Sg[:, g, :], Ssum[:, 0:T], Ssum[:, T:H2], ALU.add)\
                    .then_inc(dve_made, tick("dve", "Sg", g))

            for i in range(8):
                dve.wait_ge(*full(("rows", i)))
                for hh in range(2):
                    h = 2 * i + hh
                    if h >= 4:
                        dve.wait_ge(pe_made, after("pe", "head", h - 4))
                    r = bank2(("rows", i))[:, hh, :]
                    for dst, src, c in ((0, 0, 0), (P, P, 3), (2 * P, P, 1)):
                        V.tensor_scalar(E[:, h % 4, dst:dst + P], r[:, src:src + P], cs[:, c, h:h + 1], 0.0,
                                        ALU.subtract, ALU.min)\
                            .then_inc(dve_made, tick("dve", *(("E", h) if dst == 2 * P else ())))
                freed("dve", ("rows", i))
                low_to(F_[("K", 0, 0)] + 2 + i + 2)
                if i == 4:
                    for q in range(2):
                        low_of(k_lo[:, 2 * q:2 * q + 2, :], k_hi[:, 2 * q:2 * q + 2, :], ("K", 0, 0, q), "K", 0, q)
                if i == 5:
                    gate_y(0)
                if i == 7:
                    gate_y(1)
                    group_sum(0)
            low_to(F_[("out", 0, "early", 0)] + 4)
            for q in range(2):
                low_of(k_lo[:, 4 + 2 * q:6 + 2 * q, :], k_hi[:, 4 + 2 * q:6 + 2 * q, :], ("K", 0, 1, q), "K", 0, 2 + q)
            for g in range(4):
                dve.wait_ge(act_made, after("act", "mp", g | 1))
                V.scalar_tensor_tensor(out=mp_lo[:, g, :], in0=bank2(("pooled", g // 2))[:, g % 2, :],
                                       scalar=vec("pscale", g), in1=f(mp_hi[:, g, :]), op0=ALU.mult,
                                       op1=ALU.subtract).then_inc(dve_made, tick("dve", "mix", 0, g))
                if g % 2 == 1:
                    freed("dve", ("pooled", g // 2))
            gate_y(2)
            gate_y(3)
            group_sum(1)
            low_to(F_[("out", 0, "early", 1)] + 3)
            dve.wait_ge(*full(("gstat",)))
            V.tensor_scalar(stat[:, 8, 0:4], bank(("gstat",))[:, 0:4], 2.0 / D, RMS_EPS, ALU.mult, ALU.add)\
                .then_inc(dve_made, tick("dve", "gv"))
            freed("dve", ("gstat",))
            dve.wait_ge(act_made, after("act", "Rg"))
            for c in range(J):
                V.scalar_tensor_tensor(out=zs[:, c, :], in0=zs[:, c, :], scalar=vec("ssmn", c), in1=Rg[:, c // 4, :],
                                       op0=ALU.mult, op1=ALU.mult).then_inc(dve_made, tick("dve", "yn", c))
                if c >= 1:
                    dve.wait_ge(act_made, after("act", "mix", 0, 4 + c - 1))
                    V.tensor_tensor(my_lo[:, c - 1, :], zs[:, c - 1, :], f(my_hi[:, c - 1, :]), ALU.subtract)\
                        .then_inc(dve_made, tick("dve", "mix", 0, 4 + c - 1))
                if c % 2 == 1:
                    low_to(F_[("out", 0, "late", 0)] + c // 2 + 2)
            dve.wait_ge(act_made, after("act", "mix", 0, 4 + J - 1))
            V.tensor_tensor(my_lo[:, J - 1, :], zs[:, J - 1, :], f(my_hi[:, J - 1, :]), ALU.subtract)\
                .then_inc(dve_made, tick("dve", "mix", 0, 4 + J - 1))

            def norm_sum(l, n, m):
                dve.wait_ge(act_made, after("act", "nsq", l, n, 1))
                V.tensor_tensor(Ssum[:, :], sq[:, 0, :], sq[:, 1, :], ALU.add)\
                    .then_inc(dve_made, tick("dve", "Ssum", l, n, 1))
                L.also("dve", "Ssum", l, n, 2)
                for i in (2, 3):
                    dve.wait_ge(act_made, after("act", "nsq", l, n, i))
                    own()
                    V.tensor_tensor(Ssum[:, :], Ssum[:, :], sq[:, i % 2, :], ALU.add).then_inc(dve_made, tick("dve"))
                own()
                V.tensor_tensor(S2[:, :], Ssum[:, 0:T], Ssum[:, T:H2], ALU.add).then_inc(dve_made, tick("dve", "S2", l, n))

            def factor(l, n):
                dve.wait_ge(*full(("nstat", l, n)))
                s_ = 1 + 3 * l + n
                if n < 2:
                    V.tensor_scalar(stat[:, s_, 0:2], bank(("nstat", l, n))[:, 0:2], 1.0 / D, RMS_EPS,
                                    ALU.mult, ALU.add).then_inc(dve_made, tick("dve", "nv", l, n))
                else:
                    dve.wait_ge(pool_made, after("pool", "r4", l))
                    V.tensor_scalar(stat[:, s_, 2:4], bank(("nstat", l, n))[:, 0:2], 1.0 / D, None, ALU.mult)\
                        .then_inc(dve_made, tick("dve"))
                    own()
                    V.tensor_tensor(stat[:, s_, 4:6], stat[:, s_, 2:4], rfac[:, 13 + l, 4:6], ALU.mult)\
                        .then_inc(dve_made, tick("dve"))
                    own()
                    V.tensor_scalar(stat[:, s_, 0:2], stat[:, s_, 4:6], RMS_EPS, None, ALU.add)\
                        .then_inc(dve_made, tick("dve", "nv", l, n))
                freed("dve", ("nstat", l, n))

            def new_x(l, n, m, tag, gl, gs):
                dve.wait_ge(act_made, after("act", "Nrow", l, n))
                for j in range(J + 2):
                    if j < J:
                        if j >= 2:
                            dve.wait_ge(dve_made, after("dve", "x", tag or "out", j - 2))
                        V.scalar_tensor_tensor(out=tmp[:, j % 2, :], in0=bank2(m[j // 2])[:, j % 2, :],
                                               scalar=gain(l, 2 * n + 1, j), in1=Nrow[:, :], op0=ALU.mult,
                                               op1=ALU.mult).then_inc(dve_made, tick("dve", "dx", l, n, j))
                        if j % 2 == 1:
                            freed("dve", m[j // 2])
                    if 1 <= j <= J:
                        dve.wait_ge(dve_made, after("dve", "dx", l, n, j - 1))
                        V.tensor_tensor(xT[:, j - 1, :], xT[:, j - 1, :], tmp[:, (j - 1) % 2, :], ALU.add)\
                            .then_inc(dve_made, tick("dve", "x", tag or "out", j - 1))
                    if tag and j >= 2:
                        low_h(tag, gl, gs, j - 2)

            def boundary(l, n, m, tag, gl, gs, nxt):
                fill = FILL.get((l, n))
                x = nxt - 4 if fill else nxt
                low_to(x + 1 if fill else x)
                norm_sum(l, n, m)
                if fill:
                    low_to(nxt - 1)
                factor(l, n)
                low_to(nxt + 2)
                new_x(l, n, m, tag, gl, gs)
                if tag:
                    low_to(nxt + 4)
                if fill:
                    for q in range(2):
                        hi, lo = fill_dst(fill, q)
                        low_of(lo, hi, fill + (q,), *fill_name(fill, q))

            def x_factor(label, s_, *name):
                dve.wait_ge(*full(label))
                V.tensor_scalar(stat[:, s_, 0:2], bank(label)[:, 0:2], 1.0 / D, RMS_EPS, ALU.mult, ALU.add)\
                    .then_inc(dve_made, tick("dve", *name))
                freed("dve", label)

            cur = [0]

            def conv31(n):
                for _ in range(n):
                    if cur[0] >= 31 * J:
                        return
                    if cur[0] >= 186 and cur[0] % 2:
                        cur[0] += 1
                        continue
                    i, k, c = cur[0] // 62, cur[0] % 62 // 2, cur[0] % 2
                    j = 2 * i + c
                    acc = ps[:, 6, c * T:(c + 1) * T]
                    src = vpad[:, j, k:k + T]
                    if k == 0:
                        dve.wait_ge(dve_made, after("dve", "v", i))
                        if i:
                            dve.wait_ge(dve_made, L.at[("dve", "tap", cur[0] - 2)])
                        V.tensor_scalar(acc, src, tap(k, j), vec("dwb", j), ALU.mult, ALU.add)\
                            .then_inc(dve_made, tick("dve", "tap", cur[0]))
                    else:
                        dve.wait_ge(dve_made, L.at[("dve", "tap", cur[0] - 2)])
                        V.scalar_tensor_tensor(out=acc if k < 30 else cv[:, j, :], in0=src, scalar=tap(k, j), in1=acc,
                                               op0=ALU.mult, op1=ALU.add)\
                            .then_inc(dve_made, tick("dve", "tap", cur[0]))
                    cur[0] += 1
                    if cur[0] in (124, 186):
                        own()
                        i = cur[0] // 62
                        V.tensor_tensor(Ssum[:, :].rearrange("p (c t) -> p c t", c=2),
                                        cv[:, 0:2, :] if i == 2 else Ssum[:, :].rearrange("p (c t) -> p c t", c=2),
                                        cv[:, 2 * i - 2:2 * i, :], ALU.add).then_inc(dve_made, tick("dve"))

            def attention(l):
                end = F_[("q", l, 1)] + 4
                low_to(F_[("q", l, 1)] + 3)
                for h in range(2):
                    low_of(q_lo[:, 2 * h:2 * h + 2, :], q_hi[:, 2 * h:2 * h + 2, :], ("q", l, 0, h), "q", l, h)
                x_factor(("astat", l), 7, "av", l)
                dve.wait_ge(pool_made, after("pool", "ar", l))
                V.tensor_scalar(rfac[:, 11 + l, 2:4], rfac[:, 11 + l, 0:2], XA_SCALE, None, ALU.mult)\
                    .then_inc(dve_made, tick("dve"))
                V.tensor_scalar(rfac[:, 11 + l, 4:6], rfac[:, 11 + l, 0:2], -XA_SCALE, None, ALU.mult)\
                    .then_inc(dve_made, tick("dve"))
                low_to(end + 1)

                def maxes(h):
                    dve.wait_ge(*full(("scores", l, h)))
                    V.tensor_reduce(stat[:, 8 + h, 0:2], bank2(("scores", l, h)), AX.X, ALU.max)\
                        .then_inc(dve_made, tick("dve"))
                    own()
                    V.tensor_tensor(stat[:, 8 + h, 2:4], stat[:, 8 + h, 0:2], rfac[:, 11 + l, 4:6], ALU.mult)\
                        .then_inc(dve_made, tick("dve", "nmax", l, h))

                def probs(h):
                    for t in range(TT):
                        dve.wait_ge(act_made, after("act", "exp", l, h, t))
                    V.reciprocal(stat[:, 8 + h, 6:8], stat[:, 8 + h, 4:6]).then_inc(dve_made, tick("dve"))
                    own()
                    for t in range(TT):
                        V.tensor_scalar(prob[:, h, t, :], prob[:, h, t, :], stat[:, 8 + h, 6 + t:7 + t], None, ALU.mult)\
                            .then_inc(dve_made, tick("dve", *(("prob", l, h) if t == TT - 1 else ())))

                def low_o(h):
                    low_of(h_lo[:, 2 * h:2 * h + 2, :], h_hi[:, 2 * h:2 * h + 2, :], ("o", l, h), "o", l, h)

                def low_pt(h):
                    low_of(pt_lo[:, h, :, :], pt_hi[:, h, :, :], ("pT", l, h), "pT", l, h)

                maxes(0)
                maxes(1)
                low_to(end + 2)
                probs(0)
                low_to(end + 3)
                probs(1)
                for h in range(2, 4):
                    low_of(q_lo[:, 2 * h:2 * h + 2, :], q_hi[:, 2 * h:2 * h + 2, :], ("q", l, 1, h - 2), "q", l, h)
                low_to(end + 5)
                if l == 0:
                    low_to(end + 7)
                maxes(2)
                maxes(3)
                probs(2)
                probs(3)
                if l == 0:
                    for t in range(TT):
                        low_of(v_lo[:, t, 512:1024], v_hi[:, t, 512:1024], ("V", 0, 1, t), "V", 0, 1, t)
                low_pt(0)
                low_pt(1)
                low_to(F_[("wo", l, 0)] + 5)
                low_o(0)
                low_o(1)
                low_pt(2)
                low_pt(3)
                low_o(2)
                low_o(3)

            def mlp(l):
                for h in range(8):
                    base = F_[("w1", l, h)]
                    low_to(base + 7)
                    for q in range(2):
                        i = 2 * h + q
                        dve.wait_ge(act_made, after("act", "relu", l, i))
                        if i >= 2:
                            dve.wait_ge(dve_made, after("dve", "r", l, h - 1, q))
                        V.scalar_tensor_tensor(out=rsq[:, q, :], in0=bank(("w1", l, h, q)), scalar=0.0,
                                               in1=relu[:, q, :], op0=ALU.max, op1=ALU.mult)\
                            .then_inc(dve_made, tick("dve", "rsq", l, i))
                        freed("dve", ("w1", l, h, q))
                        if q == 1:
                            low_r(l, h, 0)
                    low_r(l, h, 1)
                    if h == 0:
                        x_factor(("hstat", l), 15, "hv", l)
                    low_to(base + 9)

            def low_r(l, h, q):
                dve.wait_ge(act_made, after("act", "r", l, h, q))
                V.tensor_tensor(r_lo[:, h % 2, 2 * q:2 * q + 2, :], rsq[:, q, :].rearrange("p (c t) -> p c t", c=2),
                                f(r_hi[:, h % 2, 2 * q:2 * q + 2, :]), ALU.subtract)\
                    .then_inc(dve_made, tick("dve", "r", l, h, q))

            for l in range(2):
                if l == 1:
                    x_factor(("xstat", 0), 7, "r1v")
                    dve.wait_ge(act_made, after("act", "Rrow", 1))
                    V.tensor_tensor(Rsq[:, :], Rrow[:, :], Rrow[:, :], ALU.mult).then_inc(dve_made, tick("dve", "Rsq"))
                    V.memset(vpad[:, :, 0:30], 0.0).then_inc(dve_made, tick("dve"))
                    V.memset(ppad[:, :, :, 0:2], 0.0).then_inc(dve_made, tick("dve"))
                    own()
                    for g in range(2):
                        for q in range(2):
                            scaled(sg[:, 2 * q:2 * q + 2, :], ("gate", g, q), Rrow, "gate", g, q)
                            low_to(F_[("gate", g)] + 4 + 2 * q + 2)
                            if g == 1:
                                conv31(8)
                            low_to(F_[("gate", g)] + 4 + 2 * q + 3)
                            if g == 1:
                                conv31(8)
                        for q in range(2):
                            i = 2 * g + q
                            dve.wait_ge(pool_made, after("pool", "sg", g, q))
                            dve.wait_ge(*full(("a", g, q)))
                            V.tensor_tensor(vpad[:, 2 * i:2 * i + 2, 30:30 + T], bank2(("a", g, q)),
                                            sg[:, 2 * q:2 * q + 2, :], ALU.mult).then_inc(dve_made, tick("dve", "v", i))
                            freed("dve", ("a", g, q))
                            low_to(F_[("a", g)] + 4 + 2 * q + 2)
                            conv31(6)
                            low_to(F_[("a", g)] + 4 + 2 * q + 3)
                            conv31(6)
                    for g in range(2):
                        for q in range(2):
                            scaled(sg[:, 2 * q:2 * q + 2, :], ("cg", g, q), Rsq, "cg", g, q)
                            conv31(8)
                            low_to(F_[("cg", g)] + 4 + 2 * q + 3)
                        for q in range(2):
                            i = 2 * g + q
                            own()
                            dve.wait_ge(*full(("hh", g, q)))
                            V.tensor_tensor(ppad[:, i % 2, :, 2:2 + T], bank2(("hh", g, q)),
                                            sg[:, 2 * q:2 * q + 2, :], ALU.mult).then_inc(dve_made, tick("dve"))
                            freed("dve", ("hh", g, q))
                            for k in range(3):
                                own()
                                for c in range(2):
                                    j = 2 * i + c
                                    src = ppad[:, i % 2, c, k:k + T]
                                    if k == 0:
                                        V.tensor_scalar(cv3[:, j, :], src, vec("scw", k * J + j), None, ALU.mult)\
                                            .then_inc(dve_made, tick("dve"))
                                    else:
                                        V.scalar_tensor_tensor(out=cv3[:, j, :], in0=src, scalar=vec("scw", k * J + j),
                                                               in1=cv3[:, j, :], op0=ALU.mult, op1=ALU.add)\
                                            .then_inc(dve_made, tick("dve", *(("cv3", i) if k == 2 and c == 1 else ())))
                            low_to(F_[("hh", g)] + 4 + 2 * q + 2)
                            conv31(5)
                            low_to(F_[("hh", g)] + 4 + 2 * q + 3)
                    for g in range(2):
                        for q in range(2):
                            i = 2 * g + q
                            dve.wait_ge(*full(("bg", g, q)))
                            dve.wait_ge(pool_made, after("pool", "cv3R", i))
                            if i >= 2:
                                dve.wait_ge(act_made, after("act", "mix", 1, J + 2 * (i - 2)))
                            V.tensor_tensor(sct[:, i % 2, :].rearrange("p (c t) -> p c t", c=2), bank2(("bg", g, q)),
                                            cv3[:, 2 * i:2 * i + 2, :], ALU.mult).then_inc(dve_made, tick("dve", "sc", i))
                            freed("dve", ("bg", g, q))
                            conv31(5)
                            dve.wait_ge(act_made, after("act", "mix", 1, J + 2 * i))
                            V.tensor_tensor(ml[:, J + 2 * i:J + 2 * i + 2, :],
                                            sct[:, i % 2, :].rearrange("p (c t) -> p c t", c=2),
                                            f(mh[:, J + 2 * i:J + 2 * i + 2, :]), ALU.subtract)\
                                .then_inc(dve_made, tick("dve", "mix", 1, J + 2 * i))
                            L.at[("dve", "mix", 1, J + 2 * i + 1)] = L.at[("dve", "mix", 1, J + 2 * i)]
                            conv31(4)
                            low_to(F_[("bg", g)] + 4 + 2 * q + 3)
                    for g in range(1):
                        for q in range(2):
                            low_of(k_lo[:, 4 * g + 2 * q:4 * g + 2 * q + 2, :], k_hi[:, 4 * g + 2 * q:4 * g + 2 * q + 2, :],
                                   ("K", 1, g, q), "K", 1, 2 * g + q)
                            conv31(12)
                            low_to(F_[("K", 1, g)] + 4 + 2 * q + 3)
                    conv31(31 * J)
                    own()
                    dve.wait_ge(act_made, after("act", "conv7"))
                    V.tensor_tensor(Ssum[:, :].rearrange("p (c t) -> p c t", c=2),
                                    Ssum[:, :].rearrange("p (c t) -> p c t", c=2), cv[:, 6:8, :], ALU.add)\
                        .then_inc(dve_made, tick("dve"))
                    own()
                    V.tensor_tensor(S2[:, :], Ssum[:, 0:T], Ssum[:, T:H2], ALU.add).then_inc(dve_made, tick("dve", "S2", "mu"))
                    low_to(F_[("out", 1, "early", 1)] + 2)
                    dve.wait_ge(*full(("mustat",)))
                    V.tensor_scalar(rfac[:, 9, 0:2], bank(("mustat",))[:, 0:2], 1.0 / D, None, ALU.mult)\
                        .then_inc(dve_made, tick("dve", "negmu"))
                    freed("dve", ("mustat",))
                    low_to(F_[("out", 1, "early", 1)] + 3)
                    dve.wait_ge(act_made, after("act", "murow"))
                    for i in range(4):
                        V.tensor_tensor(cv[:, 2 * i:2 * i + 2, :], cv[:, 2 * i:2 * i + 2, :], row2(Nrow), ALU.subtract)\
                            .then_inc(dve_made, tick("dve", "vc", i))
                    dve.wait_ge(act_made, after("act", "vsq", 1))
                    V.tensor_tensor(Ssum[:, :], sq[:, 0, :], sq[:, 1, :], ALU.add).then_inc(dve_made, tick("dve", "Sv", 0))
                    L.also("dve", "Sv", 1)
                    low_to(F_[("out", 1, "early", 1)] + 4)
                    for i in (2, 3):
                        dve.wait_ge(act_made, after("act", "vsq", i))
                        own()
                        V.tensor_tensor(Ssum[:, :], Ssum[:, :], sq[:, i % 2, :], ALU.add).then_inc(dve_made, tick("dve"))
                    own()
                    V.tensor_tensor(S2[:, :], Ssum[:, 0:T], Ssum[:, T:H2], ALU.add)\
                        .then_inc(dve_made, tick("dve", "S2", "var"))
                    low_to(F_[("out", 1, "late", 0)] + 2)
                    dve.wait_ge(*full(("varstat",)))
                    V.tensor_scalar(stat[:, 9, 0:2], bank(("varstat",))[:, 0:2], 1.0 / D, LN_EPS, ALU.mult, ALU.add)\
                        .then_inc(dve_made, tick("dve", "lnv"))
                    freed("dve", ("varstat",))
                    low_to(F_[("out", 1, "late", 0)] + 3)
                    dve.wait_ge(act_made, after("act", "varrow"))
                    for c in range(J + 1):
                        if c < J:
                            V.scalar_tensor_tensor(out=cv[:, c, :], in0=cv[:, c, :], scalar=vec("lng", c), in1=Rrow[:, :],
                                                   op0=ALU.mult, op1=ALU.mult).then_inc(dve_made, tick("dve", "vn", c))
                        if c >= 1:
                            dve.wait_ge(act_made, after("act", "mix", 1, c - 1))
                            V.tensor_tensor(ml[:, c - 1, :], cv[:, c - 1, :], f(mh[:, c - 1, :]), ALU.subtract)\
                                .then_inc(dve_made, tick("dve", "mix", 1, c - 1))
                        if c % 2 == 1:
                            low_to(F_[("out", 1, "late", 0)] + 1 + c // 2 + 2)
                m = [("out", l, g, q) for g in range(2) for q in range(2)]
                boundary(l, 0, m, f"q{l}", l, 2, F_[("q", l, 0)])
                attention(l)
                boundary(l, 1, [("wo", l, g, q) for g in range(2) for q in range(2)], f"mlp{l}", l, 4,
                         F_[("w1", l, 0)])
                mlp(l)
                boundary(l, 2, [("w2", l, g, q) for g in range(2) for q in range(2)],
                         "in1" if l == 0 else None, 1, 0, F_[("gate", 0)] if l == 0 else NU)
            for i in (1, 3):
                dve.wait_ge(*full(("outT", i)))
                V.tensor_copy(otok[:, i // 2, 512:1024], bank(("outT", i))).then_inc(dve_made, tick("dve", "otok", i))

        @block.gpsimd
        def _(pool):
            G = nc.gpsimd
            nu = [0]

            def low_to(u):
                while nu[0] <= min(u, NU - 1):
                    v = nu[0]
                    if pool_lo[v]:
                        pool.wait_ge(hi_ready, v + 1)
                        G.tensor_tensor(w_lo[:, v % SLOTS, :, :], raw[:, v % SLOTS, :, :], f(w_hi[:, v % SLOTS, :, :]),
                                        ALU.subtract).then_inc(lo_ready_pool, 1)
                    nu[0] += 1

            def own():
                pool.wait_ge(pool_made, now("pool"))

            F_ = first
            G.memset(ident[:, :], 0.0).then_inc(pool_made, tick("pool"))
            G.memset(ones[:, :], 1.0).then_inc(pool_made, tick("pool"))
            own()
            G.affine_select(out=ident[:, :], in_=ident[:, :], compare_op=ALU.not_equal, fill=1.0, base=0,
                            pattern=[[-1, P]], channel_multiplier=1).then_inc(pool_made, tick("pool", "ident"))
            G.affine_select(out=tri[:, :], in_=ones[:, :], compare_op=ALU.is_ge, fill=0.0, base=0,
                            pattern=[[1, P]], channel_multiplier=-1).then_inc(pool_made, tick("pool"))
            own()
            G.tensor_copy(cbmask[:, 0:P], tri[:, :]).then_inc(pool_made, tick("pool"))
            G.memset(cbmask[:, P:2 * P], 1.0).then_inc(pool_made, tick("pool"))
            G.tensor_copy(cbmask[:, 2 * P:3 * P], tri[:, :]).then_inc(pool_made, tick("pool", "cbmask"))
            pool.wait_ge(dve_made, after("dve", "mhalf"))

            def rsqrt(dst, src, *name):
                G.tensor_tensor(dst, src, mhalf[:, 0:dst.shape[1]], ALU.pow).then_inc(pool_made, tick("pool", *name))

            pool.wait_ge(dve_made, after("dve", "v0"))
            rsqrt(rfac[:, 0, 0:2], stat[:, 1, 0:2], "r0")
            for g, w in enumerate(POOL_WINDOWS):
                G.memset(icnt[:, g, :], 1.0 / w).then_inc(pool_made, tick("pool"))
                own()
                for c in range(w - 1):
                    G.memset(icnt[:, g, c:c + 1], 1.0 / (c + 1)).then_inc(pool_made, tick("pool"))
            low_to(F_[("pool", 0)] + 5)

            def heads(i):
                for h in (2 * i, 2 * i + 1):
                    pool.wait_ge(act_made, after("act", "E", h))
                    if h == 0:
                        pool.wait_ge(dve_made, after("dve", "cbm", 1))
                    G.tensor_tensor(E[:, h % 4, :], E[:, h % 4, :], cbm[:, h // 8, :], ALU.mult)\
                        .then_inc(pool_made, tick("pool", "E", h))

            def window(g):
                w = POOL_WINDOWS[g]
                pool.wait_ge(dve_made, after("dve", "pu", g // 2))
                src, step, k = pu[:, g, :], 1, 0
                N = T + 16
                bufs = (pw1, pw2)
                while step < w:
                    dst = bufs[k % 2]
                    own()
                    G.tensor_tensor(dst[:, step:N], src[:, step:N], src[:, 0:N - step], ALU.add)\
                        .then_inc(pool_made, tick("pool"))
                    G.memset(dst[:, 0:step], 0.0).then_inc(pool_made, tick("pool"))
                    src, step, k = dst[:, :], step * 2, k + 1
                own()
                dst = bufs[k % 2]
                G.tensor_scalar(dst[:, 32:N], src[:, 32:N], 1.0 / w, None, ALU.mult).then_inc(pool_made, tick("pool"))
                G.tensor_tensor(dst[:, 16:32], src[:, 16:32], icnt[:, g, :], ALU.mult).then_inc(pool_made, tick("pool"))
                own()
                G.tensor_tensor(pdiff[:, g, :], dst[:, 16:N], pu[:, g, 16:N], ALU.subtract)\
                    .then_inc(pool_made, tick("pool", "pdiff", g))

            for i in range(8):
                low_to(F_[("K", 0, 0)] + i + 2)
                heads(i)
                if i >= 4:
                    window(i - 4)
            low_to(F_[("out", 0, "early", 1)] + 3)
            pool.wait_ge(dve_made, after("dve", "gv"))
            rsqrt(rfac[:, 8, 0:4], stat[:, 8, 0:4], "gr")
            low_to(F_[("V", 0, 0)] - 1)

            def x_sums(tag):
                pool.wait_ge(act_made, after("act", "xsq", tag, 1))
                G.tensor_tensor(Ssum[:, :], sq[:, 0, :], sq[:, 1, :], ALU.add).then_inc(pool_made, tick("pool", "Sx", tag, 0))
                L.also("pool", "Sx", tag, 1)
                for i in (2, 3):
                    pool.wait_ge(act_made, after("act", "xsq", tag, i))
                    own()
                    G.tensor_tensor(Ssum[:, :], Ssum[:, :], sq[:, i % 2, :], ALU.add).then_inc(pool_made, tick("pool"))
                own()
                G.tensor_tensor(S2[:, :], Ssum[:, 0:T], Ssum[:, T:H2], ALU.add).then_inc(pool_made, tick("pool", "Sx", tag))

            for l in range(2):
                if l == 1:
                    pool.wait_ge(dve_made, after("dve", "r1v"))
                    rsqrt(rfac[:, 7, 0:2], stat[:, 7, 0:2], "r1")
                    pool.wait_ge(act_made, after("act", "Rrow", 1))
                    for g in range(2):
                        for q in range(2):
                            low_to(F_[("gate", g)] + 4 + 2 * q + 1)
                            pool.wait_ge(act_made, after("act", "sig", g, q))
                            G.tensor_tensor(sg[:, 2 * q:2 * q + 2, :], sg[:, 2 * q:2 * q + 2, :], row2(Rrow), ALU.mult)\
                                .then_inc(pool_made, tick("pool", "sg", g, q))
                            low_to(F_[("gate", g)] + 4 + 2 * q + 3)
                        low_to(F_[("a", g)] + 9)
                    for g in range(2):
                        for q in range(2):
                            i = 2 * g + q
                            low_to(F_[("hh", g)] + 3 + 2 * q + 2)
                            pool.wait_ge(dve_made, after("dve", "cv3", i))
                            G.tensor_tensor(cv3[:, 2 * i:2 * i + 2, :], cv3[:, 2 * i:2 * i + 2, :], row2(Rrow), ALU.mult)\
                                .then_inc(pool_made, tick("pool", "cv3R", i))
                    low_to(F_[("out", 1, "early", 1)] + 5)
                    pool.wait_ge(dve_made, after("dve", "lnv"))
                    rsqrt(rfac[:, 10, 0:2], stat[:, 9, 0:2], "lnr")
                    low_to(F_[("K", 1, 1)] - 1)
                pool.wait_ge(dve_made, after("dve", "nv", l, 0))
                rsqrt(rfac[:, 1 + 3 * l, 0:2], stat[:, 1 + 3 * l, 0:2], "nr", l, 0)
                low_to(F_[("q", l, 0)] + 3)
                x_sums(f"q{l}")
                pool.wait_ge(dve_made, after("dve", "av", l))
                rsqrt(rfac[:, 11 + l, 0:2], stat[:, 7, 0:2], "ar", l)
                low_to(F_[("wo", l, 0)] + 7)
                if (l, 1) not in FILL:
                    low_to(F_[("w1", l, 0)] + 1)
                pool.wait_ge(dve_made, after("dve", "nv", l, 1))
                rsqrt(rfac[:, 2 + 3 * l, 0:2], stat[:, 2 + 3 * l, 0:2], "nr", l, 1)
                low_to(F_[("w1", l, 0)] + 3)
                x_sums(f"mlp{l}")
                pool.wait_ge(dve_made, after("dve", "hv", l))
                rsqrt(rfac[:, 13 + l, 0:2], stat[:, 15, 0:2])
                own()
                G.tensor_tensor(rfac[:, 13 + l, 2:4], rfac[:, 13 + l, 0:2], rfac[:, 13 + l, 0:2], ALU.mult)\
                    .then_inc(pool_made, tick("pool"))
                own()
                G.tensor_tensor(rfac[:, 13 + l, 4:6], rfac[:, 13 + l, 2:4], rfac[:, 13 + l, 2:4], ALU.mult)\
                    .then_inc(pool_made, tick("pool", "r4", l))
                pool.wait_ge(dve_made, after("dve", "nv", l, 2))
                s_ = 3 + 3 * l
                rsqrt(rfac[:, s_, 2:4], stat[:, s_, 0:2])
                own()
                G.tensor_tensor(rfac[:, s_, 0:2], rfac[:, s_, 2:4], rfac[:, 13 + l, 2:4], ALU.mult)\
                    .then_inc(pool_made, tick("pool", "nr", l, 2))
                if l == 0:
                    low_to(F_[("gate", 0)] + 3)
                    x_sums("in1")

    return L.at


INPUTS = ["x", "mem", "norm_gains", "xa_wq", "xa_wkv", "xa_wo", "mlp_w1", "mlp_w2", "ab_w_in", "pool_w",
          "pool_scale", "ssm_conv_w", "ssm_conv_b", "ssm_dt_bias", "ssm_a_log", "ssm_d", "ssm_norm", "ab_w_out",
          "cd_w_in", "conf_dw_w", "conf_dw_b", "conf_ln_g", "conf_ln_b", "sc_conv_w", "cd_w_out"]


def kernel(**inputs):
    import concourse.bacc as bacc
    from concourse.bass_utils import run_bass_kernel_spmd

    arrays = {f"in_{n}": np.ascontiguousarray(inputs[n]) for n in INPUTS}
    counts = None
    for _ in range(2):
        nc = bacc.Bacc("TRN2", target_bir_lowering=False, num_devices=1)
        A = {n: nc.dram_tensor(f"in_{n}", inputs[n].shape, F32, kind="ExternalInput").ap() for n in INPUTS}
        out = nc.dram_tensor("out_0", inputs["x"].shape, F32, kind="ExternalOutput").ap()
        counts = trunk(nc, A, out, counts)
    return run_bass_kernel_spmd(nc, [arrays], core_ids=[0]).results[0]["out_0"]
```

```python
from contextlib import ExitStack

import numpy as np
import concourse.bass as bass
from concourse import mybir

F32 = mybir.dt.float32
F32R = mybir.dt.float32r
ALU = mybir.AluOpType
ACT = mybir.ActivationFunctionType
AX = mybir.AxisListType

P = 128
SLOTS = 6
POOL_WINDOWS = (2, 4, 8, 16)
RMS_EPS, LN_EPS = 1e-6, 1e-5


class Ledger:

    def __init__(self, known):
        self.count, self.at, self.known = {}, {}, known

    def tick(self, sem, *label):
        self.count[sem] = self.count.get(sem, 0) + 1
        if label:
            assert (sem, *label) not in self.at, label
            self.at[(sem, *label)] = self.count[sem]
        return 1

    def after(self, sem, *label):
        if self.known is None:
            return 1
        return self.known[(sem, *label)]

    def also(self, sem, *label):
        self.at[(sem, *label)] = self.count[sem]

    def now(self, sem):
        return self.count[sem]


def weight_plan():
    s = []
    for j in range(3):
        s.append((("xbc", j), "ab_in", 0, 0, 8, 1536 + 512 * j))
    for j in range(2):
        s.append((("z", j), "ab_in", 0, 0, 8, 512 + 512 * j))
    s.append((("pool", 0), "ab_in", 0, 0, 8, 0))
    for l in range(2):
        if l == 1:
            for name, c in (("gate", 1024), ("a", 0), ("gate", 1536), ("a", 512), ("cg", 3072), ("hh", 4096),
                            ("cg", 3584), ("hh", 4608), ("bg", 2048), ("bg", 2560)):
                s.append(((name, (c // 512) % 2), "cd_in", 0, 0, 8, c))
        if l == 0:
            for g in range(2):
                s.append((("K", 0, g), "wkv", 0, 0, 8, 512 * g))
        else:
            s.append((("K", 1, 0, "early"), "wkv", 1, 0, 4, 0))
        out, early, late = (("ab_out", (0, 4), (4, 8)), ("cd_out", (8, 8), (0, 8)))[l]
        for part, (k0, nk) in (("early", early), ("late", late)):
            for g in range(2):
                s.append((("out", l, part, g), out, 0, 128 * k0, nk, 512 * g))
            if l == 1 and part == "early":
                s.append((("K", 1, 0, "late"), "wkv", 1, 512, 4, 0))
        s.append((("V", 0, 0), "wkv", 0, 0, 8, 1024) if l == 0 else (("K", 1, 1), "wkv", 1, 0, 8, 512))
        for g in range(2):
            s.append((("q", l, g), "wq", l, 0, 8, 512 * g))
        if l == 0:
            s.append((("V", 0, 1), "wkv", 0, 0, 8, 1536))
        for k0, part in ((0, "early"), (4, "late")):
            for g in range(2):
                s.append((("wo", l, part, g), "wo", l, 128 * k0, 4, 512 * g))
        if l == 0:
            s.append((("V", 1, 0), "wkv", 1, 0, 8, 1024))
        for h in range(9):
            for i in ([0, 1] if h == 0 else [h + 1] if h < 7 else []):
                s.append((("w1", l, i), "w1", l, 0, 8, 512 * i))
            if h < 8:
                for g in range(2):
                    s.append((("w2", l, h, g), "w2", l, 512 * h, 4, 512 * g))
        if l == 0:
            s.append((("V", 1, 1), "wkv", 1, 0, 8, 1536))
    return s


SETS = {0: dict(M0=(0, 1), M1=(2, 3), FI=(4, 5), T=(6, 7)),
        1: dict(M0=(2, 3), M1=(4, 5), FI=(0, 1), T=(6, 7))}


def bank_plan():
    u = []

    def pair(label, banks):
        u.extend([(label + (0,), banks[0]), (label + (1,), banks[1])])

    u.append((("gains",), 4))
    for i in range(4):
        u.append((("xT", i), i))
    pair(("xbc", 0), (6, 7))
    u.append((("R0",), 5))
    u.append((("vecs",), 4))
    u.append((("dt",), 5))
    pair(("xbc", 1), (0, 1))
    u.append((("dtT",), 5))
    for i, b in enumerate((4, 6, 7, 5)):
        u.append((("memT", i), b))
    pair(("xbc", 2), (2, 3))
    u.append((("cs",), 4))
    pair(("z", 0), (0, 1))
    for i, b in enumerate((6, 7, 4, 5)):
        u.append((("xsT", i), b))
    pair(("z", 1), (2, 3))
    u.append((("cb", 0), 6))
    u.append((("cb", 1), 7))
    pair(("pool", 0), (0, 1))
    for i in range(8):
        if i == 3:
            pair(("K", 0, 0), (2, 3))
        if i == 7:
            pair(("K", 0, 1), (0, 1))
        u.append((("rows", i), 6 + i % 2))
        if i >= 2 and i % 2 == 1:
            u.append((("y", (i - 3) // 2), 4 + (i - 3) // 2 % 2))
    u.append((("y", 3), 5))
    u.append((("pooled", 0), 6))
    u.append((("pooled", 1), 7))
    u.append((("gstat",), 4))
    u.append((("grow",), 5))
    for l in range(2):
        b = SETS[l]
        M0, M1, FI, T = b["M0"], b["M1"], b["FI"], b["T"]
        if l == 1:
            cycle = [(4, 5), (0, 1), (2, 3)]
            names = [("gate", 0), ("a", 0), ("gate", 1), ("a", 1), ("cg", 0), ("hh", 0), ("cg", 1), ("hh", 1),
                     ("bg", 0), ("bg", 1), ("K", 1, 0)]
            for n, name in enumerate(names):
                pair(name, cycle[n % 3])
                if n == 0:
                    u.append((("xstat", 0), 6))
                    u.append((("R1",), 7))
            u.append((("conv7",), 7))
            u.append((("mustat",), 7))
            u.append((("murow",), 6))
            u.append((("varstat",), 7))
            u.append((("varrow",), 6))
        pair(("out", l, 0), M0)
        pair(("out", l, 1), M1)
        pair(("V", 0, 0) if l == 0 else ("K", 1, 1), FI)
        u.append((("nstat", l, 0), T[0]))
        u.append((("nrow", l, 0), T[1]))
        pair(("q", l, 0), T)
        u.append((("astat", l), FI[0]))
        pair(("q", l, 1), M0)
        u.append((("scores", l, 0), FI[1]))
        u.append((("scores", l, 1), M1[0]))
        if l == 0:
            pair(("V", 0, 1), T)
        u.append((("pT", l, 0), FI[1]))
        u.append((("pT", l, 1), M1[0]))
        u.append((("scores", l, 2), M1[1]))
        u.append((("scores", l, 3), FI[0]))
        u.append((("o", l, 0), M0[0]))
        u.append((("o", l, 1), M0[1]))
        u.append((("pT", l, 2), M1[1]))
        u.append((("pT", l, 3), FI[0]))
        u.append((("o", l, 2), FI[1]))
        u.append((("o", l, 3), M1[0]))
        pair(("wo", l, 0), T)
        pair(("wo", l, 1), M0)
        if l == 0:
            pair(("V", 1, 0), M1)
        u.append((("nstat", l, 1), FI[0]))
        u.append((("nrow", l, 1), FI[1]))
        for h in range(8):
            pair(("w1", l, h), FI if h % 2 == 0 else M1)
            if h == 0:
                u.append((("hstat", l), T[0]))
        if l == 0:
            pair(("w2", 0, 0), T)
            pair(("w2", 0, 1), M0)
            pair(("V", 1, 1), M1)
            u.append((("nstat", 0, 2), FI[0]))
            u.append((("nrow", 0, 2), FI[1]))
        else:
            pair(("xout", 0), FI)
            pair(("xout", 1), FI)
            pair(("w2", 1, 0), T)
            pair(("w2", 1, 1), M0)
            pair(("mout", 0), M1)
            u.append((("nstat", 1, 2), T[0]))
            pair(("mout", 1), FI)
    return u


def trunk(nc, A, out, known):
    T = A["x"].shape[1]
    D = A["x"].shape[2]
    J = D // P
    HEADS = A["ssm_a_log"].shape[1]
    TT = T // P
    H2 = T * 2
    XA_SCALE = 1.0 / 16.0
    L = Ledger(known)
    tick, after, now = L.tick, L.after, L.now

    mats = {"ab_in": A["ab_w_in"], "ab_out": A["ab_w_out"], "cd_in": A["cd_w_in"], "cd_out": A["cd_w_out"],
            "wkv": A["xa_wkv"], "wq": A["xa_wq"], "wo": A["xa_wo"], "w1": A["mlp_w1"], "w2": A["mlp_w2"]}
    units, first, size = [], {}, {}
    for name, m, l, row, nk, col in weight_plan():
        first[name], size[name] = len(units), nk // 2
        for i in range(nk // 2):
            r = row + 256 * i
            units.append(mats[m][l, r:r + 256, col:col + 512].rearrange("(i p) c -> p i c", p=P))
    NU = len(units)
    pool_lo = [False] * NU
    for u in range(first[("xbc", 0)], first[("out", 0, "late", 0)]):
        pool_lo[u] = u % 2 == 1
    for u in range(first[("gate", 1)], first[("out", 1, "late", 0)]):
        pool_lo[u] = u % 8 != 7
    for seg in [("q", 0, 0), ("q", 1, 0), ("w1", 0, 0), ("w1", 1, 0), ("gate", 0)]:
        pool_lo[first[seg] + 1] = pool_lo[first[seg] + 3] = True
    for u in [first[("V", 0, 1)] + 1, first[("V", 0, 1)] + 3] + [first[("wo", l, p, g)] + 1 for l in range(2)
                                                                for p in ("early", "late") for g in range(2)]:
        pool_lo[u] = True
    for l in range(2):
        for u in range(first[("out", l, "late", 0)], first[("out", l, "late", 1)] + size[("out", l, "late", 1)]):
            pool_lo[u] = True
    lo_count, nd, npl = [], 0, 0
    for u in range(NU):
        nd, npl = nd + (not pool_lo[u]), npl + pool_lo[u]
        lo_count.append(npl if pool_lo[u] else nd)

    use, by_use, uses = {}, {}, [0] * 8
    for label, b in bank_plan():
        assert label not in use, label
        use[label] = (b, uses[b])
        by_use[b, uses[b]] = label
        uses[b] += 1

    ctx = ExitStack()
    with ctx:
        def sb(name, shape, dt=F32, scope=ctx):
            return scope.enter_context(nc.sbuf_tensor(name, [P, *shape], dt))

        def sem(name):
            return ctx.enter_context(nc.semaphore(name))

        xT = sb("xT", [J, T])
        h_hi, h_lo = sb("h_hi", [J, T], F32R), sb("h_lo", [J, T], F32R)
        mem_hi, mem_lo = sb("mem_hi", [J, T], F32R), sb("mem_lo", [J, T], F32R)
        k_hi, k_lo = sb("k_hi", [J, T], F32R), sb("k_lo", [J, T], F32R)
        w_hi = sb("w_hi", [SLOTS, 2, 512], F32R)
        with ExitStack() as s:
            raw = sb("raw", [SLOTS, 2, 512], scope=s)
        w_lo = sb("w_lo", [SLOTS, 2, 512], F32R)
        ident, ones, tri, cbmask = sb("ident", [P]), sb("ones", [P]), sb("tri", [P]), sb("cbmask", [3 * P])
        Rrow, Nrow = sb("Rrow", [T]), sb("Nrow", [T])
        vecs = sb("vecs", [512])
        sq = sb("sq", [2, H2])
        Ssum, S2 = sb("Ssum", [H2]), sb("S2", [T])
        stat = sb("stat", [16, 8])
        rfac = sb("rfac", [16, 8])
        mhalf = sb("mhalf", [8])
        tmp = sb("tmp", [2, T])
        with ExitStack() as s:
            v_hi, v_lo = sb("v_hi", [TT, D], F32R, s), sb("v_lo", [TT, D], F32R, s)
        with ExitStack() as s:
            my_hi, my_lo = sb("my_hi", [J, T], F32R, s), sb("my_lo", [J, T], F32R, s)
            hold = s.pop_all()
        ctx.enter_context(hold)
        with ExitStack() as s:
            xtok, memtok = sb("xtok", [TT, D], scope=s), sb("memtok", [TT, D], scope=s)
            stage = sb("stage", [4, P], scope=s)
        with ExitStack() as s:
            xdt = sb("xdt", [TT, D], scope=s)
            mp_hi, mp_lo = sb("mp_hi", [4, T], F32R, s), sb("mp_lo", [4, T], F32R, s)
            E = sb("E", [4, 3 * P], scope=s)
            cbm = sb("cbm", [2, 3 * P], scope=s)
            zs = sb("zs", [J, T], scope=s)
            xc = sb("xc", [12, T], scope=s)
            upad = sb("upad", [2, 2, T + 3], scope=s)
            pu = sb("pu", [4, T + 16], scope=s)
            pw1, pw2 = sb("pw1", [T + 16], scope=s), sb("pw2", [T + 16], scope=s)
            pdiff = sb("pdiff", [4, T], scope=s)
            Sg = sb("Sg", [2, T], scope=s)
            Rg = sb("Rg", [2, T], scope=s)
            icnt = sb("icnt", [4, 16], scope=s)
            poolw = sb("poolw", [4, P], scope=s)
            wdt, wdtg = sb("wdt", [J, HEADS], scope=s), sb("wdtg", [J, HEADS], scope=s)
            dtT = sb("dtT", [T], scope=s)
            dtb, expA, dskip = sb("dtb", [HEADS], scope=s), sb("expA", [HEADS], scope=s), sb("dskip", [J], scope=s)
            sp = sb("sp", [10, 2 * HEADS], scope=s)
            cs = sb("cs", [4, HEADS], scope=s)
        with ExitStack() as s:
            vpad = sb("vpad", [J, T + 30], scope=s)
            cv, cv3 = sb("cv", [J, T], scope=s), sb("cv3", [J, T], scope=s)
            ppad = sb("ppad", [2, 2, T + 2], scope=s)
            sg = sb("sg", [4, T], scope=s)
            mh, ml = sb("mh", [2 * J, T], F32R, s), sb("ml", [2 * J, T], F32R, s)
            Rsq = sb("Rsq", [T], scope=s)
            sct = sb("sct", [2, H2], scope=s)
        with ExitStack() as s:
            q_hi, q_lo = sb("q_hi", [J, T], F32R, s), sb("q_lo", [J, T], F32R, s)
            prob = sb("prob", [4, TT, T], scope=s)
            pt_hi, pt_lo = sb("pt_hi", [4, TT, T], F32R, s), sb("pt_lo", [4, TT, T], F32R, s)
        with ExitStack() as s:
            r_hi, r_lo = sb("r_hi", [2, 4, T], F32R, s), sb("r_lo", [2, 4, T], F32R, s)
            relu, rsq = sb("relu", [2, H2], scope=s), sb("rsq", [2, H2], scope=s)
            otok = sb("otok", [TT, D], scope=s)
            mg = sb("mg", [J, T], scope=s)
        ps = ctx.enter_context(nc.psum_tensor("ps", [P, 8, 512], F32))

        x_landed, gain_landed, mem_landed, vec_landed, ssm_landed, out_stored = (
            sem(n) for n in ("x_landed", "gain_landed", "mem_landed", "vec_landed", "ssm_landed", "out_stored"))
        raw_landed = [sem(f"raw_landed{i}") for i in range(SLOTS)]
        hi_ready, lo_ready_dve, lo_ready_pool = (sem(n) for n in ("hi_ready", "lo_ready_dve", "lo_ready_pool"))
        pe_made, act_made, dve_made, pool_made = sem("pe_made"), sem("act_made"), sem("dve_made"), sem("pool_made")

        GAIN, MISC, DW = 0, 128, 256

        def gain(l, s, j):
            return vecs[:, GAIN + (l * 6 + s) * J + j:GAIN + (l * 6 + s) * J + j + 1]

        MISC_ROWS = [("convw", A["ssm_conv_w"].rearrange("a k (j p) -> (a k j) p", p=P)),
                     ("convb", A["ssm_conv_b"].rearrange("a (j p) -> (a j) p", p=P)),
                     ("ssmn", A["ssm_norm"].rearrange("a (j p) -> (a j) p", p=P)),
                     ("pscale", A["pool_scale"].rearrange("a (j p) -> (a j) p", p=P)),
                     ("dwb", A["conf_dw_b"].rearrange("a (j p) -> (a j) p", p=P)),
                     ("lng", A["conf_ln_g"].rearrange("a (j p) -> (a j) p", p=P)),
                     ("lnb", A["conf_ln_b"].rearrange("a (j p) -> (a j) p", p=P)),
                     ("scw", A["sc_conv_w"].rearrange("a k (j p) -> (a k j) p", p=P))]
        misc_at, n = {}, 0
        for name, v in MISC_ROWS:
            misc_at[name] = MISC + n
            n += v.shape[0]
        MISC_N = n

        def vec(name, j):
            return vecs[:, misc_at[name] + j:misc_at[name] + j + 1]

        def tap(k, j):
            return vecs[:, DW + k * J + j:DW + k * J + j + 1]

        dw_rows = A["conf_dw_w"].rearrange("a k (j p) -> (a k j) p", p=P)
        DWN = dw_rows.shape[0]

        def bank(label):
            return ps[:, use[label][0], :]

        def bank2(label):
            return ps[:, use[label][0], :].rearrange("p (c t) -> p c t", c=2)

        def full(label):
            return pe_made, after("pe", label)

        def freed(engine, label):
            L.at[("free", label)] = (engine, now(engine))

        def row2(r):
            return r[:, :].unsqueeze(1).broadcast_to([P, 2, T])

        def f(ap):
            return ap.bitcast(F32)

        def lo_wait(u):
            return (lo_ready_pool if pool_lo[u] else lo_ready_dve), lo_count[u]

        def mixer_out(l, kt):
            if l == 0:
                return (mp_hi[:, kt, :], mp_lo[:, kt, :]) if kt < 4 else (my_hi[:, kt - 4, :], my_lo[:, kt - 4, :])
            return mh[:, kt, :], ml[:, kt, :]

        FILL = {(0, 0): ("V", 0, 0), (0, 1): ("V", 1, 0), (0, 2): ("V", 1, 1), (1, 0): ("K", 1, 1)}

        def fill_dst(seg, q):
            if seg[0] == "V":
                c = slice(512 * seg[2], 512 * seg[2] + 512)
                return v_hi[:, q, c], v_lo[:, q, c]
            c = slice(4 * seg[2] + 2 * q, 4 * seg[2] + 2 * q + 2)
            return k_hi[:, c, :], k_lo[:, c, :]

        def fill_name(seg, q):
            return seg + (q,) if seg[0] == "V" else ("K", seg[1], 2 * seg[2] + q)

        def diag(k):
            return tmp[:, k % 4 // 2, k % 2 * P:(k % 2 + 1) * P]

        k_ahead = [i + 5 for i in range(8)]

        block = ctx.enter_context(nc.Block())

        @block.sync
        def _(sp_):
            sp_.dma_start(xtok[:, :, :], A["x"][0].rearrange("(t p) d -> p t d", p=P)).then_inc(x_landed, 16)

            def later_inputs():
                for name, v in MISC_ROWS:
                    r0 = misc_at[name] - MISC
                    sp_.dma_start(stage[r0:r0 + v.shape[0], 1, :], v).then_inc(vec_landed, 16)
                sp_.dma_start(stage[:, 2, :], dw_rows[0:P, :]).then_inc(vec_landed, 16)
                sp_.dma_start(stage[0:DWN - P, 3, :], dw_rows[P:DWN, :]).then_inc(vec_landed, 16)
                sp_.dma_start(wdt[:, :, :], A["ab_w_in"][0, :, 3072:3088].rearrange("(j p) h -> p j h", p=P))\
                    .then_inc(ssm_landed, 16)
                sp_.dma_start(dtb[:, :], A["ssm_dt_bias"].broadcast_to([P, HEADS])).then_inc(ssm_landed, 16)
                sp_.dma_start(expA[:, :], A["ssm_a_log"].broadcast_to([P, HEADS])).then_inc(ssm_landed, 16)
                for hf in range(2):
                    sp_.dma_start(dskip[64 * hf:64 * hf + 64, :],
                                  A["ssm_d"].rearrange("a (j two) -> a two j", two=2)[:, hf, :].broadcast_to([64, J]),
                                  allow_slow_non_contiguous=True).then_inc(ssm_landed, 16)
                sp_.dma_start(poolw[:, :, :], A["pool_w"][0].rearrange("g i o -> i g o")).then_inc(ssm_landed, 16)
                sp_.dma_start(memtok[:, :, :], A["mem"][0].rearrange("(t p) d -> p t d", p=P)).then_inc(mem_landed, 16)

            for u in range(NU):
                if u == 4:
                    later_inputs()
                if u >= SLOTS:
                    sp_.wait_ge(pe_made, after("pe", "unit", u - SLOTS))
                sp_.dma_start(raw[:, u % SLOTS, :, :], units[u]).then_inc(raw_landed[u % SLOTS], 16)
            for i in range(4):
                hf, t = i // 2, i % 2
                sp_.wait_ge(dve_made, after("dve", "otok", i))
                sp_.dma_start(out[0, t * P:(t + 1) * P, hf * 512:(hf + 1) * 512],
                              otok[:, t, hf * 512:(hf + 1) * 512]).then_inc(out_stored, 16)
            sp_.wait_ge(out_stored, 16 * 2 * TT)

        @block.tensor
        def _(pe):
            done = [0] * 8
            def acquire(label):
                b, k = use[label]
                assert done[b] == k, label
                if k and known is not None:
                    engine, n = known[("free", by_use[b, k - 1])]
                    pe.wait_ge(act_made if engine == "act" else dve_made, n)

            def finish(label):
                b, k = use[label]
                assert done[b] == k, label
                done[b] += 1
                return pe_made, tick("pe", label)

            def three(dst, wt, x, start, stop):
                nc.tensor.matmul(dst, wt[0], x[0], start=start, stop=False, skip_group_check=True)
                nc.tensor.matmul(dst, wt[0], x[1], start=False, stop=False, skip_group_check=True)
                return nc.tensor.matmul(dst, wt[1], x[0], start=False, stop=stop, skip_group_check=True)

            def unit_w(u, i, n):
                c = slice(n * P, (n + 1) * P)
                return w_hi[:, u % SLOTS, i, c], w_lo[:, u % SLOTS, i, c]

            def project(seg, dest, src, k0=0, first_k=True, last_k=True, ready=None, only=None, tail=2):
                nu = size[seg]
                us = range(nu) if only is None else only
                if not last_k or us[-1] != nu - 1:
                    tail = 0
                for ui in us:
                    if tail and ui >= nu - tail:
                        break
                    u = first[seg] + ui
                    pe.wait_ge(*lo_wait(u))
                    for i in range(2):
                        kt = k0 + 2 * ui + i
                        if ready:
                            ready(kt)
                        for n in range(4):
                            st = first_k and ui == 0 and i == 0 and n % 2 == 0
                            if st:
                                acquire(dest[n // 2])
                            ends = last_k and ui == nu - 1 and i == 1
                            mm = three(bank2(dest[n // 2])[:, n % 2, :], unit_w(u, i, n), src(kt), st, ends)
                            if ends and n == 1:
                                mm.then_inc(*finish(dest[0]))
                    if ends:
                        mm.then_inc(*finish(dest[1]))
                        L.also("pe", "unit", u)
                    else:
                        mm.then_inc(pe_made, tick("pe", "unit", u))
                if tail:
                    u0 = first[seg] + nu - tail
                    for u in range(u0, u0 + tail):
                        pe.wait_ge(*lo_wait(u))
                    kts = 2 * tail
                    if ready:
                        for q in range(kts):
                            ready(k0 + 2 * nu - kts + q)
                    for n in range(4):
                        for q in range(kts):
                            st = first_k and nu == tail and q == 0 and n % 2 == 0
                            if st:
                                acquire(dest[n // 2])
                            mm = three(bank2(dest[n // 2])[:, n % 2, :], unit_w(u0 + q // 2, q % 2, n),
                                       src(k0 + 2 * nu - kts + q), st, q == kts - 1)
                            if n == 3 and q % 2 == 1 and q < kts - 1:
                                mm.then_inc(pe_made, tick("pe", "unit", u0 + q // 2))
                            if n == 1 and q == kts - 1:
                                mm.then_inc(*finish(dest[0]))
                    mm.then_inc(*finish(dest[1]))
                    L.also("pe", "unit", u0 + tail - 1)

            def h_src(kt):
                return h_hi[:, kt, :], h_lo[:, kt, :]

            def transposes(label, parts):
                acquire(label)
                for c, src, k in parts:
                    mm = nc.tensor.transpose(bank(label)[:, c:c + k], src, ident[0:k, 0:k])
                mm.then_inc(*finish(label))

            def token_sums(label, sources):
                acquire(label)
                for i, s_ in enumerate(sources):
                    mm = nc.tensor.matmul(bank(label)[:, i:i + 1], s_, ones[:, 0:1], start=True, stop=True)
                mm.then_inc(*finish(label))

            def rows(label, cols):
                acquire(label)
                for i, c in enumerate(cols):
                    mm = nc.tensor.matmul(bank(label)[:, i * P:(i + 1) * P], c.broadcast_to([P, P]), ident[:, :],
                                          start=True, stop=True)
                mm.then_inc(*finish(label))

            def halves(s_):
                return [s_[:, t * P:(t + 1) * P] for t in range(TT)]

            pe.wait_ge(pool_made, after("pool", "ident"))
            pe.wait_ge(gain_landed, 16)
            transposes(("gains",), [(0, stage[0:96, 0, :], 96)])
            pe.wait_ge(x_landed, 16)
            for i in range(4):
                transposes(("xT", i), [((c * TT + t) * P, xtok[:, t, (2 * i + c) * P:(2 * i + c + 1) * P], P)
                                       for c in range(2) for t in range(TT)])

            def h_ready(tag):
                def ready(kt):
                    pe.wait_ge(dve_made, after("dve", "h", tag, kt))
                return ready

            project(("xbc", 0), [("xbc", 0, 0), ("xbc", 0, 1)], h_src, ready=h_ready("in0"), tail=0)
            pe.wait_ge(pool_made, after("pool", "r0"))
            rows(("R0",), [rfac[:, 0, t:t + 1] for t in range(TT)])
            pe.wait_ge(vec_landed, 16 * (2 + len(MISC_ROWS)))
            transposes(("vecs",), [(P, stage[0:MISC_N, 1, :], MISC_N), (2 * P, stage[:, 2, :], P),
                                   (3 * P, stage[0:DWN - P, 3, :], DWN - P)])
            pe.wait_ge(dve_made, after("dve", "wdtg"))
            acquire(("dt",))
            for j in range(J):
                mm = nc.tensor.matmul(ps[0:HEADS, use[("dt",)][0], 0:T], wdtg[:, j, :], xT[:, j, :],
                                      start=(j == 0), stop=(j == J - 1))
            mm.then_inc(*finish(("dt",)))
            project(("xbc", 1), [("xbc", 1, 0), ("xbc", 1, 1)], h_src)
            pe.wait_ge(act_made, after("act", "dtT"))
            acquire(("dtT",))
            for t in range(TT):
                mm = nc.tensor.matmul(bank(("dtT",))[:, t * HEADS:(t + 1) * HEADS], dtT[0:HEADS, t * P:(t + 1) * P],
                                      ident[0:HEADS, 0:HEADS], start=True, stop=True)
            mm.then_inc(*finish(("dtT",)))
            pe.wait_ge(mem_landed, 16)
            for i in range(4):
                transposes(("memT", i), [((c * TT + t) * P, memtok[:, t, (2 * i + c) * P:(2 * i + c + 1) * P], P)
                                         for c in range(2) for t in range(TT)])
            project(("xbc", 2), [("xbc", 2, 0), ("xbc", 2, 1)], h_src)
            project(("z", 0), [("z", 0, 0), ("z", 0, 1)], h_src)
            pe.wait_ge(dve_made, after("dve", "dA"))
            acquire(("cs",))
            dt_ = sp[:, 8, :].rearrange("p (t h) -> p t h", t=TT)
            dA = sp[:, 9, :].rearrange("p (t h) -> p t h", t=TT)
            for t in range(TT):
                nc.tensor.matmul(bank(("cs",))[:, t * HEADS:(t + 1) * HEADS], tri[:, :], dA[:, t, :],
                                 start=True, stop=True)
            nc.tensor.matmul(bank(("cs",))[:, 2 * HEADS:3 * HEADS], ones[:, :], dA[:, 0, :],
                             start=True, stop=True).then_inc(*finish(("cs",)))
            pe.wait_ge(act_made, after("act", "xc", 3))
            for i in range(4):
                t, q = i // 2, i % 2
                transposes(("xsT", i), [(c * P, xc[:, 4 * q + c, t * P:(t + 1) * P], P) for c in range(4)])
            project(("z", 1), [("z", 1, 0), ("z", 1, 1)], h_src)
            pe.wait_ge(act_made, after("act", "xc", 5))
            for g in range(2):
                acquire(("cb", g))
                nc.tensor.matmul(bank(("cb", g))[:, 0:T], xc[:, 8 + g, 0:P], xc[:, 10 + g, :], start=True, stop=True)
                nc.tensor.matmul(bank(("cb", g))[:, T:T + P], xc[:, 8 + g, P:T], xc[:, 10 + g, P:T],
                                 start=True, stop=True).then_inc(*finish(("cb", g)))
            project(("pool", 0), [("pool", 0, 0), ("pool", 0, 1)], h_src)

            def mem_src(kt):
                return mem_hi[:, kt, :], mem_lo[:, kt, :]

            def y_pair(i):
                for h in (2 * i, 2 * i + 1):
                    yb = ("y", h // 4)
                    if h % 4 == 0:
                        acquire(yb)
                    pe.wait_ge(dve_made, after("dve", "EC", h))
                    dst = ps[64 * (h % 2):64 * (h % 2) + 64, use[yb][0], :].rearrange("p (c t) -> p c t", c=2)
                    nc.tensor.matmul(dst[:, i % 2, :], xdt[:, 0, h * 64:(h + 1) * 64], E[:, h % 4, 0:T],
                                     start=True, stop=False, skip_group_check=True)
                    mm = nc.tensor.matmul(dst[:, i % 2, P:T], xdt[:, 1, h * 64:(h + 1) * 64], E[:, h % 4, T:T + P],
                                          start=False, stop=True, skip_group_check=True)
                    if h % 4 == 3:
                        mm.then_inc(*finish(yb))
                        L.also("pe", "head", h)
                    else:
                        mm.then_inc(pe_made, tick("pe", "head", h))

            for i in range(8):
                g = i // 4
                pe.wait_ge(dve_made, after("dve", "mem", 3))
                project(("K", 0, g), [("K", 0, g, 0), ("K", 0, g, 1)], mem_src, only=[i % 4], tail=1)
                if i == 0:
                    pe.wait_ge(dve_made, after("dve", "cs"))
                acquire(("rows", i))
                for hh in range(2):
                    for t in range(TT):
                        mm = nc.tensor.matmul(bank(("rows", i))[:, hh * T + t * P:hh * T + (t + 1) * P],
                                              dA[:, t, 2 * i + hh:2 * i + hh + 1].broadcast_to([P, P]), tri[:, :],
                                              start=True, stop=True)
                mm.then_inc(*finish(("rows", i)))
                if i == 2:
                    pe.wait_ge(dve_made, after("dve", "xdt", 3))
                if i >= 2:
                    y_pair(i - 2)
            pe.wait_ge(ssm_landed, 16 * 6)
            for i in range(2):
                acquire(("pooled", i))
                for c in range(2):
                    g = 2 * i + c
                    pe.wait_ge(pool_made, after("pool", "pdiff", g))
                    mm = nc.tensor.matmul(bank2(("pooled", i))[:, c, :], poolw[:, g, :], pdiff[:, g, :],
                                          start=True, stop=True)
                mm.then_inc(*finish(("pooled", i)))
                y_pair(6 + i)

            def mix0(kt):
                return mixer_out(0, kt)

            def mix1(kt):
                return mixer_out(1, kt)

            def out_banks(l, g):
                return [("out", l, g, 0), ("out", l, g, 1)]

            def mix_ready(l):
                return lambda kt: pe.wait_ge(dve_made, after("dve", "mix", l, kt))

            def boundary(l, n, filler):
                filler([0, 1])
                pe.wait_ge(dve_made, after("dve", "S2", l, n))
                token_sums(("nstat", l, n), halves(S2))
                filler([2])
                pe.wait_ge(pool_made, after("pool", "nr", l, n))
                rows(("nrow", l, n), [rfac[:, 1 + 3 * l + n, t:t + 1] for t in range(TT)])
                filler([3])

            def v_group(l, g, only):
                seg = ("V", l, g)
                for ui in only:
                    u = first[seg] + ui
                    pe.wait_ge(*lo_wait(u))
                    for i in range(2):
                        kt = 2 * ui + i
                        for t in range(TT):
                            if kt == 0:
                                acquire(seg + (t,))
                            ms = slice(t * P, (t + 1) * P)
                            wh, wl = w_hi[:, u % SLOTS, i, :], w_lo[:, u % SLOTS, i, :]
                            dst = bank(seg + (t,))
                            nc.tensor.matmul(dst, mem_hi[:, kt, ms], wh, start=(kt == 0), stop=False)
                            nc.tensor.matmul(dst, mem_hi[:, kt, ms], wl, start=False, stop=False)
                            mm = nc.tensor.matmul(dst, mem_lo[:, kt, ms], wh, start=False, stop=(kt == J - 1))
                            if kt == J - 1:
                                mm.then_inc(*finish(seg + (t,)))
                    if ui == 3:
                        L.also("pe", "unit", u)
                    else:
                        mm.then_inc(pe_made, tick("pe", "unit", u))

            def scores(l, h):
                acquire(("scores", l, h))
                pe.wait_ge(dve_made, after("dve", "q", l, h))
                pe.wait_ge(dve_made, after("dve", "K", l, h))
                for t in range(TT):
                    for c in range(2):
                        j = 2 * h + c
                        mm = three(bank2(("scores", l, h))[:, t, :],
                                   (q_hi[:, j, t * P:(t + 1) * P], q_lo[:, j, t * P:(t + 1) * P]),
                                   (k_hi[:, j, :], k_lo[:, j, :]), t == 0 and c == 0, c == 1)
                mm.then_inc(*finish(("scores", l, h)))

            def prob_T(l, h):
                pe.wait_ge(dve_made, after("dve", "prob", l, h))
                transposes(("pT", l, h), [((m * TT + t) * P, prob[:, h, t, m * P:(m + 1) * P], P)
                                          for m in range(TT) for t in range(TT)])

            def attend(l, h):
                acquire(("o", l, h))
                pe.wait_ge(dve_made, after("dve", "pT", l, h))
                pe.wait_ge(dve_made, after("dve", "V", l, h // 2, 1))
                for c in range(2):
                    for m in range(TT):
                        col = slice(h * T + c * P, h * T + (c + 1) * P)
                        mm = three(bank2(("o", l, h))[:, c, :], (v_hi[:, m, col], v_lo[:, m, col]),
                                   (pt_hi[:, h, m, :], pt_lo[:, h, m, :]), c == 0 and m == 0, m == 1)
                mm.then_inc(*finish(("o", l, h)))

            def nothing(us):
                pass

            for l in range(2):
                if l == 1:
                    for n, name in enumerate([("gate", 0), ("a", 0), ("gate", 1), ("a", 1), ("cg", 0), ("hh", 0),
                                              ("cg", 1), ("hh", 1), ("bg", 0), ("bg", 1)]):
                        project(name, [name + (0,), name + (1,)], h_src, ready=h_ready("in1") if n == 0 else None,
                                tail=2 if n else 0)
                        if n == 0:
                            pe.wait_ge(pool_made, after("pool", "Sx", "in1"))
                            token_sums(("xstat", 0), halves(S2))
                            pe.wait_ge(pool_made, after("pool", "r1"))
                            rows(("R1",), [rfac[:, 7, t:t + 1] for t in range(TT)])
                    project(("K", 1, 0, "early"), [("K", 1, 0, 0), ("K", 1, 0, 1)], mem_src, last_k=False)
                ke, kl = ((0, 4), (8, 0))[l]
                if l == 0:
                    project(("out", 0, "early", 0), out_banks(0, 0), mix0, k0=ke, last_k=False,
                            ready=mix_ready(0))
                    pe.wait_ge(dve_made, after("dve", "Sg", 1))
                    token_sums(("gstat",), halves(Sg[:, 0, :]) + halves(Sg[:, 1, :]))
                    project(("out", 0, "early", 1), out_banks(0, 1), mix0, k0=ke, last_k=False, only=[0])
                    pe.wait_ge(pool_made, after("pool", "gr"))
                    rows(("grow",), [rfac[:, 8, i:i + 1] for i in range(4)])
                    project(("out", 0, "early", 1), out_banks(0, 1), mix0, k0=ke, last_k=False, only=[1])
                else:
                    acquire(("conv7",))
                    pe.wait_ge(dve_made, after("dve", "v", 3))
                    for k in range(31):
                        pe.wait_ge(act_made, after("act", "diag", k))
                        mm = nc.tensor.matmul(bank(("conv7",))[:, 0:T], diag(k), vpad[:, J - 1, k:k + T],
                                              start=(k == 0), stop=(k == 30))
                        mm.then_inc(*(finish(("conv7",)) if k == 30 else (pe_made, tick("pe", "tap", k))))
                    project(("out", 1, "early", 0), out_banks(1, 0), mix1, k0=ke, last_k=False,
                            ready=mix_ready(1))
                    pe.wait_ge(dve_made, after("dve", "S2", "mu"))
                    token_sums(("mustat",), halves(S2))
                    pe.wait_ge(dve_made, after("dve", "negmu"))
                    rows(("murow",), [rfac[:, 9, t:t + 1] for t in range(TT)])
                    project(("out", 1, "early", 1), out_banks(1, 1), mix1, k0=ke, last_k=False,
                            only=[0, 1, 2])
                    pe.wait_ge(dve_made, after("dve", "S2", "var"))
                    token_sums(("varstat",), halves(S2))
                    project(("out", 1, "early", 1), out_banks(1, 1), mix1, k0=ke, last_k=False, only=[3])
                    pe.wait_ge(pool_made, after("pool", "lnr"))
                    rows(("varrow",), [rfac[:, 10, t:t + 1] for t in range(TT)])
                    project(("K", 1, 0, "late"), [("K", 1, 0, 0), ("K", 1, 0, 1)], mem_src, k0=4, first_k=False,
                            tail=0)
                for g in range(2):
                    project(("out", l, "late", g), out_banks(l, g), (mix0, mix1)[l], k0=kl, first_k=False,
                            ready=mix_ready(l) if g == 0 else None, tail=2 * g)
                boundary(l, 0, (lambda us: v_group(0, 0, us)) if l == 0 else
                         (lambda us: project(("K", 1, 1), [("K", 1, 1, 0), ("K", 1, 1, 1)], mem_src, only=us, tail=1)))
                project(("q", l, 0), [("q", l, 0, 0), ("q", l, 0, 1)], h_src, ready=h_ready(f"q{l}"), tail=0)
                q1 = [("q", l, 1, 0), ("q", l, 1, 1)]
                project(("q", l, 1), q1, h_src, only=[0])
                pe.wait_ge(pool_made, after("pool", "Sx", f"q{l}"))
                token_sums(("astat", l), halves(S2))
                project(("q", l, 1), q1, h_src, only=[1])
                scores(l, 0)
                scores(l, 1)
                project(("q", l, 1), q1, h_src, only=[2, 3])
                if l == 0:
                    v_group(0, 1, [0, 1])
                prob_T(l, 0)
                prob_T(l, 1)
                scores(l, 2)
                scores(l, 3)
                attend(l, 0)
                attend(l, 1)

                def wo(part, g, only=None):
                    k0 = 0 if part == "early" else 4
                    project(("wo", l, part, g), [("wo", l, g, 0), ("wo", l, g, 1)], h_src, k0=k0,
                            first_k=part == "early", last_k=part == "late", only=only,
                            ready=lambda kt: pe.wait_ge(dve_made, after("dve", "o", l, kt // 2)))

                if l == 0:
                    v_group(0, 1, [2, 3])
                    prob_T(l, 2)
                    prob_T(l, 3)
                    wo("early", 0)
                else:
                    wo("early", 0, [0])
                    prob_T(l, 2)
                    prob_T(l, 3)
                    wo("early", 0, [1])
                attend(l, 2)
                attend(l, 3)
                wo("early", 1)
                for g in range(2):
                    wo("late", g)
                boundary(l, 1, (lambda us: v_group(1, 0, us)) if l == 0 else nothing)

                def w1(h):
                    project(("w1", l, h), [("w1", l, h, 0), ("w1", l, h, 1)], h_src,
                            ready=h_ready(f"mlp{l}") if h == 0 else None, tail=2 if h else 0)

                def w2(h, gs=(0, 1)):
                    for g in gs:
                        project(("w2", l, h, g), [("w2", l, g, 0), ("w2", l, g, 1)],
                                lambda kt: (r_hi[:, h % 2, kt, :], r_lo[:, h % 2, kt, :]),
                                first_k=h == 0, last_k=h == 7,
                                ready=(lambda kt: pe.wait_ge(dve_made, after("dve", "r", l, h, kt // 2))) if g == 0
                                else None)

                w1(0)
                pe.wait_ge(pool_made, after("pool", "Sx", f"mlp{l}"))
                token_sums(("hstat", l), halves(S2))
                w1(1)
                for h in range(7):
                    w2(h)
                    if h < 6:
                        w1(h + 2)
                if l == 0:
                    w2(7)
                    boundary(0, 2, lambda us: v_group(1, 1, us))
            pe.wait_ge(dve_made, after("dve", "x", "mlp1", J - 1))
            for g in range(2):
                for t in range(TT):
                    transposes(("xout", g, t), [(q * P, xT[:, 4 * g + q, t * P:(t + 1) * P], P) for q in range(4)])
                w2(7, (g,))
            for g in range(2):
                pe.wait_ge(act_made, after("act", "mg", 4 * g + 3))
                for t in range(TT):
                    transposes(("mout", g, t), [(q * P, mg[:, 4 * g + q, t * P:(t + 1) * P], P) for q in range(4)])
                if g == 0:
                    pe.wait_ge(dve_made, after("dve", "S2", 1, 2))
                    token_sums(("nstat", 1, 2), halves(S2))

        @block.scalar
        def _(act):
            nu = [0]

            def round_to(u):
                while nu[0] <= min(u, NU - 1):
                    v = nu[0]
                    act.wait_ge(raw_landed[v % SLOTS], 16 * (v // SLOTS + 1))
                    nc.scalar.activation(w_hi[:, v % SLOTS, :, :], raw[:, v % SLOTS, :, :], ACT.Copy)\
                        .then_inc(hi_ready, 1)
                    nu[0] += 1

            def own():
                act.wait_ge(act_made, now("act"))

            act.dma_start(stage[0:96, 0, :], A["norm_gains"].rearrange("l s (j p) -> (l s j) p", p=P))\
                .then_inc(gain_landed, 16)

            act.wait_ge(*full(("gains",)))
            nc.scalar.activation(vecs[:, GAIN:GAIN + 96], bank(("gains",))[:, 0:96], ACT.Copy)\
                .then_inc(act_made, tick("act", "gains"))
            freed("act", ("gains",))
            own()

            def h_part(tag, l, s, j):
                act.wait_ge(dve_made, after("dve", "x", tag, j))
                nc.scalar.activation(h_hi[:, j, :], xT[:, j, :], ACT.Identity, scale=gain(l, s, j))\
                    .then_inc(act_made, tick("act", "h", tag, j))

            for j in range(J):
                round_to(j // 2 + 1)
                h_part("in0", 0, 0, j)
            act.wait_ge(x_landed, 16)
            for t in range(TT):
                if t:
                    own()
                nc.scalar.activation(sq[:, :, :].rearrange("p a b -> p (a b)"), xtok[:, t, :], ACT.Square,
                                     accum_out=stat[:, 0, t:t + 1]).then_inc(act_made, tick("act", "ss0", t))
            act.wait_ge(*full(("R0",)))
            nc.scalar.activation(Rrow[:, :], bank(("R0",))[:, 0:T], ACT.Copy).then_inc(act_made, tick("act", "Rrow", 0))
            freed("act", ("R0",))
            act.wait_ge(ssm_landed, 16 * 6)
            nc.scalar.activation(expA[:, :], expA[:, :], ACT.Exp).then_inc(act_made, tick("act", "expA"))

            def silu_pair(i):
                act.wait_ge(dve_made, after("dve", "conv", i))
                nc.scalar.activation(xc[:, 2 * i:2 * i + 2, :], xc[:, 2 * i:2 * i + 2, :], ACT.Silu)\
                    .then_inc(act_made, tick("act", "xc", i))

            F_ = first
            round_to(F_[("xbc", 0)] + 5)
            act.wait_ge(*full(("vecs",)))
            for c, k in ((MISC, MISC_N), (DW, DWN)):
                nc.scalar.activation(vecs[:, c:c + k], bank(("vecs",))[:, c:c + k], ACT.Copy)\
                    .then_inc(act_made, tick("act", *(("vecs",) if c == DW else ())))
            freed("act", ("vecs",))
            act.wait_ge(*full(("dt",)))
            nc.scalar.activation(dtT[0:HEADS, :], ps[0:HEADS, use[("dt",)][0], 0:T], ACT.Copy)\
                .then_inc(act_made, tick("act", "dtT"))
            freed("act", ("dt",))
            round_to(F_[("xbc", 1)] + 3)
            for i in range(2):
                silu_pair(i)
                round_to(F_[("xbc", 1)] + i + 4)
            for i in range(4):
                act.wait_ge(*full(("memT", i)))
                nc.scalar.activation(mem_hi[:, 2 * i:2 * i + 2, :], bank2(("memT", i)), ACT.Copy)\
                    .then_inc(act_made, tick("act", "mem", i))
            round_to(F_[("z", 0)] + 1)
            act.wait_ge(dve_made, after("dve", "spabs"))
            nc.scalar.activation(sp[:, 2, :], sp[:, 1, :], ACT.Exp, scale=-1.0).then_inc(act_made, tick("act", "spexp"))
            round_to(F_[("z", 0)] + 2)
            act.wait_ge(dve_made, after("dve", "sp1"))
            nc.scalar.activation(sp[:, 4, :], sp[:, 3, :], ACT.Ln).then_inc(act_made, tick("act", "spln"))
            round_to(F_[("z", 0)] + 3)
            for i in range(2, 4):
                silu_pair(i)
                round_to(F_[("z", 1)] + i - 2)
            for i in range(4, 6):
                silu_pair(i)
                round_to(F_[("z", 1)] + 2 * (i - 4) + 3)
            for i in range(4):
                act.wait_ge(dve_made, after("dve", "z", i))
                nc.scalar.activation(zs[:, 2 * i:2 * i + 2, :], zs[:, 2 * i:2 * i + 2, :], ACT.Silu)\
                    .then_inc(act_made, tick("act", "z", i))
                if i < 2:
                    round_to(F_[("pool", 0)] + 2 * i + 3)
                else:
                    round_to(F_[("K", 0, 0)] + 2 * (i - 2) + 3)

            def hi_of(dst, label, *name, wait=None):
                act.wait_ge(*full(label))
                if wait:
                    act.wait_ge(*wait)
                nc.scalar.activation(dst, bank2(label) if len(dst.shape) == 3 else bank(label), ACT.Copy)\
                    .then_inc(act_made, tick("act", *name))

            def y_squares(i):
                act.wait_ge(dve_made, after("dve", "yg", i))
                if i >= 2:
                    act.wait_ge(dve_made, after("dve", "Sg", 0))
                nc.scalar.activation(sq[:, i % 2, :].rearrange("p (c t) -> p c t", c=2), zs[:, 2 * i:2 * i + 2, :],
                                     ACT.Square).then_inc(act_made, tick("act", "ysq", i))

            for i in range(8):
                for h in (2 * i, 2 * i + 1):
                    act.wait_ge(dve_made, after("dve", "E", h))
                    nc.scalar.activation(E[:, h % 4, :], E[:, h % 4, :], ACT.Exp)\
                        .then_inc(act_made, tick("act", "E", h))
                if i == 4:
                    for q in range(2):
                        hi_of(k_hi[:, 2 * q:2 * q + 2, :], ("K", 0, 0, q), "K", 0, q)
                round_to(F_[("K", 0, 0)] + k_ahead[i])
                if i in (5, 6):
                    y_squares(i - 5)
            for q in range(2):
                hi_of(k_hi[:, 4 + 2 * q:6 + 2 * q, :], ("K", 0, 1, q), "K", 0, 2 + q)
            for i in range(2):
                for c in range(2):
                    g = 2 * i + c
                    if c == 0:
                        act.wait_ge(*full(("pooled", i)))
                    nc.scalar.activation(mp_hi[:, g, :], bank2(("pooled", i))[:, c, :], ACT.Identity,
                                         scale=vec("pscale", g)).then_inc(act_made, tick("act", "mp", g))
            y_squares(2)
            y_squares(3)
            round_to(F_[("out", 0, "late", 0)] + 1)
            act.wait_ge(*full(("grow",)))
            nc.scalar.activation(Rg[:, :, :], bank2(("grow",)), ACT.Copy).then_inc(act_made, tick("act", "Rg"))
            freed("act", ("grow",))
            for c in range(J):
                act.wait_ge(dve_made, after("dve", "yn", c))
                nc.scalar.activation(my_hi[:, c, :], zs[:, c, :], ACT.Copy).then_inc(act_made, tick("act", "mix", 0, 4 + c))
                if c % 2 == 1:
                    round_to(F_[("out", 0, "late", 0)] + c // 2 + 2)

            def attention(l):
                W = F_[("wo", l, "early", 0)]
                end = F_[("q", l, 1)] + 4
                round_to(F_[("q", l, 1)] + 3)
                for h in range(2):
                    hi_of(q_hi[:, 2 * h:2 * h + 2, :], ("q", l, 0, h), "q", l, h)
                round_to(end + 1)

                def exp(h):
                    for t in range(TT):
                        act.wait_ge(dve_made, after("dve", "nmax", l, h))
                        nc.scalar.activation(prob[:, h, t, :], bank2(("scores", l, h))[:, t, :], ACT.Exp,
                                             bias=stat[:, 8 + h, 2 + t:3 + t], scale=rfac[:, 11 + l, 2 + t:3 + t],
                                             accum_out=stat[:, 8 + h, 4 + t:5 + t])\
                            .then_inc(act_made, tick("act", "exp", l, h, t))
                    freed("act", ("scores", l, h))

                exp(0)
                round_to(end + 2)
                exp(1)
                round_to(end + 3)
                for h in range(2, 4):
                    hi_of(q_hi[:, 2 * h:2 * h + 2, :], ("q", l, 1, h - 2), "q", l, h)
                hi_of(pt_hi[:, 0, :, :], ("pT", l, 0), "pT", l, 0)
                hi_of(pt_hi[:, 1, :, :], ("pT", l, 1), "pT", l, 1)
                if l == 0:
                    round_to(end + 7)
                exp(2)
                exp(3)
                if l == 1:
                    round_to(end + 4)
                hi_of(h_hi[:, 0:2, :], ("o", l, 0), "o", l, 0)
                hi_of(h_hi[:, 2:4, :], ("o", l, 1), "o", l, 1)
                round_to(end + 5)
                if l == 0:
                    for t in range(TT):
                        hi_of(v_hi[:, t, 512:1024], ("V", 0, 1, t), "V", 0, 1, t)
                    round_to(W + 5)
                hi_of(pt_hi[:, 2, :, :], ("pT", l, 2), "pT", l, 2)
                hi_of(pt_hi[:, 3, :, :], ("pT", l, 3), "pT", l, 3)
                round_to(W + 6)
                hi_of(h_hi[:, 4:6, :], ("o", l, 2), "o", l, 2)
                hi_of(h_hi[:, 6:8, :], ("o", l, 3), "o", l, 3)
                round_to(W + 7)

            def mlp(l):
                for h in range(8):
                    base = F_[("w1", l, h)]
                    round_to(base + 7)
                    for q in range(2):
                        act.wait_ge(*full(("w1", l, h, q)))
                        i = 2 * h + q
                        if i >= 2:
                            act.wait_ge(dve_made, after("dve", "rsq", l, i - 2))
                        nc.scalar.activation(relu[:, q, :], bank(("w1", l, h, q)), ACT.Relu)\
                            .then_inc(act_made, tick("act", "relu", l, i))
                        act.wait_ge(dve_made, after("dve", "rsq", l, i))
                        nc.scalar.activation(r_hi[:, h % 2, 2 * q:2 * q + 2, :],
                                             rsq[:, q, :].rearrange("p (c t) -> p c t", c=2), ACT.Copy)\
                            .then_inc(act_made, tick("act", "r", l, h, q))
                        round_to(base + 6 + q + 2)

            round_to(F_[("V", 0, 0)] + 1)
            for l in range(2):
                m_out = [("out", l, g, q) for g in range(2) for q in range(2)]
                if l == 1:
                    act.wait_ge(*full(("R1",)))
                    nc.scalar.activation(Rrow[:, :], bank(("R1",))[:, 0:T], ACT.Copy)\
                        .then_inc(act_made, tick("act", "Rrow", 1))
                    freed("act", ("R1",))
                    for g in range(2):
                        base = F_[("gate", g)]
                        for q in range(2):
                            act.wait_ge(dve_made, after("dve", "gate", g, q))
                            nc.scalar.activation(sg[:, 2 * q:2 * q + 2, :], sg[:, 2 * q:2 * q + 2, :], ACT.Sigmoid)\
                                .then_inc(act_made, tick("act", "sig", g, q))
                            round_to(base + 4 + 2 * q + 3)
                        round_to(F_[("a", g)] + 9)
                    for g in range(2):
                        for q in range(2):
                            i = 2 * g + q
                            round_to(F_[("bg", g)] + 4 + q + 2)
                            act.wait_ge(dve_made, after("dve", "sc", i))
                            nc.scalar.activation(mh[:, J + 2 * i:J + 2 * i + 2, :],
                                                 sct[:, i % 2, :].rearrange("p (c t) -> p c t", c=2), ACT.Copy)\
                                .then_inc(act_made, tick("act", "mix", 1, J + 2 * i))
                    round_to(F_[("out", 1, "early", 0)] + 1)
                    for k in range(31):
                        if k >= 4:
                            act.wait_ge(pe_made, after("pe", "tap", k - 4))
                        nc.scalar.activation(diag(k), ident[:, :], ACT.Copy, scale=tap(k, J - 1))\
                            .then_inc(act_made, tick("act", "diag", k))
                        if k % 8 == 7:
                            round_to(F_[("out", 1, "early", 0)] + 2 + k // 8)
                    act.wait_ge(*full(("conv7",)))
                    nc.scalar.activation(cv[:, J - 1, :], bank(("conv7",))[:, 0:T], ACT.Identity,
                                         bias=vec("dwb", J - 1)).then_inc(act_made, tick("act", "conv7"))
                    freed("act", ("conv7",))
                    round_to(F_[("out", 1, "early", 1)] + 1)
                    round_to(F_[("out", 1, "early", 1)] + 3)
                    act.wait_ge(*full(("murow",)))
                    nc.scalar.activation(Nrow[:, :], bank(("murow",))[:, 0:T], ACT.Copy)\
                        .then_inc(act_made, tick("act", "murow"))
                    freed("act", ("murow",))
                    for i in range(4):
                        act.wait_ge(dve_made, after("dve", "vc", i))
                        if i >= 2:
                            act.wait_ge(dve_made, after("dve", "Sv", 0 if i == 2 else 1))
                        nc.scalar.activation(sq[:, i % 2, :].rearrange("p (c t) -> p c t", c=2),
                                             cv[:, 2 * i:2 * i + 2, :], ACT.Square)\
                            .then_inc(act_made, tick("act", "vsq", i))
                        if i % 2 == 1:
                            round_to(F_[("out", 1, "early", 1)] + 2 + i // 2 + 2)
                    round_to(F_[("out", 1, "late", 0)] + 1)
                    act.wait_ge(*full(("varrow",)))
                    nc.scalar.activation(Rrow[:, :], bank(("varrow",))[:, 0:T], ACT.Copy)\
                        .then_inc(act_made, tick("act", "varrow"))
                    freed("act", ("varrow",))
                    for c in range(J):
                        act.wait_ge(dve_made, after("dve", "vn", c))
                        nc.scalar.activation(cv[:, c, :], cv[:, c, :], ACT.Silu, bias=vec("lnb", c))\
                            .then_inc(act_made, tick("act", "vs", c))
                        own()
                        nc.scalar.activation(mh[:, c, :], cv[:, c, :], ACT.Copy).then_inc(act_made, tick("act", "mix", 1, c))
                        if c % 2 == 1:
                            round_to(F_[("out", 1, "late", 0)] + c // 2 + 2)
                    for q in range(2):
                        hi_of(k_hi[:, 2 * q:2 * q + 2, :], ("K", 1, 0, q), "K", 1, q)
                def new_h(tag, gl, gs, base):
                    for j in range(J):
                        h_part(tag, gl, gs, j)
                        if j % 2 == 1:
                            i = j // 2
                            if i >= 2:
                                act.wait_ge(pool_made, after("pool", "Sx", tag, 0 if i == 2 else 1))
                            nc.scalar.activation(sq[:, i % 2, :].rearrange("p (c t) -> p c t", c=2),
                                                 xT[:, j - 1:j + 1, :], ACT.Square)\
                                .then_inc(act_made, tick("act", "xsq", tag, i))
                            round_to(base + i + 2)

                def boundary(n, m, tag, gl, gs, nxt):
                    fill = FILL.get((l, n))
                    x = nxt - 4 if fill else nxt
                    round_to(x + 1)
                    for i in range(4):
                        act.wait_ge(*full(m[i]))
                        if i >= 2:
                            act.wait_ge(dve_made, after("dve", "Ssum", l, n, 1 if i == 2 else 2))
                        nc.scalar.activation(sq[:, i % 2, :].rearrange("p (c t) -> p c t", c=2), bank2(m[i]),
                                             ACT.Square).then_inc(act_made, tick("act", "nsq", l, n, i))
                        if i == 1:
                            round_to(x + 3)
                    if fill:
                        round_to(nxt + 2)
                    act.wait_ge(*full(("nrow", l, n)))
                    nc.scalar.activation(Nrow[:, :], bank(("nrow", l, n))[:, 0:T], ACT.Copy)\
                        .then_inc(act_made, tick("act", "Nrow", l, n))
                    freed("act", ("nrow", l, n))
                    round_to(nxt + 3)
                    if tag:
                        new_h(tag, gl, gs, nxt)
                    if fill:
                        for q in range(2):
                            hi_of(fill_dst(fill, q)[0], fill + (q,), *fill_name(fill, q))

                boundary(0, m_out, f"q{l}", l, 2, F_[("q", l, 0)])
                attention(l)
                round_to(F_[("wo", l, "late", 1)] + 1)
                boundary(1, [("wo", l, g, q) for g in range(2) for q in range(2)], f"mlp{l}", l, 4, F_[("w1", l, 0)])
                mlp(l)
                round_to(F_[("w2", l, 7, 1)] + 1)
                m = [("w2", l, g, q) for g in range(2) for q in range(2)]
                if l == 0:
                    boundary(2, m, "in1", 1, 0, F_[("gate", 0)])
                    round_to(F_[("gate", 0)] + 5)
            for g in range(2):
                for t in range(TT):
                    act.wait_ge(*full(("xout", g, t)))
                    nc.scalar.activation(otok[:, t, 512 * g:512 * g + 512], bank(("xout", g, t)), ACT.Copy)\
                        .then_inc(act_made, tick("act", "xout", g, t))
                    freed("act", ("xout", g, t))
            for g in range(2):
                for i in (2 * g, 2 * g + 1):
                    act.wait_ge(*full(m[i]))
                    if g:
                        act.wait_ge(dve_made, after("dve", "Ssum", 1, 2, i - 1))
                    nc.scalar.activation(sq[:, i % 2, :].rearrange("p (c t) -> p c t", c=2), bank2(m[i]), ACT.Square)\
                        .then_inc(act_made, tick("act", "nsq", 1, 2, i))
                for i in (2 * g, 2 * g + 1):
                    for c in range(2):
                        j = 2 * i + c
                        nc.scalar.activation(mg[:, j, :], bank2(m[i])[:, c, :], ACT.Copy, scale=gain(1, 5, j))\
                            .then_inc(act_made, tick("act", "mg", j))
                    freed("act", m[i])

        @block.vector
        def _(dve):
            V = nc.vector
            nu = [0]

            def low_to(u):
                while nu[0] <= min(u, NU - 1):
                    v = nu[0]
                    if not pool_lo[v]:
                        dve.wait_ge(hi_ready, v + 1)
                        V.tensor_tensor(w_lo[:, v % SLOTS, :, :], raw[:, v % SLOTS, :, :], f(w_hi[:, v % SLOTS, :, :]),
                                        ALU.subtract).then_inc(lo_ready_dve, 1)
                    nu[0] += 1

            def own():
                dve.wait_ge(dve_made, now("dve"))

            F_ = first

            def low_h(tag, l, s, j):
                dve.wait_ge(act_made, after("act", "h", tag, j))
                V.scalar_tensor_tensor(out=h_lo[:, j, :], in0=xT[:, j, :], scalar=gain(l, s, j), in1=f(h_hi[:, j, :]),
                                       op0=ALU.mult, op1=ALU.subtract).then_inc(dve_made, tick("dve", "h", tag, j))

            V.memset(mhalf[:, :], -0.5).then_inc(dve_made, tick("dve", "mhalf"))
            V.memset(upad[:, :, :, 0:3], 0.0).then_inc(dve_made, tick("dve"))
            V.memset(pu[:, :, 0:16], 0.0).then_inc(dve_made, tick("dve", "pads"))
            for i in range(4):
                dve.wait_ge(*full(("xT", i)))
                V.tensor_copy(xT[:, 2 * i:2 * i + 2, :], bank2(("xT", i))).then_inc(dve_made, tick("dve", "xTc", i))
                freed("dve", ("xT", i))
                for c in range(2):
                    L.also("dve", "x", "in0", 2 * i + c)
            dve.wait_ge(act_made, after("act", "gains"))
            low_to(0)
            for j in range(J):
                low_h("in0", 0, 0, j)
                if j % 2 == 1:
                    low_to(j // 2 + 1)
            for t in range(TT):
                dve.wait_ge(act_made, after("act", "ss0", t))
            V.tensor_scalar(stat[:, 1, 0:2], stat[:, 0, 0:2], 1.0 / D, RMS_EPS, ALU.mult, ALU.add)\
                .then_inc(dve_made, tick("dve", "v0"))
            dve.wait_ge(ssm_landed, 16 * 6)
            for j in range(J):
                V.tensor_scalar(wdtg[:, j, :], wdt[:, j, :], gain(0, 0, j), None, ALU.mult)\
                    .then_inc(dve_made, tick("dve", *(("wdtg",) if j == J - 1 else ())))

            def scaled(dst, label, row, *name):
                dve.wait_ge(*full(label))
                V.tensor_tensor(dst, bank2(label), row2(row), ALU.mult)\
                    .then_inc(dve_made, tick("dve", *name))
                freed("dve", label)

            def low_of(dst, hi, label, *name):
                dve.wait_ge(act_made, after("act", *name))
                src = bank2(label) if len(dst.shape) == 3 else bank(label)
                V.tensor_tensor(dst, src, f(hi), ALU.subtract).then_inc(dve_made, tick("dve", *name))
                freed("dve", label)

            dve.wait_ge(act_made, after("act", "Rrow", 0))

            def conv4(i):
                for k in range(4):
                    own()
                    for c in range(2):
                        j = 2 * i + c
                        src = upad[:, i % 2, c, k:k + T]
                        if k == 0:
                            V.tensor_scalar(xc[:, j, :], src, vec("convw", k * 12 + j), vec("convb", j),
                                            ALU.mult, ALU.add).then_inc(dve_made, tick("dve"))
                        else:
                            V.scalar_tensor_tensor(out=xc[:, j, :], in0=src, scalar=vec("convw", k * 12 + j),
                                                   in1=xc[:, j, :], op0=ALU.mult, op1=ALU.add)\
                                .then_inc(dve_made, tick("dve", *(("conv", i) if k == 3 and c == 1 else ())))

            low_to(F_[("xbc", 0)] + 3)

            def scaled_u(i):
                if i >= 2:
                    dve.wait_ge(dve_made, after("dve", "conv", i - 2))
                scaled(upad[:, i % 2, :, 3:3 + T], ("xbc", i // 2, i % 2), Rrow, "u", i)

            low_to(F_[("xbc", 1)] + 1)
            for i in range(2):
                scaled_u(i)
            dve.wait_ge(act_made, after("act", "vecs"))
            conv4(0)
            low_to(F_[("xbc", 1)] + 3)
            conv4(1)
            low_to(F_[("xbc", 2)])
            for i in range(2, 4):
                scaled_u(i)
            dve.wait_ge(*full(("dtT",)))
            for t in range(TT):
                V.scalar_tensor_tensor(out=sp[:, 0, t * HEADS:(t + 1) * HEADS],
                                       in0=bank(("dtT",))[:, t * HEADS:(t + 1) * HEADS], scalar=rfac[:, 0, t:t + 1],
                                       in1=dtb[:, :], op0=ALU.mult, op1=ALU.add)\
                    .then_inc(dve_made, tick("dve", *(("dtv",) if t == TT - 1 else ())))
            freed("dve", ("dtT",))
            for i in range(4):
                low_of(mem_lo[:, 2 * i:2 * i + 2, :], mem_hi[:, 2 * i:2 * i + 2, :], ("memT", i), "mem", i)
            low_to(F_[("xbc", 2)] + 3)
            conv4(2)
            low_to(F_[("z", 0)] + 1)
            conv4(3)
            dve.wait_ge(dve_made, after("dve", "dtv"))
            V.scalar_tensor_tensor(out=sp[:, 1, :], in0=sp[:, 0, :], scalar=-1.0, in1=sp[:, 0, :],
                                   op0=ALU.mult, op1=ALU.max).then_inc(dve_made, tick("dve", "spabs"))
            dve.wait_ge(act_made, after("act", "spexp"))
            V.tensor_scalar(sp[:, 3, :], sp[:, 2, :], 1.0, None, ALU.add).then_inc(dve_made, tick("dve", "sp1"))
            own()
            V.tensor_scalar(sp[:, 5, :], sp[:, 3, :], -1.0, None, ALU.add).then_inc(dve_made, tick("dve"))
            own()
            V.tensor_scalar(sp[:, 6, :], sp[:, 5, :], 0.0, None, ALU.is_equal).then_inc(dve_made, tick("dve"))
            own()
            V.tensor_tensor(sp[:, 5, :], sp[:, 5, :], sp[:, 6, :], ALU.add).then_inc(dve_made, tick("dve"))
            own()
            V.reciprocal(sp[:, 7, :], sp[:, 5, :]).then_inc(dve_made, tick("dve"))
            dve.wait_ge(act_made, after("act", "spln"))
            V.tensor_tensor(sp[:, 4, :], sp[:, 4, :], sp[:, 6, :], ALU.add).then_inc(dve_made, tick("dve"))
            own()
            V.tensor_tensor(sp[:, 4, :], sp[:, 4, :], sp[:, 7, :], ALU.mult).then_inc(dve_made, tick("dve"))
            own()
            V.tensor_tensor(sp[:, 4, :], sp[:, 4, :], sp[:, 2, :], ALU.mult).then_inc(dve_made, tick("dve"))
            own()
            V.scalar_tensor_tensor(out=sp[:, 8, :], in0=sp[:, 0, :], scalar=0.0, in1=sp[:, 4, :],
                                   op0=ALU.max, op1=ALU.add).then_inc(dve_made, tick("dve", "dt"))
            own()
            dve.wait_ge(act_made, after("act", "expA"))
            dt_ = sp[:, 8, :].rearrange("p (t h) -> p t h", t=TT)
            V.scalar_tensor_tensor(out=sp[:, 9, :].rearrange("p (t h) -> p t h", t=TT), in0=dt_, scalar=-1.0,
                                   in1=expA[:, :].unsqueeze(1).broadcast_to([P, TT, HEADS]),
                                   op0=ALU.mult, op1=ALU.mult).then_inc(dve_made, tick("dve", "dA"))
            low_to(F_[("z", 0)] + 2)
            for i in range(4, 6):
                scaled_u(i)
            for i in range(4, 6):
                conv4(i)
                low_to(F_[("z", 0)] + i - 1)
            dve.wait_ge(*full(("cs",)))
            V.tensor_copy(cs[:, 0:3, :], bank(("cs",))[:, 0:3 * HEADS].rearrange("p (a h) -> p a h", a=3))\
                .then_inc(dve_made, tick("dve"))
            freed("dve", ("cs",))
            own()
            V.tensor_tensor(cs[:, 3, :], cs[:, 0, :], cs[:, 2, :], ALU.subtract).then_inc(dve_made, tick("dve", "cs"))
            low_to(F_[("z", 1)] + 2)
            for i in range(2):
                scaled(zs[:, 2 * i:2 * i + 2, :], ("z", 0, i), Rrow, "z", i)
            for i in range(4):
                t, q = i // 2, i % 2
                dve.wait_ge(*full(("xsT", i)))
                V.tensor_tensor(xdt[:, t, q * 512:(q + 1) * 512].rearrange("p (h c) -> p h c", c=64),
                                bank(("xsT", i)).rearrange("p (h c) -> p h c", c=64),
                                dt_[:, t, 8 * q:8 * q + 8].unsqueeze(2).broadcast_to([P, 8, 64]), ALU.mult)\
                    .then_inc(dve_made, tick("dve", "xdt", i))
                freed("dve", ("xsT", i))
                low_to(F_[("z", 1)] + i + 2)
            low_to(F_[("pool", 0)] + 2)
            for i in range(2, 4):
                scaled(zs[:, 2 * i:2 * i + 2, :], ("z", 1, i - 2), Rrow, "z", i)
            low_to(F_[("pool", 0)] + 3)
            dve.wait_ge(pool_made, after("pool", "cbmask"))
            for g in range(2):
                dve.wait_ge(*full(("cb", g)))
                V.tensor_tensor(cbm[:, g, :], bank(("cb", g))[:, 0:3 * P], cbmask[:, :], ALU.mult)\
                    .then_inc(dve_made, tick("dve", "cbm", g))
                freed("dve", ("cb", g))
                low_to(F_[("pool", 0)] + 2 + g + 2)
            low_to(F_[("K", 0, 0)] + 2)
            for i in range(2):
                scaled(pu[:, 2 * i:2 * i + 2, 16:16 + T], ("pool", 0, i), Rrow, "pu", i)
            low_to(F_[("K", 0, 0)] + 3)

            def gate_y(i):
                dve.wait_ge(*full(("y", i)))
                dve.wait_ge(act_made, after("act", "z", i))
                if i:
                    dve.wait_ge(dve_made, after("dve", "yg", i - 1))
                for c in range(2):
                    j = 2 * i + c
                    V.scalar_tensor_tensor(out=tmp[:, c, :], in0=xc[:, j, :], scalar=dskip[:, j:j + 1],
                                           in1=bank2(("y", i))[:, c, :], op0=ALU.mult, op1=ALU.add)\
                        .then_inc(dve_made, tick("dve"))
                freed("dve", ("y", i))
                own()
                V.tensor_tensor(zs[:, 2 * i:2 * i + 2, :], zs[:, 2 * i:2 * i + 2, :], tmp[:, :, :], ALU.mult)\
                    .then_inc(dve_made, tick("dve", "yg", i))

            def group_sum(g):
                dve.wait_ge(act_made, after("act", "ysq", 2 * g + 1))
                V.tensor_tensor(Ssum[:, :], sq[:, 0, :], sq[:, 1, :], ALU.add).then_inc(dve_made, tick("dve"))
                own()
                V.tensor_tensor(Sg[:, g, :], Ssum[:, 0:T], Ssum[:, T:H2], ALU.add)\
                    .then_inc(dve_made, tick("dve", "Sg", g))

            for i in range(9):
                if i < 8:
                    dve.wait_ge(*full(("rows", i)))
                    for hh in range(2):
                        h = 2 * i + hh
                        if h >= 4:
                            dve.wait_ge(pe_made, after("pe", "head", h - 4))
                        r = bank2(("rows", i))[:, hh, :]
                        for dst, src, c in ((0, 0, 0), (P, P, 3), (2 * P, P, 1)):
                            V.tensor_scalar(E[:, h % 4, dst:dst + P], r[:, src:src + P], cs[:, c, h:h + 1], 0.0,
                                            ALU.subtract, ALU.min)\
                                .then_inc(dve_made, tick("dve", *(("E", h) if dst == 2 * P else ())))
                    freed("dve", ("rows", i))
                if i >= 1:
                    low_to(F_[("K", 0, 0)] + k_ahead[i - 1])
                    for h in (2 * i - 2, 2 * i - 1):
                        dve.wait_ge(act_made, after("act", "E", h))
                        V.tensor_tensor(E[:, h % 4, :], E[:, h % 4, :], cbm[:, h // 8, :], ALU.mult)\
                            .then_inc(dve_made, tick("dve", "EC", h))
                if i == 4:
                    for q in range(2):
                        low_of(k_lo[:, 2 * q:2 * q + 2, :], k_hi[:, 2 * q:2 * q + 2, :], ("K", 0, 0, q), "K", 0, q)
                if i in (5, 6):
                    gate_y(i - 5)
                if i == 7:
                    group_sum(0)
            for q in range(2):
                low_of(k_lo[:, 4 + 2 * q:6 + 2 * q, :], k_hi[:, 4 + 2 * q:6 + 2 * q, :], ("K", 0, 1, q), "K", 0, 2 + q)
            for g in range(4):
                dve.wait_ge(act_made, after("act", "mp", g | 1))
                V.scalar_tensor_tensor(out=mp_lo[:, g, :], in0=bank2(("pooled", g // 2))[:, g % 2, :],
                                       scalar=vec("pscale", g), in1=f(mp_hi[:, g, :]), op0=ALU.mult,
                                       op1=ALU.subtract).then_inc(dve_made, tick("dve", "mix", 0, g))
                if g % 2 == 1:
                    freed("dve", ("pooled", g // 2))
            gate_y(2)
            gate_y(3)
            group_sum(1)
            low_to(F_[("out", 0, "early", 1)] + 3)
            dve.wait_ge(*full(("gstat",)))
            V.tensor_scalar(stat[:, 8, 0:4], bank(("gstat",))[:, 0:4], 2.0 / D, RMS_EPS, ALU.mult, ALU.add)\
                .then_inc(dve_made, tick("dve", "gv"))
            freed("dve", ("gstat",))
            dve.wait_ge(act_made, after("act", "Rg"))
            for c in range(J):
                V.scalar_tensor_tensor(out=zs[:, c, :], in0=zs[:, c, :], scalar=vec("ssmn", c), in1=Rg[:, c // 4, :],
                                       op0=ALU.mult, op1=ALU.mult).then_inc(dve_made, tick("dve", "yn", c))
                if c >= 1:
                    dve.wait_ge(act_made, after("act", "mix", 0, 4 + c - 1))
                    V.tensor_tensor(my_lo[:, c - 1, :], zs[:, c - 1, :], f(my_hi[:, c - 1, :]), ALU.subtract)\
                        .then_inc(dve_made, tick("dve", "mix", 0, 4 + c - 1))
                if c % 2 == 1:
                    low_to(F_[("out", 0, "late", 0)] + c // 2 + 2)
            dve.wait_ge(act_made, after("act", "mix", 0, 4 + J - 1))
            V.tensor_tensor(my_lo[:, J - 1, :], zs[:, J - 1, :], f(my_hi[:, J - 1, :]), ALU.subtract)\
                .then_inc(dve_made, tick("dve", "mix", 0, 4 + J - 1))

            def norm_sum(l, n, m):
                dve.wait_ge(act_made, after("act", "nsq", l, n, 1))
                V.tensor_tensor(Ssum[:, :], sq[:, 0, :], sq[:, 1, :], ALU.add)\
                    .then_inc(dve_made, tick("dve", "Ssum", l, n, 1))
                L.also("dve", "Ssum", l, n, 2)
                for i in (2, 3):
                    dve.wait_ge(act_made, after("act", "nsq", l, n, i))
                    own()
                    V.tensor_tensor(Ssum[:, :], Ssum[:, :], sq[:, i % 2, :], ALU.add).then_inc(dve_made, tick("dve"))
                own()
                V.tensor_tensor(S2[:, :], Ssum[:, 0:T], Ssum[:, T:H2], ALU.add).then_inc(dve_made, tick("dve", "S2", l, n))

            def factor(l, n):
                dve.wait_ge(*full(("nstat", l, n)))
                s_ = 1 + 3 * l + n
                if n < 2:
                    V.tensor_scalar(stat[:, s_, 0:2], bank(("nstat", l, n))[:, 0:2], 1.0 / D, RMS_EPS,
                                    ALU.mult, ALU.add).then_inc(dve_made, tick("dve", "nv", l, n))
                else:
                    dve.wait_ge(pool_made, after("pool", "r4", l))
                    V.tensor_scalar(stat[:, s_, 2:4], bank(("nstat", l, n))[:, 0:2], 1.0 / D, None, ALU.mult)\
                        .then_inc(dve_made, tick("dve"))
                    own()
                    V.tensor_tensor(stat[:, s_, 4:6], stat[:, s_, 2:4], rfac[:, 13 + l, 4:6], ALU.mult)\
                        .then_inc(dve_made, tick("dve"))
                    own()
                    V.tensor_scalar(stat[:, s_, 0:2], stat[:, s_, 4:6], RMS_EPS, None, ALU.add)\
                        .then_inc(dve_made, tick("dve", "nv", l, n))
                freed("dve", ("nstat", l, n))

            def new_x(l, n, m, tag, gl, gs):
                dve.wait_ge(act_made, after("act", "Nrow", l, n))
                for j in range(J + 2):
                    if j < J:
                        if j >= 2:
                            dve.wait_ge(dve_made, after("dve", "x", tag, j - 2))
                        V.scalar_tensor_tensor(out=tmp[:, j % 2, :], in0=bank2(m[j // 2])[:, j % 2, :],
                                               scalar=gain(l, 2 * n + 1, j), in1=Nrow[:, :], op0=ALU.mult,
                                               op1=ALU.mult).then_inc(dve_made, tick("dve", "dx", l, n, j))
                        if j % 2 == 1:
                            freed("dve", m[j // 2])
                    if 1 <= j <= J:
                        dve.wait_ge(dve_made, after("dve", "dx", l, n, j - 1))
                        V.tensor_tensor(xT[:, j - 1, :], xT[:, j - 1, :], tmp[:, (j - 1) % 2, :], ALU.add)\
                            .then_inc(dve_made, tick("dve", "x", tag, j - 1))
                    if j >= 2:
                        low_h(tag, gl, gs, j - 2)

            def boundary(l, n, m, tag, gl, gs, nxt):
                fill = FILL.get((l, n))
                x = nxt - 4 if fill else nxt
                low_to(x + 1 if fill else x)
                norm_sum(l, n, m)
                if fill:
                    low_to(nxt - 1)
                factor(l, n)
                low_to(nxt + 2)
                new_x(l, n, m, tag, gl, gs)
                if tag:
                    low_to(nxt + 4)
                if fill:
                    for q in range(2):
                        hi, lo = fill_dst(fill, q)
                        low_of(lo, hi, fill + (q,), *fill_name(fill, q))

            def x_factor(label, s_, *name):
                dve.wait_ge(*full(label))
                V.tensor_scalar(stat[:, s_, 0:2], bank(label)[:, 0:2], 1.0 / D, RMS_EPS, ALU.mult, ALU.add)\
                    .then_inc(dve_made, tick("dve", *name))
                freed("dve", label)

            cur = [0]

            def conv31(n):
                for _ in range(n):
                    if cur[0] >= 31 * J:
                        return
                    if cur[0] >= 186 and cur[0] % 2:
                        cur[0] += 1
                        continue
                    i, k, c = cur[0] // 62, cur[0] % 62 // 2, cur[0] % 2
                    j = 2 * i + c
                    acc = ps[:, 6, c * T:(c + 1) * T]
                    src = vpad[:, j, k:k + T]
                    if k == 0:
                        dve.wait_ge(dve_made, after("dve", "v", i))
                        if i:
                            dve.wait_ge(dve_made, L.at[("dve", "tap", cur[0] - 2)])
                        V.tensor_scalar(acc, src, tap(k, j), vec("dwb", j), ALU.mult, ALU.add)\
                            .then_inc(dve_made, tick("dve", "tap", cur[0]))
                    else:
                        dve.wait_ge(dve_made, L.at[("dve", "tap", cur[0] - 2)])
                        V.scalar_tensor_tensor(out=acc if k < 30 else cv[:, j, :], in0=src, scalar=tap(k, j), in1=acc,
                                               op0=ALU.mult, op1=ALU.add)\
                            .then_inc(dve_made, tick("dve", "tap", cur[0]))
                    cur[0] += 1
                    if cur[0] in (124, 186):
                        own()
                        i = cur[0] // 62
                        V.tensor_tensor(Ssum[:, :].rearrange("p (c t) -> p c t", c=2),
                                        cv[:, 0:2, :] if i == 2 else Ssum[:, :].rearrange("p (c t) -> p c t", c=2),
                                        cv[:, 2 * i - 2:2 * i, :], ALU.add).then_inc(dve_made, tick("dve"))

            def attention(l):
                W = F_[("wo", l, "early", 0)]
                end = F_[("q", l, 1)] + 4
                low_to(F_[("q", l, 1)] + 3)
                for h in range(2):
                    low_of(q_lo[:, 2 * h:2 * h + 2, :], q_hi[:, 2 * h:2 * h + 2, :], ("q", l, 0, h), "q", l, h)
                x_factor(("astat", l), 7, "av", l)
                dve.wait_ge(pool_made, after("pool", "ar", l))
                V.tensor_scalar(rfac[:, 11 + l, 2:4], rfac[:, 11 + l, 0:2], XA_SCALE, None, ALU.mult)\
                    .then_inc(dve_made, tick("dve"))
                V.tensor_scalar(rfac[:, 11 + l, 4:6], rfac[:, 11 + l, 0:2], -XA_SCALE, None, ALU.mult)\
                    .then_inc(dve_made, tick("dve"))
                low_to(end + 1)

                def maxes(h):
                    dve.wait_ge(*full(("scores", l, h)))
                    V.tensor_reduce(stat[:, 8 + h, 0:2], bank2(("scores", l, h)), AX.X, ALU.max)\
                        .then_inc(dve_made, tick("dve"))
                    own()
                    V.tensor_tensor(stat[:, 8 + h, 2:4], stat[:, 8 + h, 0:2], rfac[:, 11 + l, 4:6], ALU.mult)\
                        .then_inc(dve_made, tick("dve", "nmax", l, h))

                def probs(h):
                    for t in range(TT):
                        dve.wait_ge(act_made, after("act", "exp", l, h, t))
                    V.reciprocal(stat[:, 8 + h, 6:8], stat[:, 8 + h, 4:6]).then_inc(dve_made, tick("dve"))
                    own()
                    for t in range(TT):
                        V.tensor_scalar(prob[:, h, t, :], prob[:, h, t, :], stat[:, 8 + h, 6 + t:7 + t], None, ALU.mult)\
                            .then_inc(dve_made, tick("dve", *(("prob", l, h) if t == TT - 1 else ())))

                def low_o(h):
                    low_of(h_lo[:, 2 * h:2 * h + 2, :], h_hi[:, 2 * h:2 * h + 2, :], ("o", l, h), "o", l, h)

                def low_pt(h):
                    low_of(pt_lo[:, h, :, :], pt_hi[:, h, :, :], ("pT", l, h), "pT", l, h)

                maxes(0)
                maxes(1)
                low_to(end + 2)
                probs(0)
                low_to(end + 3)
                probs(1)
                for h in range(2, 4):
                    low_of(q_lo[:, 2 * h:2 * h + 2, :], q_hi[:, 2 * h:2 * h + 2, :], ("q", l, 1, h - 2), "q", l, h)
                low_pt(0)
                low_pt(1)
                if l == 0:
                    low_to(end + 7)
                maxes(2)
                maxes(3)
                if l == 1:
                    low_to(end + 4)
                    low_o(0)
                    probs(2)
                    low_o(1)
                    probs(3)
                    low_to(end + 5)
                else:
                    probs(2)
                    low_o(0)
                    probs(3)
                    low_o(1)
                if l == 0:
                    for t in range(TT):
                        low_of(v_lo[:, t, 512:1024], v_hi[:, t, 512:1024], ("V", 0, 1, t), "V", 0, 1, t)
                    low_to(W + 5)
                low_pt(2)
                low_pt(3)
                low_to(W + 6)
                low_o(2)
                low_o(3)
                low_to(W + 7)

            def mlp(l):
                for h in range(8):
                    base = F_[("w1", l, h)]
                    low_to(base + 7)
                    for q in range(2):
                        i = 2 * h + q
                        dve.wait_ge(act_made, after("act", "relu", l, i))
                        if i >= 2:
                            dve.wait_ge(dve_made, after("dve", "r", l, h - 1, q))
                        V.scalar_tensor_tensor(out=rsq[:, q, :], in0=bank(("w1", l, h, q)), scalar=0.0,
                                               in1=relu[:, q, :], op0=ALU.max, op1=ALU.mult)\
                            .then_inc(dve_made, tick("dve", "rsq", l, i))
                        freed("dve", ("w1", l, h, q))
                        if q == 1:
                            low_r(l, h, 0)
                    low_r(l, h, 1)
                    if h == 0:
                        x_factor(("hstat", l), 15, "hv", l)
                    low_to(base + 9)

            def low_r(l, h, q):
                dve.wait_ge(act_made, after("act", "r", l, h, q))
                V.tensor_tensor(r_lo[:, h % 2, 2 * q:2 * q + 2, :], rsq[:, q, :].rearrange("p (c t) -> p c t", c=2),
                                f(r_hi[:, h % 2, 2 * q:2 * q + 2, :]), ALU.subtract)\
                    .then_inc(dve_made, tick("dve", "r", l, h, q))

            for l in range(2):
                if l == 1:
                    x_factor(("xstat", 0), 7, "r1v")
                    dve.wait_ge(act_made, after("act", "Rrow", 1))
                    V.tensor_tensor(Rsq[:, :], Rrow[:, :], Rrow[:, :], ALU.mult).then_inc(dve_made, tick("dve", "Rsq"))
                    V.memset(vpad[:, :, 0:30], 0.0).then_inc(dve_made, tick("dve"))
                    V.memset(ppad[:, :, :, 0:2], 0.0).then_inc(dve_made, tick("dve"))
                    own()
                    for g in range(2):
                        for q in range(2):
                            scaled(sg[:, 2 * q:2 * q + 2, :], ("gate", g, q), Rrow, "gate", g, q)
                            low_to(F_[("gate", g)] + 4 + 2 * q + 2)
                            if g == 1:
                                conv31(8)
                            low_to(F_[("gate", g)] + 4 + 2 * q + 3)
                            if g == 1:
                                conv31(8)
                        for q in range(2):
                            i = 2 * g + q
                            dve.wait_ge(pool_made, after("pool", "sg", g, q))
                            dve.wait_ge(*full(("a", g, q)))
                            V.tensor_tensor(vpad[:, 2 * i:2 * i + 2, 30:30 + T], bank2(("a", g, q)),
                                            sg[:, 2 * q:2 * q + 2, :], ALU.mult).then_inc(dve_made, tick("dve", "v", i))
                            freed("dve", ("a", g, q))
                            low_to(F_[("a", g)] + 4 + 2 * q + 2)
                            conv31(6)
                            low_to(F_[("a", g)] + 4 + 2 * q + 3)
                            conv31(6)
                    for g in range(2):
                        for q in range(2):
                            scaled(sg[:, 2 * q:2 * q + 2, :], ("cg", g, q), Rsq, "cg", g, q)
                            conv31(8 + 5 * g)
                            low_to(F_[("cg", g)] + 4 + 2 * q + 3)
                        for q in range(2):
                            i = 2 * g + q
                            own()
                            dve.wait_ge(*full(("hh", g, q)))
                            V.tensor_tensor(ppad[:, i % 2, :, 2:2 + T], bank2(("hh", g, q)),
                                            sg[:, 2 * q:2 * q + 2, :], ALU.mult).then_inc(dve_made, tick("dve"))
                            freed("dve", ("hh", g, q))
                            for k in range(3):
                                own()
                                for c in range(2):
                                    j = 2 * i + c
                                    src = ppad[:, i % 2, c, k:k + T]
                                    if k == 0:
                                        V.tensor_scalar(cv3[:, j, :], src, vec("scw", k * J + j), None, ALU.mult)\
                                            .then_inc(dve_made, tick("dve"))
                                    else:
                                        V.scalar_tensor_tensor(out=cv3[:, j, :], in0=src, scalar=vec("scw", k * J + j),
                                                               in1=cv3[:, j, :], op0=ALU.mult, op1=ALU.add)\
                                            .then_inc(dve_made, tick("dve", *(("cv3", i) if k == 2 and c == 1 else ())))
                            low_to(F_[("hh", g)] + 4 + 2 * q + 2)
                            conv31(5)
                            low_to(F_[("hh", g)] + 4 + 2 * q + 3)
                    for g in range(2):
                        for q in range(2):
                            i = 2 * g + q
                            dve.wait_ge(*full(("bg", g, q)))
                            dve.wait_ge(pool_made, after("pool", "cv3R", i))
                            if i >= 2:
                                dve.wait_ge(act_made, after("act", "mix", 1, J + 2 * (i - 2)))
                            V.tensor_tensor(sct[:, i % 2, :].rearrange("p (c t) -> p c t", c=2), bank2(("bg", g, q)),
                                            cv3[:, 2 * i:2 * i + 2, :], ALU.mult).then_inc(dve_made, tick("dve", "sc", i))
                            freed("dve", ("bg", g, q))
                            conv31(5)
                            dve.wait_ge(act_made, after("act", "mix", 1, J + 2 * i))
                            V.tensor_tensor(ml[:, J + 2 * i:J + 2 * i + 2, :],
                                            sct[:, i % 2, :].rearrange("p (c t) -> p c t", c=2),
                                            f(mh[:, J + 2 * i:J + 2 * i + 2, :]), ALU.subtract)\
                                .then_inc(dve_made, tick("dve", "mix", 1, J + 2 * i))
                            L.also("dve", "mix", 1, J + 2 * i + 1)
                            conv31(4 + 2 * q)
                            low_to(F_[("bg", g)] + 4 + 2 * q + 3)
                    for u in range(F_[("K", 1, 0, "early")], F_[("out", 1, "early", 0)] + 4):
                        low_to(u)
                        conv31(6)
                    conv31(31 * J)
                    own()
                    dve.wait_ge(act_made, after("act", "conv7"))
                    V.tensor_tensor(Ssum[:, :].rearrange("p (c t) -> p c t", c=2),
                                    Ssum[:, :].rearrange("p (c t) -> p c t", c=2), cv[:, 6:8, :], ALU.add)\
                        .then_inc(dve_made, tick("dve"))
                    own()
                    V.tensor_tensor(S2[:, :], Ssum[:, 0:T], Ssum[:, T:H2], ALU.add).then_inc(dve_made, tick("dve", "S2", "mu"))
                    low_to(F_[("out", 1, "early", 1)] + 2)
                    dve.wait_ge(*full(("mustat",)))
                    V.tensor_scalar(rfac[:, 9, 0:2], bank(("mustat",))[:, 0:2], 1.0 / D, None, ALU.mult)\
                        .then_inc(dve_made, tick("dve", "negmu"))
                    freed("dve", ("mustat",))
                    low_to(F_[("out", 1, "early", 1)] + 3)
                    dve.wait_ge(act_made, after("act", "murow"))
                    for i in range(4):
                        V.tensor_tensor(cv[:, 2 * i:2 * i + 2, :], cv[:, 2 * i:2 * i + 2, :], row2(Nrow), ALU.subtract)\
                            .then_inc(dve_made, tick("dve", "vc", i))
                    dve.wait_ge(act_made, after("act", "vsq", 1))
                    V.tensor_tensor(Ssum[:, :], sq[:, 0, :], sq[:, 1, :], ALU.add).then_inc(dve_made, tick("dve", "Sv", 0))
                    L.also("dve", "Sv", 1)
                    low_to(F_[("out", 1, "early", 1)] + 4)
                    for i in (2, 3):
                        dve.wait_ge(act_made, after("act", "vsq", i))
                        own()
                        V.tensor_tensor(Ssum[:, :], Ssum[:, :], sq[:, i % 2, :], ALU.add).then_inc(dve_made, tick("dve"))
                    own()
                    V.tensor_tensor(S2[:, :], Ssum[:, 0:T], Ssum[:, T:H2], ALU.add)\
                        .then_inc(dve_made, tick("dve", "S2", "var"))
                    low_to(F_[("out", 1, "late", 0)] + 2)
                    dve.wait_ge(*full(("varstat",)))
                    V.tensor_scalar(stat[:, 9, 0:2], bank(("varstat",))[:, 0:2], 1.0 / D, LN_EPS, ALU.mult, ALU.add)\
                        .then_inc(dve_made, tick("dve", "lnv"))
                    freed("dve", ("varstat",))
                    low_to(F_[("out", 1, "late", 0)] + 3)
                    dve.wait_ge(act_made, after("act", "varrow"))
                    for c in range(J + 1):
                        if c < J:
                            V.scalar_tensor_tensor(out=cv[:, c, :], in0=cv[:, c, :], scalar=vec("lng", c), in1=Rrow[:, :],
                                                   op0=ALU.mult, op1=ALU.mult).then_inc(dve_made, tick("dve", "vn", c))
                        if c >= 1:
                            dve.wait_ge(act_made, after("act", "mix", 1, c - 1))
                            V.tensor_tensor(ml[:, c - 1, :], cv[:, c - 1, :], f(mh[:, c - 1, :]), ALU.subtract)\
                                .then_inc(dve_made, tick("dve", "mix", 1, c - 1))
                        if c % 2 == 1:
                            low_to(F_[("out", 1, "late", 0)] + c // 2 + 3)
                    for q in range(2):
                        low_of(k_lo[:, 2 * q:2 * q + 2, :], k_hi[:, 2 * q:2 * q + 2, :], ("K", 1, 0, q), "K", 1, q)
                m = [("out", l, g, q) for g in range(2) for q in range(2)]
                boundary(l, 0, m, f"q{l}", l, 2, F_[("q", l, 0)])
                attention(l)
                boundary(l, 1, [("wo", l, g, q) for g in range(2) for q in range(2)], f"mlp{l}", l, 4,
                         F_[("w1", l, 0)])
                mlp(l)
                m = [("w2", l, g, q) for g in range(2) for q in range(2)]
                if l == 0:
                    boundary(0, 2, m, "in1", 1, 0, F_[("gate", 0)])
            low_to(NU)
            norm_sum(1, 2, m)
            factor(1, 2)
            dve.wait_ge(pool_made, after("pool", "nr", 1, 2))
            for i in range(4):
                g, t = i // 2, i % 2
                dve.wait_ge(*full(("mout", g, t)))
                dve.wait_ge(act_made, after("act", "xout", g, t))
                V.scalar_tensor_tensor(out=otok[:, t, 512 * g:512 * g + 512], in0=bank(("mout", g, t)),
                                       scalar=rfac[:, 6, t:t + 1], in1=otok[:, t, 512 * g:512 * g + 512],
                                       op0=ALU.mult, op1=ALU.add).then_inc(dve_made, tick("dve", "otok", i))

        @block.gpsimd
        def _(pool):
            G = nc.gpsimd
            nu = [0]

            def low_to(u):
                while nu[0] <= min(u, NU - 1):
                    v = nu[0]
                    if pool_lo[v]:
                        pool.wait_ge(hi_ready, v + 1)
                        G.tensor_tensor(w_lo[:, v % SLOTS, :, :], raw[:, v % SLOTS, :, :], f(w_hi[:, v % SLOTS, :, :]),
                                        ALU.subtract).then_inc(lo_ready_pool, 1)
                    nu[0] += 1

            def own():
                pool.wait_ge(pool_made, now("pool"))

            F_ = first
            G.memset(ident[:, :], 0.0).then_inc(pool_made, tick("pool"))
            G.memset(ones[:, :], 1.0).then_inc(pool_made, tick("pool"))
            own()
            G.affine_select(out=ident[:, :], in_=ident[:, :], compare_op=ALU.not_equal, fill=1.0, base=0,
                            pattern=[[-1, P]], channel_multiplier=1).then_inc(pool_made, tick("pool", "ident"))
            G.affine_select(out=tri[:, :], in_=ones[:, :], compare_op=ALU.is_ge, fill=0.0, base=0,
                            pattern=[[1, P]], channel_multiplier=-1).then_inc(pool_made, tick("pool"))
            own()
            G.tensor_copy(cbmask[:, 0:P], tri[:, :]).then_inc(pool_made, tick("pool"))
            G.memset(cbmask[:, P:2 * P], 1.0).then_inc(pool_made, tick("pool"))
            G.tensor_copy(cbmask[:, 2 * P:3 * P], tri[:, :]).then_inc(pool_made, tick("pool", "cbmask"))
            pool.wait_ge(dve_made, after("dve", "mhalf"))

            def rsqrt(dst, src, *name):
                G.tensor_tensor(dst, src, mhalf[:, 0:dst.shape[1]], ALU.pow).then_inc(pool_made, tick("pool", *name))

            low_to(F_[("xbc", 0)] + 3)
            pool.wait_ge(dve_made, after("dve", "v0"))
            rsqrt(rfac[:, 0, 0:2], stat[:, 1, 0:2], "r0")
            for g, w in enumerate(POOL_WINDOWS):
                G.memset(icnt[:, g, :], 1.0 / w).then_inc(pool_made, tick("pool"))
                own()
                for c in range(w - 1):
                    G.memset(icnt[:, g, c:c + 1], 1.0 / (c + 1)).then_inc(pool_made, tick("pool"))
            low_to(F_[("pool", 0)] + 5)

            def window(g):
                w = POOL_WINDOWS[g]
                pool.wait_ge(dve_made, after("dve", "pu", g // 2))
                src, step, k = pu[:, g, :], 1, 0
                N = T + 16
                bufs = (pw1, pw2)
                while step < w:
                    dst = bufs[k % 2]
                    own()
                    G.tensor_tensor(dst[:, step:N], src[:, step:N], src[:, 0:N - step], ALU.add)\
                        .then_inc(pool_made, tick("pool"))
                    G.memset(dst[:, 0:step], 0.0).then_inc(pool_made, tick("pool"))
                    src, step, k = dst[:, :], step * 2, k + 1
                own()
                dst = bufs[k % 2]
                G.tensor_scalar(dst[:, 32:N], src[:, 32:N], 1.0 / w, None, ALU.mult).then_inc(pool_made, tick("pool"))
                G.tensor_tensor(dst[:, 16:32], src[:, 16:32], icnt[:, g, :], ALU.mult).then_inc(pool_made, tick("pool"))
                own()
                G.tensor_tensor(pdiff[:, g, :], dst[:, 16:N], pu[:, g, 16:N], ALU.subtract)\
                    .then_inc(pool_made, tick("pool", "pdiff", g))

            for i in range(8):
                low_to(F_[("K", 0, 0)] + k_ahead[i])
                if i < 4:
                    window(i)
            low_to(F_[("out", 0, "early", 1)] + 3)
            pool.wait_ge(dve_made, after("dve", "gv"))
            rsqrt(rfac[:, 8, 0:4], stat[:, 8, 0:4], "gr")
            low_to(F_[("V", 0, 0)] - 1)

            def x_sums(tag):
                pool.wait_ge(act_made, after("act", "xsq", tag, 1))
                G.tensor_tensor(Ssum[:, :], sq[:, 0, :], sq[:, 1, :], ALU.add).then_inc(pool_made, tick("pool", "Sx", tag, 0))
                L.also("pool", "Sx", tag, 1)
                for i in (2, 3):
                    pool.wait_ge(act_made, after("act", "xsq", tag, i))
                    own()
                    G.tensor_tensor(Ssum[:, :], Ssum[:, :], sq[:, i % 2, :], ALU.add).then_inc(pool_made, tick("pool"))
                own()
                G.tensor_tensor(S2[:, :], Ssum[:, 0:T], Ssum[:, T:H2], ALU.add).then_inc(pool_made, tick("pool", "Sx", tag))

            for l in range(2):
                if l == 1:
                    pool.wait_ge(dve_made, after("dve", "r1v"))
                    rsqrt(rfac[:, 7, 0:2], stat[:, 7, 0:2], "r1")
                    pool.wait_ge(act_made, after("act", "Rrow", 1))
                    for g in range(2):
                        for q in range(2):
                            low_to(F_[("gate", g)] + 4 + 2 * q + 1)
                            pool.wait_ge(act_made, after("act", "sig", g, q))
                            G.tensor_tensor(sg[:, 2 * q:2 * q + 2, :], sg[:, 2 * q:2 * q + 2, :], row2(Rrow), ALU.mult)\
                                .then_inc(pool_made, tick("pool", "sg", g, q))
                            low_to(F_[("gate", g)] + 4 + 2 * q + 3)
                        low_to(F_[("a", g)] + 9)
                    for g in range(2):
                        for q in range(2):
                            i = 2 * g + q
                            low_to(F_[("hh", g)] + 3 + 2 * q + 2)
                            pool.wait_ge(dve_made, after("dve", "cv3", i))
                            G.tensor_tensor(cv3[:, 2 * i:2 * i + 2, :], cv3[:, 2 * i:2 * i + 2, :], row2(Rrow), ALU.mult)\
                                .then_inc(pool_made, tick("pool", "cv3R", i))
                    low_to(F_[("out", 1, "early", 1)] + 5)
                    pool.wait_ge(dve_made, after("dve", "lnv"))
                    rsqrt(rfac[:, 10, 0:2], stat[:, 9, 0:2], "lnr")
                    low_to(F_[("K", 1, 1)] - 1)
                pool.wait_ge(dve_made, after("dve", "nv", l, 0))
                rsqrt(rfac[:, 1 + 3 * l, 0:2], stat[:, 1 + 3 * l, 0:2], "nr", l, 0)
                low_to(F_[("q", l, 0)] + 3)
                x_sums(f"q{l}")
                pool.wait_ge(dve_made, after("dve", "av", l))
                rsqrt(rfac[:, 11 + l, 0:2], stat[:, 7, 0:2], "ar", l)
                low_to(F_[("wo", l, "late", 1)] + 1)
                if (l, 1) not in FILL:
                    low_to(F_[("w1", l, 0)] + 1)
                pool.wait_ge(dve_made, after("dve", "nv", l, 1))
                rsqrt(rfac[:, 2 + 3 * l, 0:2], stat[:, 2 + 3 * l, 0:2], "nr", l, 1)
                low_to(F_[("w1", l, 0)] + 3)
                x_sums(f"mlp{l}")
                pool.wait_ge(dve_made, after("dve", "hv", l))
                rsqrt(rfac[:, 13 + l, 0:2], stat[:, 15, 0:2])
                own()
                G.tensor_tensor(rfac[:, 13 + l, 2:4], rfac[:, 13 + l, 0:2], rfac[:, 13 + l, 0:2], ALU.mult)\
                    .then_inc(pool_made, tick("pool"))
                own()
                G.tensor_tensor(rfac[:, 13 + l, 4:6], rfac[:, 13 + l, 2:4], rfac[:, 13 + l, 2:4], ALU.mult)\
                    .then_inc(pool_made, tick("pool", "r4", l))
                pool.wait_ge(dve_made, after("dve", "nv", l, 2))
                s_ = 3 + 3 * l
                rsqrt(rfac[:, s_, 2:4], stat[:, s_, 0:2])
                own()
                G.tensor_tensor(rfac[:, s_, 0:2], rfac[:, s_, 2:4], rfac[:, 13 + l, 2:4], ALU.mult)\
                    .then_inc(pool_made, tick("pool", "nr", l, 2))
                if l == 0:
                    low_to(F_[("gate", 0)] + 3)
                    x_sums("in1")

    return L.at


INPUTS = ["x", "mem", "norm_gains", "xa_wq", "xa_wkv", "xa_wo", "mlp_w1", "mlp_w2", "ab_w_in", "pool_w",
          "pool_scale", "ssm_conv_w", "ssm_conv_b", "ssm_dt_bias", "ssm_a_log", "ssm_d", "ssm_norm", "ab_w_out",
          "cd_w_in", "conf_dw_w", "conf_dw_b", "conf_ln_g", "conf_ln_b", "sc_conv_w", "cd_w_out"]


def kernel(**inputs):
    import concourse.bacc as bacc
    from concourse.bass_utils import run_bass_kernel_spmd

    arrays = {f"in_{n}": np.ascontiguousarray(inputs[n]) for n in INPUTS}
    counts = None
    for _ in range(2):
        nc = bacc.Bacc("TRN2", target_bir_lowering=False, num_devices=1)
        A = {n: nc.dram_tensor(f"in_{n}", inputs[n].shape, F32, kind="ExternalInput").ap() for n in INPUTS}
        out = nc.dram_tensor("out_0", inputs["x"].shape, F32, kind="ExternalOutput").ap()
        counts = trunk(nc, A, out, counts)
    return run_bass_kernel_spmd(nc, [arrays], core_ids=[0]).results[0]["out_0"]
```
